# Optimizing a Trainium2 kernel written in Bass

```python
import math
import jax, jax.numpy as jnp
from jax import lax
import numpy as np

D_MODEL = 1024
BATCH = 1
SEQ = 256
DEPTH = 2

GRID_W = 64
CTX_LEN = 256
N_MIXERS = 3
N_POOL_LAYERS = len(range(0, DEPTH, N_MIXERS))
N_DIFF_LAYERS = len(range(1, DEPTH, N_MIXERS))
N_NAT_LAYERS = len(range(2, DEPTH, N_MIXERS))
D_FF = ((8 * D_MODEL // 3 + 255) // 256) * 256
N_MOD = 9
POOL_WINDOWS = (2, 4, 8, 16)
POOL_GROUPS = len(POOL_WINDOWS)
POOL_GW = D_MODEL // POOL_GROUPS
DIFF_HEADS = 8
DIFF_HD = D_MODEL // DIFF_HEADS // 2
NAT_HEADS = 16
NAT_HD = D_MODEL // NAT_HEADS
NAT_WIN_ROWS = 8
NAT_WIN_COLS = 16
ROPE_THETA = 10000.0
Q_BLOCK = 128
NORM_EPS = 1e-6


def rms_norm(x, g):
    xf = x.astype(jnp.float32)
    y = xf * lax.rsqrt(jnp.mean(xf * xf, axis=-1, keepdims=True) + NORM_EPS)
    return (y * g.astype(jnp.float32)).astype(x.dtype)

def modulate(h, shift, scale):
    return h * (1 + scale) + shift

def swiglu(h, w_in, w_out):
    g, u = jnp.split(h @ w_in, 2, axis=-1)
    return (jax.nn.silu(g) * u) @ w_out

def ffn_step(s, g, shift, scale, gate, w_in, w_out):
    return s + 0.5 * gate * swiglu(modulate(rms_norm(s, g), shift, scale), w_in, w_out)

def pool_mix(h, w, scale):
    b, n, d = h.shape
    hf = h.astype(jnp.float32)
    cs = jnp.concatenate([jnp.zeros((b, 1, d), jnp.float32), jnp.cumsum(hf, axis=1)], axis=1)
    t = jnp.arange(n)
    outs = []
    for gi, win in enumerate(POOL_WINDOWS):
        lo = jnp.clip(t - win // 2, 0, n - 1)
        hi = jnp.clip(t - win // 2 + win - 1, 0, n - 1)
        sl = slice(gi * POOL_GW, (gi + 1) * POOL_GW)
        csg = cs[:, :, sl]
        mean = (csg[:, hi + 1] - csg[:, lo]) / (hi - lo + 1).astype(jnp.float32)[None, :, None]
        outs.append(mean - hf[:, :, sl])
    diff = jnp.stack(outs, axis=2).astype(h.dtype)
    y = jnp.einsum('bngc,gce->bnge', diff, w).reshape(b, n, d)
    return y * scale

def axial_angles(n):
    t = jnp.arange(n)
    rows = (t // GRID_W).astype(jnp.float32)
    cols = (t % GRID_W).astype(jnp.float32)
    per_axis = DIFF_HD // 2
    inv = ROPE_THETA ** (-jnp.arange(0, per_axis, 2, dtype=jnp.float32) / per_axis)
    return rows[:, None] * inv, cols[:, None] * inv

def rotate(x, ang):
    m = x.shape[-1] // 2
    x1, x2 = x[..., :m], x[..., m:]
    cos, sin = jnp.cos(ang), jnp.sin(ang)
    return jnp.concatenate([x1 * cos - x2 * sin, x2 * cos + x1 * sin], axis=-1)

def rope_2d(x, row_ang, col_ang):
    shape = (1, x.shape[1]) + (1,) * (x.ndim - 3) + (row_ang.shape[-1],)
    ra, ca = row_ang.reshape(shape), col_ang.reshape(shape)
    xf = x.astype(jnp.float32)
    half = x.shape[-1] // 2
    out = jnp.concatenate([rotate(xf[..., :half], ra), rotate(xf[..., half:], ca)], axis=-1)
    return out.astype(x.dtype)

def diff_attention(h_lat, h_ctx, w_qkv, lam, subln_g, w_o, lam_init, want_ctx):
    b, n, d = h_lat.shape
    scale = DIFF_HD ** -0.5

    def proj(h):
        q, k, v = jnp.split(h @ w_qkv, 3, axis=-1)
        s = h.shape[:2]
        return (q.reshape(s + (DIFF_HEADS, 2, DIFF_HD)), k.reshape(s + (DIFF_HEADS, 2, DIFF_HD)),
                v.reshape(s + (DIFF_HEADS, 2 * DIFF_HD)))

    q_l, k_l, v_l = proj(h_lat)
    q_c, k_c, v_c = proj(h_ctx)
    ra, ca = axial_angles(n)
    q_l = rope_2d(q_l, ra, ca)
    k_l = rope_2d(k_l, ra, ca)
    lf = lam.astype(jnp.float32)
    lam_full = jnp.exp(jnp.sum(lf[0] * lf[1])) - jnp.exp(jnp.sum(lf[2] * lf[3])) + lam_init

    def attend(q, k, v):
        s = jnp.einsum('bqhjd,bkhjd->bhjqk', q, k).astype(jnp.float32) * scale
        p = jax.nn.softmax(s, axis=-1)
        a = p[:, :, 0] - lam_full * p[:, :, 1]
        return jnp.einsum('bhqk,bkhe->bqhe', a.astype(v.dtype), v)

    k_all = jnp.concatenate([k_l, k_c], axis=1)
    v_all = jnp.concatenate([v_l, v_c], axis=1)
    nb = n // Q_BLOCK
    q_blocks = jnp.moveaxis(q_l.reshape(b, nb, Q_BLOCK, DIFF_HEADS, 2, DIFF_HD), 1, 0)
    o_l = lax.map(lambda qb: attend(qb, k_all, v_all), q_blocks)
    o_l = jnp.moveaxis(o_l, 0, 1).reshape(b, n, DIFF_HEADS, 2 * DIFF_HD)

    def finish(o):
        o = rms_norm(o, subln_g) * (1 - lam_init)
        return o.reshape(o.shape[:2] + (d,)) @ w_o

    out_l = finish(o_l)
    out_c = finish(attend(q_c, k_c, v_c)) if want_ctx else None
    return out_l, out_c

def neighbourhood_attention(h_lat, h_ctx, w_qkv, b_qkv, rpb, w_o, b_o, want_ctx):
    b, n, d = h_lat.shape
    n_rows = n // GRID_W
    wr = min(NAT_WIN_ROWS, n_rows)
    wc = min(NAT_WIN_COLS, GRID_W)
    scale = NAT_HD ** -0.5

    def proj(h):
        q, k, v = jnp.split(h @ w_qkv + b_qkv, 3, axis=-1)
        s = h.shape[:2] + (NAT_HEADS, NAT_HD)
        return q.reshape(s) * scale, k.reshape(s), v.reshape(s)

    q_l, k_l, v_l = proj(h_lat)
    q_c, k_c, v_c = proj(h_ctx)
    gshape = (b, n_rows, GRID_W, NAT_HEADS, NAT_HD)
    k_g = k_l.reshape(gshape)
    v_g = v_l.reshape(gshape)
    q_rows = jnp.moveaxis(q_l.reshape(gshape), 1, 0)
    qcol = jnp.arange(GRID_W)
    col_start = jnp.clip(qcol - wc // 2, 0, GRID_W - wc)
    col_idx = col_start[:, None] + jnp.arange(wc)[None, :]
    col_off = col_idx - qcol[:, None] + (NAT_WIN_COLS - 1)

    def row_block(args):
        r, q = args
        rs = jnp.clip(r - wr // 2, 0, n_rows - wr)
        k_band = lax.dynamic_slice_in_dim(k_g, rs, wr, axis=1)
        v_band = lax.dynamic_slice_in_dim(v_g, rs, wr, axis=1)
        k_win = k_band[:, :, col_idx]
        v_win = v_band[:, :, col_idx]
        row_off = rs + jnp.arange(wr) - r + (NAT_WIN_ROWS - 1)
        bias = rpb[:, row_off[:, None, None], col_off[None, :, :]]
        bias = jnp.transpose(bias, (0, 2, 1, 3)).astype(jnp.float32)
        s_win = jnp.einsum('bqhd,bwqchd->bhqwc', q, k_win).astype(jnp.float32) + bias[None]
        s_ctx = jnp.einsum('bqhd,bkhd->bhqk', q, k_c).astype(jnp.float32)
        s = jnp.concatenate([s_win.reshape(b, NAT_HEADS, GRID_W, wr * wc), s_ctx], axis=-1)
        p = jax.nn.softmax(s, axis=-1).astype(v_win.dtype)
        p_win = p[..., :wr * wc].reshape(b, NAT_HEADS, GRID_W, wr, wc)
        p_ctx = p[..., wr * wc:]
        return (jnp.einsum('bhqwc,bwqchd->bqhd', p_win, v_win)
                + jnp.einsum('bhqk,bkhd->bqhd', p_ctx, v_c))

    o = lax.map(row_block, (jnp.arange(n_rows), q_rows))
    out_l = jnp.moveaxis(o, 0, 1).reshape(b, n, d) @ w_o + b_o
    out_c = None
    if want_ctx:
        s = jnp.einsum('bqhd,bkhd->bhqk', q_c, k_c).astype(jnp.float32)
        p = jax.nn.softmax(s, axis=-1).astype(v_c.dtype)
        o_c = jnp.einsum('bhqk,bkhd->bqhd', p, v_c)
        out_c = o_c.reshape(o_c.shape[0], o_c.shape[1], d) @ w_o + b_o
    return out_l, out_c

def first_inputs(seed: int = 0) -> dict:
    key = jax.random.key(seed)
    ks = jax.random.split(key, 24)
    D = D_MODEL

    def nrm(k, shape, std):
        return jax.random.normal(k, shape, jnp.float32) * std

    return {
        'x': nrm(ks[0], (BATCH, SEQ, D), 1.0),
        'c': nrm(ks[1], (BATCH, D), 1.0),
        'ctx': nrm(ks[2], (BATCH, CTX_LEN, D), 1.0),
        'c_ctx': nrm(ks[3], (D,), 1.0),
        'ada_w': nrm(ks[4], (DEPTH, D, N_MOD * D), 0.5 * D ** -0.5),
        'ada_b': nrm(ks[5], (DEPTH, N_MOD * D), 0.01),
        'norm_g': 1.0 + nrm(ks[6], (DEPTH, 3, D), 0.1),
        'ffn_w_in': nrm(ks[7], (DEPTH, 2, D, 2 * D_FF), D ** -0.5),
        'ffn_w_out': nrm(ks[8], (DEPTH, 2, D_FF, D), D_FF ** -0.5),
        'pool_w': nrm(ks[9], (N_POOL_LAYERS, POOL_GROUPS, POOL_GW, POOL_GW), POOL_GW ** -0.5),
        'pool_scale': 1.0 + nrm(ks[10], (N_POOL_LAYERS, D), 0.1),
        'diff_w_qkv': nrm(ks[11], (N_DIFF_LAYERS, D, 3 * D), D ** -0.5),
        'diff_lam': nrm(ks[12], (N_DIFF_LAYERS, 4, DIFF_HD), 0.1),
        'diff_subln_g': 1.0 + nrm(ks[13], (N_DIFF_LAYERS, 2 * DIFF_HD), 0.1),
        'diff_w_o': nrm(ks[14], (N_DIFF_LAYERS, D, D), D ** -0.5),
        'nat_w_qkv': nrm(ks[15], (N_NAT_LAYERS, D, 3 * D), D ** -0.5),
        'nat_b_qkv': nrm(ks[16], (N_NAT_LAYERS, 3 * D), 0.01),
        'nat_rpb': nrm(ks[17], (N_NAT_LAYERS, NAT_HEADS, 2 * NAT_WIN_ROWS - 1, 2 * NAT_WIN_COLS - 1), 0.1),
        'nat_w_o': nrm(ks[18], (N_NAT_LAYERS, D, D), D ** -0.5),
        'nat_b_o': nrm(ks[19], (N_NAT_LAYERS, D), 0.01),
        'final_g': 1.0 + nrm(ks[20], (D,), 0.1),
    }

def first_block(x, c, ctx, c_ctx, ada_w, ada_b, norm_g, ffn_w_in, ffn_w_out, pool_w, pool_scale,
              diff_w_qkv, diff_lam, diff_subln_g, diff_w_o, nat_w_qkv, nat_b_qkv, nat_rpb,
              nat_w_o, nat_b_o, final_g):
    xc = ctx
    s_c = jax.nn.silu(c)
    s_cc = jax.nn.silu(c_ctx)
    for i in range(DEPTH):
        kind = i % N_MIXERS
        j = i // N_MIXERS
        last = i == DEPTH - 1
        update_ctx = not last
        ctx_needed = update_ctx or kind != 0
        mx = jnp.split((s_c @ ada_w[i] + ada_b[i])[:, None, :], N_MOD, axis=-1)
        mc = jnp.split((s_cc @ ada_w[i] + ada_b[i])[None, None, :], N_MOD, axis=-1)
        x = ffn_step(x, norm_g[i, 0], mx[0], mx[1], mx[2], ffn_w_in[i, 0], ffn_w_out[i, 0])
        if ctx_needed:
            xc = ffn_step(xc, norm_g[i, 0], mc[0], mc[1], mc[2], ffn_w_in[i, 0], ffn_w_out[i, 0])
        hx = modulate(rms_norm(x, norm_g[i, 1]), mx[3], mx[4])
        hc = modulate(rms_norm(xc, norm_g[i, 1]), mc[3], mc[4]) if ctx_needed else None
        if kind == 0:
            ox = pool_mix(hx, pool_w[j], pool_scale[j])
            oc = pool_mix(hc, pool_w[j], pool_scale[j]) if update_ctx else None
        elif kind == 1:
            lam_init = 0.8 - 0.6 * math.exp(-0.3 * i)
            ox, oc = diff_attention(hx, hc, diff_w_qkv[j], diff_lam[j], diff_subln_g[j], diff_w_o[j],
                                    lam_init, update_ctx)
        else:
            ox, oc = neighbourhood_attention(hx, hc, nat_w_qkv[j], nat_b_qkv[j], nat_rpb[j],
                                             nat_w_o[j], nat_b_o[j], update_ctx)
        x = x + mx[5] * ox
        if update_ctx:
            xc = xc + mc[5] * oc
        x = ffn_step(x, norm_g[i, 2], mx[6], mx[7], mx[8], ffn_w_in[i, 1], ffn_w_out[i, 1])
        if update_ctx:
            xc = ffn_step(xc, norm_g[i, 2], mc[6], mc[7], mc[8], ffn_w_in[i, 1], ffn_w_out[i, 1])
    return rms_norm(x, final_g)


HEAD_DIM = 64
N_A_LAYERS = DEPTH // 2
N_B_LAYERS = DEPTH - N_A_LAYERS
MEM_LEN = 256
MEM_HEADS = 4
MEM_W = MEM_HEADS * HEAD_DIM
RWKV_HEADS = (D_MODEL - MEM_W) // HEAD_DIM
RWKV_W = RWKV_HEADS * HEAD_DIM
DECAY_LORA = 64
AAA_LORA = 64
GATE_LORA = 128
RWKV_SHIFT_W = 3 * RWKV_W + DECAY_LORA + AAA_LORA + GATE_LORA
A_IN_W = RWKV_SHIFT_W + MEM_W
DIL_GROUPS = ((128, 1), (512, 4), (2048, 16))
DIL_GROUP_HEADS = 4
DIL_HEADS = len(DIL_GROUPS) * DIL_GROUP_HEADS
DIL_W = DIL_HEADS * HEAD_DIM
DIL_OUT_W = DIL_GROUP_HEADS * HEAD_DIM
BLOCK = 128
NUM_BUCKETS = 32
MAX_DISTANCE = 2048
D_FF_2 = 2816
LNX_EPS = 64e-5
NEG_INF = -1e30


def rms_norm_2(x, g):
    xf = x.astype(jnp.float32)
    y = xf * lax.rsqrt(jnp.mean(xf * xf, axis=-1, keepdims=True) + NORM_EPS)
    return (y * g.astype(jnp.float32)).astype(x.dtype)

def split_heads(t):
    return t.reshape(t.shape[:-1] + (t.shape[-1] // HEAD_DIM, HEAD_DIM))

def swiglu_ffn(x, norm_g, w_in, w_out):
    gate, up = jnp.split(rms_norm_2(x, norm_g) @ w_in, 2, axis=-1)
    return (jax.nn.silu(gate) * up) @ w_out

def token_shift(p, mu):
    prev = jnp.pad(p, ((0, 0), (1, 0), (0, 0)))[:, :-1]
    return p + mu * (prev - p)

def rwkv7_scan(r, w, k, v, kk, a):
    b, _, h, n = r.shape

    def step(state, inp):
        r_t, w_t, k_t, v_t, kk_t, a_t = inp
        sa = jnp.einsum('bhvk,bhk->bhv', state, -kk_t)
        state = (state * w_t[:, :, None, :]
                 + sa[..., None] * (kk_t * a_t)[:, :, None, :]
                 + v_t[..., None] * k_t[:, :, None, :])
        return state, jnp.einsum('bhvk,bhk->bhv', state, r_t)

    xs = tuple(jnp.moveaxis(t.astype(jnp.float32), 1, 0) for t in (r, w, k, v, kk, a))
    _, ys = lax.scan(step, jnp.zeros((b, h, n, n), jnp.float32), xs)
    return jnp.moveaxis(ys, 0, 1)

def rwkv7_mix(p, mu, w0, w_up, a0, a_up, g_up, kk_scale, k_a, r_k, lnx_g, lnx_b):
    out_dtype = p.dtype
    b, s = p.shape[:2]
    p = token_shift(p, mu).astype(jnp.float32)
    cuts = [RWKV_W, 2 * RWKV_W, 3 * RWKV_W, 3 * RWKV_W + DECAY_LORA,
            3 * RWKV_W + DECAY_LORA + AAA_LORA]
    r, k, v, w_lo, a_lo, g_lo = jnp.split(p, cuts, axis=-1)
    w_log = -jax.nn.softplus(-(w0 + jnp.tanh(w_lo) @ w_up)) - 0.5
    decay = jnp.exp(-jnp.exp(w_log))
    a = jax.nn.sigmoid(a0 + a_lo @ a_up)
    g = jax.nn.sigmoid(g_lo) @ g_up
    kk = split_heads(k * kk_scale)
    kk = kk / jnp.maximum(jnp.linalg.norm(kk, axis=-1, keepdims=True), 1e-12)
    k = k * (1.0 + (a - 1.0) * k_a)
    r_h, k_h, v_h, a_h, w_h = (split_heads(t) for t in (r, k, v, a, decay))
    y = rwkv7_scan(r_h, w_h, k_h, v_h, kk, a_h)
    mean = jnp.mean(y, axis=-1, keepdims=True)
    var = jnp.mean(jnp.square(y - mean), axis=-1, keepdims=True)
    y = ((y - mean) * lax.rsqrt(var + LNX_EPS)).reshape(b, s, RWKV_W) * lnx_g + lnx_b
    bonus = jnp.sum(r_h * k_h * r_k, axis=-1, keepdims=True) * v_h
    y = (y + bonus.reshape(b, s, RWKV_W)) * g
    return y.astype(out_dtype)

def memory_attention(q, mem, mem_norm_g, w_kv, q_gain, k_gain):
    k, v = jnp.split(rms_norm_2(mem, mem_norm_g) @ w_kv, 2, axis=-1)
    k = rms_norm_2(split_heads(k), k_gain)
    v = split_heads(v)
    q = rms_norm_2(q, q_gain)
    logits = jnp.einsum('bshd,bmhd->bhsm', q, k).astype(jnp.float32) / math.sqrt(HEAD_DIM)
    probs = jax.nn.softmax(logits, axis=-1)
    return jnp.einsum('bhsm,bmhd->bshd', probs.astype(v.dtype), v)

def padded_len(seq_len, dil):
    unit = dil * BLOCK
    return -(-seq_len // unit) * unit

def strided_blocks(t, dil, s_pad):
    b, s = t.shape[:2]
    t = jnp.pad(t, ((0, 0), (0, s_pad - s)) + ((0, 0),) * (t.ndim - 2))
    t = t.reshape((b, s_pad // dil, dil) + t.shape[2:])
    t = jnp.moveaxis(t, 2, 1)
    return t.reshape((b, dil, s_pad // (dil * BLOCK), BLOCK) + t.shape[3:])

def unstride_blocks(t, seq_len):
    b, dil, nb, blk = t.shape[:4]
    t = t.reshape((b, dil, nb * blk) + t.shape[4:])
    t = jnp.moveaxis(t, 1, 2)
    return t.reshape((b, dil * nb * blk) + t.shape[3:])[:, :seq_len]

def with_prev_block(t):
    prev = jnp.pad(t[:, :, :-1], ((0, 0), (0, 0), (1, 0), (0, 0), (0, 0), (0, 0)))
    return jnp.concatenate([prev, t], axis=3)

def t5_bucket(dist):
    max_exact = NUM_BUCKETS // 2
    d_f = jnp.maximum(dist, 1).astype(jnp.float32)
    large = max_exact + (jnp.log(d_f / max_exact) / math.log(MAX_DISTANCE / max_exact)
                         * (NUM_BUCKETS - max_exact)).astype(jnp.int32)
    large = jnp.minimum(large, NUM_BUCKETS - 1)
    return jnp.where(dist < max_exact, dist, large)

def band_mask_and_bias(window, dil, n_blocks, table):
    span = window // dil
    qi = jnp.arange(BLOCK)[:, None]
    kj = jnp.arange(2 * BLOCK)[None, :]
    dsub = BLOCK + qi - kj
    band = (dsub >= 0) & (dsub <= span)
    first = (jnp.arange(n_blocks)[:, None, None] > 0) | (kj[None] >= BLOCK)
    mask = band[None] & first
    bias = jnp.transpose(table[t5_bucket(jnp.maximum(dsub, 0) * dil)], (2, 0, 1))
    return mask, bias

def shared_kv_blocks(x, kv_norm, kv_w, k_gain):
    k, v = jnp.split(rms_norm_2(x, kv_norm) @ kv_w, 2, axis=-1)
    k = rms_norm_2(split_heads(k), k_gain)
    v = split_heads(v)
    seq_len = x.shape[1]
    k_blocks, v_blocks = [], []
    for g, (_, dil) in enumerate(DIL_GROUPS):
        hs = slice(g * DIL_GROUP_HEADS, (g + 1) * DIL_GROUP_HEADS)
        s_pad = padded_len(seq_len, dil)
        k_blocks.append(strided_blocks(k[:, :, hs], dil, s_pad))
        v_blocks.append(strided_blocks(v[:, :, hs], dil, s_pad))
    return k_blocks, v_blocks

def dilated_attention(q, k_blocks, v_blocks, q_gain, rel_bias, seq_len):
    q = rms_norm_2(q, q_gain)
    scale = 1.0 / math.sqrt(HEAD_DIM)
    outs, lses = [], []
    for g, (window, dil) in enumerate(DIL_GROUPS):
        hs = slice(g * DIL_GROUP_HEADS, (g + 1) * DIL_GROUP_HEADS)
        qb = strided_blocks(q[:, :, hs], dil, padded_len(seq_len, dil))
        kw = with_prev_block(k_blocks[g])
        vw = with_prev_block(v_blocks[g]).astype(jnp.float32)
        mask, bias = band_mask_and_bias(window, dil, qb.shape[2], rel_bias[:, hs])
        logits = jnp.einsum('brnqhd,brnkhd->brnhqk', qb, kw).astype(jnp.float32) * scale
        logits = jnp.where(mask[:, None], logits + bias, NEG_INF)
        m = jnp.max(logits, axis=-1, keepdims=True)
        p = jnp.exp(logits - m)
        l = jnp.sum(p, axis=-1, keepdims=True)
        o = jnp.einsum('brnhqk,brnkhd->brnqhd', p, vw) / jnp.swapaxes(l, 3, 4)
        lse = jnp.swapaxes(m + jnp.log(l), 3, 4)
        outs.append(unstride_blocks(o, seq_len))
        lses.append(unstride_blocks(lse, seq_len))
    weights = jax.nn.softmax(jnp.stack(lses), axis=0)
    return jnp.sum(weights * jnp.stack(outs), axis=0).astype(q.dtype)

def second_inputs(seed: int = 0) -> dict:
    key = jax.random.key(seed)
    keys = iter(jax.random.split(key, 48))

    def normal(shape, scale):
        return jax.random.normal(next(keys), shape, jnp.float32) * scale

    def gain(shape):
        return 1.0 + normal(shape, 0.02)

    def uniform(shape, lo, hi):
        return jax.random.uniform(next(keys), shape, jnp.float32, lo, hi)

    d, f = D_MODEL, D_FF_2
    return {
        'x': normal((BATCH, SEQ, d), 1.0),
        'mem': normal((BATCH, MEM_LEN, d), 1.0),
        'ffn_pre_norm': gain((DEPTH, d)),
        'ffn_pre_w_in': normal((DEPTH, d, 2 * f), d ** -0.5),
        'ffn_pre_w_out': normal((DEPTH, f, d), f ** -0.5),
        'mix_norm': gain((DEPTH, d)),
        'ffn_post_norm': gain((DEPTH, d)),
        'ffn_post_w_in': normal((DEPTH, d, 2 * f), d ** -0.5),
        'ffn_post_w_out': normal((DEPTH, f, d), f ** -0.5),
        'mem_norm': gain((DEPTH, d)),
        'mem_w_kv': normal((DEPTH, d, 2 * MEM_W), d ** -0.5),
        'mem_q_norm': gain((DEPTH, HEAD_DIM)),
        'mem_k_norm': gain((DEPTH, HEAD_DIM)),
        'a_w_in': normal((N_A_LAYERS, d, A_IN_W), d ** -0.5),
        'a_shift_mu': uniform((N_A_LAYERS, RWKV_SHIFT_W), 0.0, 1.0),
        'a_w0': uniform((N_A_LAYERS, RWKV_W), -6.0, -1.0),
        'a_w_up': normal((N_A_LAYERS, DECAY_LORA, RWKV_W), 0.5 * DECAY_LORA ** -0.5),
        'a_a0': normal((N_A_LAYERS, RWKV_W), 0.1),
        'a_a_up': normal((N_A_LAYERS, AAA_LORA, RWKV_W), AAA_LORA ** -0.5),
        'a_g_up': normal((N_A_LAYERS, GATE_LORA, RWKV_W), GATE_LORA ** -0.5),
        'a_kk_scale': 0.85 + normal((N_A_LAYERS, RWKV_W), 0.02),
        'a_k_a': gain((N_A_LAYERS, RWKV_W)),
        'a_r_k': normal((N_A_LAYERS, RWKV_HEADS, HEAD_DIM), 0.1),
        'a_lnx_g': gain((N_A_LAYERS, RWKV_W)),
        'a_lnx_b': normal((N_A_LAYERS, RWKV_W), 0.01),
        'a_w_out': normal((N_A_LAYERS, RWKV_W + MEM_W, d), (RWKV_W + MEM_W) ** -0.5),
        'b_w_q': normal((N_B_LAYERS, d, DIL_W + MEM_W), d ** -0.5),
        'b_q_norm': gain((N_B_LAYERS, HEAD_DIM)),
        'b_w_out': normal((N_B_LAYERS, DIL_OUT_W + MEM_W, d), (DIL_OUT_W + MEM_W) ** -0.5),
        'kv_norm': gain((d,)),
        'kv_w': normal((d, 2 * DIL_W), d ** -0.5),
        'kv_k_norm': gain((HEAD_DIM,)),
        'rel_bias': normal((NUM_BUCKETS, DIL_HEADS), 0.2),
    }

def second_block(x, mem, ffn_pre_norm, ffn_pre_w_in, ffn_pre_w_out, mix_norm,
              ffn_post_norm, ffn_post_w_in, ffn_post_w_out,
              mem_norm, mem_w_kv, mem_q_norm, mem_k_norm,
              a_w_in, a_shift_mu, a_w0, a_w_up, a_a0, a_a_up, a_g_up,
              a_kk_scale, a_k_a, a_r_k, a_lnx_g, a_lnx_b, a_w_out,
              b_w_q, b_q_norm, b_w_out, kv_norm, kv_w, kv_k_norm, rel_bias):
    b, s = x.shape[:2]
    k_blocks, v_blocks = None, None
    for layer in range(DEPTH):
        x = x + 0.5 * swiglu_ffn(x, ffn_pre_norm[layer], ffn_pre_w_in[layer], ffn_pre_w_out[layer])
        u = rms_norm_2(x, mix_norm[layer])
        if layer < N_A_LAYERS:
            i = layer
            proj = u @ a_w_in[i]
            y_main = rwkv7_mix(proj[..., :RWKV_SHIFT_W], a_shift_mu[i], a_w0[i], a_w_up[i],
                               a_a0[i], a_a_up[i], a_g_up[i], a_kk_scale[i], a_k_a[i],
                               a_r_k[i], a_lnx_g[i], a_lnx_b[i])
            y_mem = memory_attention(split_heads(proj[..., RWKV_SHIFT_W:]), mem, mem_norm[layer],
                                     mem_w_kv[layer], mem_q_norm[layer], mem_k_norm[layer])
            y = jnp.concatenate([y_main, y_mem.reshape(b, s, MEM_W)], axis=-1) @ a_w_out[i]
        else:
            j = layer - N_A_LAYERS
            q_all = u @ b_w_q[j]
            y_dil = dilated_attention(split_heads(q_all[..., :DIL_W]), k_blocks, v_blocks,
                                      b_q_norm[j], rel_bias, s)
            y_mem = memory_attention(split_heads(q_all[..., DIL_W:]), mem, mem_norm[layer],
                                     mem_w_kv[layer], mem_q_norm[layer], mem_k_norm[layer])
            y = jnp.concatenate([y_dil.reshape(b, s, DIL_OUT_W),
                                 y_mem.reshape(b, s, MEM_W)], axis=-1) @ b_w_out[j]
        x = x + y
        x = x + 0.5 * swiglu_ffn(x, ffn_post_norm[layer], ffn_post_w_in[layer], ffn_post_w_out[layer])
        if layer == N_A_LAYERS - 1:
            k_blocks, v_blocks = shared_kv_blocks(x, kv_norm, kv_w, kv_k_norm)
    return x


def setup_inputs(seed=0):
    out = dict(first_inputs(seed))
    for name, value in second_inputs(seed + 1).items():
        if name != "x":
            out[name + "_2"] = value
    return out


def reference(
    x, c, ctx, c_ctx, ada_w, ada_b, norm_g, ffn_w_in, ffn_w_out, pool_w, pool_scale, diff_w_qkv,
    diff_lam, diff_subln_g, diff_w_o, nat_w_qkv, nat_b_qkv, nat_rpb, nat_w_o, nat_b_o, final_g,
    mem_2, ffn_pre_norm_2, ffn_pre_w_in_2, ffn_pre_w_out_2, mix_norm_2, ffn_post_norm_2,
    ffn_post_w_in_2, ffn_post_w_out_2, mem_norm_2, mem_w_kv_2, mem_q_norm_2, mem_k_norm_2,
    a_w_in_2, a_shift_mu_2, a_w0_2, a_w_up_2, a_a0_2, a_a_up_2, a_g_up_2, a_kk_scale_2, a_k_a_2,
    a_r_k_2, a_lnx_g_2, a_lnx_b_2, a_w_out_2, b_w_q_2, b_q_norm_2, b_w_out_2, kv_norm_2, kv_w_2,
    kv_k_norm_2, rel_bias_2,
):
    x = first_block(
        x, c, ctx, c_ctx, ada_w, ada_b, norm_g, ffn_w_in, ffn_w_out, pool_w, pool_scale,
        diff_w_qkv, diff_lam, diff_subln_g, diff_w_o, nat_w_qkv, nat_b_qkv, nat_rpb, nat_w_o,
        nat_b_o, final_g,
    )
    return second_block(
        x, mem_2, ffn_pre_norm_2, ffn_pre_w_in_2, ffn_pre_w_out_2, mix_norm_2, ffn_post_norm_2,
        ffn_post_w_in_2, ffn_post_w_out_2, mem_norm_2, mem_w_kv_2, mem_q_norm_2, mem_k_norm_2,
        a_w_in_2, a_shift_mu_2, a_w0_2, a_w_up_2, a_a0_2, a_a_up_2, a_g_up_2, a_kk_scale_2,
        a_k_a_2, a_r_k_2, a_lnx_g_2, a_lnx_b_2, a_w_out_2, b_w_q_2, b_q_norm_2, b_w_out_2,
        kv_norm_2, kv_w_2, kv_k_norm_2, rel_bias_2,
    )


_drawn_inputs = setup_inputs


def setup_inputs(seed=0):
    import zlib

    import numpy as np

    out = dict(_drawn_inputs(seed))
    spreads = {}
    factors = {'ffn_pre_norm_2': 4.526,
     'mix_norm_2': 3.098,
     'ffn_post_norm_2': 5.571,
     'mem_norm_2': 8.0,
     'mem_q_norm_2': 8.0,
     'mem_k_norm_2': 8.0,
     'a_w_up_2': 4.593,
     'a_a0_2': 3.288,
     'a_kk_scale_2': 51.008,
     'a_k_a_2': 5.88,
     'a_lnx_g_2': 26.386,
     'a_lnx_b_2': 53.551,
     'b_q_norm_2': 8.0,
     'kv_norm_2': 8.0,
     'kv_k_norm_2': 8.0,
     'rel_bias_2': 12.093}
    for name, (base, spread) in spreads.items():
        noise = np.random.default_rng([zlib.crc32(name.encode()), seed]).standard_normal(out[name].shape)
        drawn = base * np.exp(spread * noise) if base else spread * noise
        out[name] = __import__('jax').numpy.asarray(drawn.astype(out[name].dtype))
    for name, factor in factors.items():
        out[name] = (out[name] * factor).astype(out[name].dtype)
    return out
```

```python
import math
from contextlib import ExitStack

import numpy as np

import concourse.bass as bass
from concourse import mybir

D = 1024
KT = D // 128
NX = 256
NTOK = 512
DFF = 2816
GROUPS = DFF // 256
CHUNK = 2048
SLOTS = 3
NMOD = 9
POOL_WINDOWS = (2, 4, 8, 16)
DIFF_HEADS = 8
RW = 768
RT = RW // 128
CH = 64
DIL = ((128, 1), (512, 4), (2048, 16))
NUM_BUCKETS, MAX_DISTANCE = 32, 2048
LAM_INIT = 0.8 - 0.6 * math.exp(-0.3)
NEG = -1e30


def vector_columns():
    sizes = [("ada_b", 144), ("norm_g", 48), ("pool_scale", 8), ("final_g", 8), ("ffn_pre_norm_2", 16),
             ("mix_norm_2", 16), ("ffn_post_norm_2", 16), ("mem_norm_2", 16), ("a_shift_mu_2", 20),
             ("a_w0_2", 6), ("a_a0_2", 6), ("a_kk_scale_2", 6), ("a_k_a_2", 6), ("a_r_k_2", 6),
             ("a_lnx_g_2", 6), ("a_lnx_b_2", 6), ("kv_norm_2", 8), ("c", 8), ("c_ctx", 8),
             ("diff_subln_g", 1), ("mem_q_norm_2", 2), ("b_q_norm_2", 1), ("mem_k_norm_2", 2),
             ("kv_k_norm_2", 1)]
    at, col = {}, 0
    for name, n in sizes:
        at[name] = col
        col += n
    return at, col


TWICE = ("mem_q_norm_2", "mem_k_norm_2", "b_q_norm_2", "kv_k_norm_2")


def constants():
    p = np.arange(128)
    half = p // 64
    same = half[:, None] == half[None, :]
    parts = {}
    parts["ident"] = np.eye(128)
    parts["ones"] = np.ones((128, 128))
    parts["blk"] = same.astype(float)
    perm = np.zeros((128, 128))
    for f in range(128):
        perm[f ^ 16, f] = 1.0
    parts["perm"] = perm
    t = np.arange(NX)
    inv = 10000.0 ** (-np.arange(0, 32, 2, dtype=np.float32) / np.float32(32))
    f32_ = np.float32
    ang = np.zeros((128, NX), f32_)
    for f in range(128):
        pos = (t // 64) if (f % 64) < 32 else (t % 64)
        ang[f] = pos.astype(f32_) * inv[f % 16].astype(f32_)
    sign = np.where((p % 32) < 16, -1.0, 1.0)[:, None]
    parts["cos"] = np.tile(np.cos(ang), 2)
    parts["sin"] = np.tile(np.sin(ang) * sign, 2)
    s_, t_ = p[:, None], p[None, :]
    parts["cum"] = np.concatenate([same & (s_ <= t_), same & (s_ < t_)], 1).astype(float)
    parts["lp_mask"] = np.concatenate([same & (s_ < t_), same & (s_ <= t_)], 1).astype(float)
    def level(b):
        return ((s_ // (2 * b) == t_ // (2 * b)) & (s_ // b % 2 == 1) & (t_ // b % 2 == 0)).astype(float)
    parts["m1"], parts["m1t"] = level(1), level(1).T
    for b in (2, 4, 8, 16, 32):
        parts[f"m{b}"] = level(b)
    parts["pick"] = np.eye(128)[:, 0:2] + np.eye(128, k=-2)[:, 0:2]
    parts["ident64"] = np.concatenate([np.eye(64), np.eye(64)], 0)
    parts["eps"] = np.full((128, 1), 1e-6)
    parts["lnx_eps"] = np.full((128, 1), 64e-5)
    at, col, cols = {}, 0, []
    for name, a in parts.items():
        at[name] = col
        col += a.shape[1]
        cols.append(np.asarray(a, f32_))
    return at, np.ascontiguousarray(np.concatenate(cols, 1))


def pool_counts():
    t = np.arange(NX)
    rows = [1.0 / (np.clip(t - w // 2 + w - 1, 0, NX - 1) - np.clip(t - w // 2, 0, NX - 1) + 1) for w in POOL_WINDOWS]
    return np.ascontiguousarray(np.broadcast_to(np.concatenate([np.tile(r, 4) for r in rows]).astype(np.float32), (128, 16 * NX)))


def bias_tables():
    u = np.arange(512)
    dist = u - 255
    exact = NUM_BUCKETS // 2
    large = exact + (np.log(np.maximum(dist, 1).astype(np.float32) / exact) / math.log(MAX_DISTANCE / exact)
                     * (NUM_BUCKETS - exact)).astype(np.int32)
    bucket = np.where(dist < exact, dist, np.minimum(large, NUM_BUCKETS - 1))
    hot = np.zeros((32, 3, 512), np.float32)
    add = np.zeros((32, 3, 512), np.float32)
    for g, (window, dil) in enumerate(DIL):
        ok = (dist >= 0) & (dist % dil == 0) & (dist <= window)
        for k in range(512):
            if ok[k]:
                hot[bucket[k], g, k] = 1.0
        add[:, g] = np.where(ok, 0.0, NEG)
    return np.ascontiguousarray(np.concatenate([hot.reshape(32, -1), add.reshape(32, -1)], 1))


FFN_PASS = [0, 0, KT]
FFN_ADA_PASS = [0, 1, 0, 1, KT, 2]
FFN_TILES = [0, 0] + FFN_PASS * (GROUPS - 1) + [KT]
FFN_ADA_TILES = [0, 0] + FFN_ADA_PASS * (GROUPS - 1) + [KT]
ADA_FIRST = 12
ADA_FFN = 3 * (GROUPS - 1)
ADA_PARTS = [(0, ADA_FIRST), (ADA_FIRST, ADA_FIRST + ADA_FFN), (ADA_FIRST + ADA_FFN, ADA_FIRST + 2 * ADA_FFN)]
assert ADA_PARTS[-1][1] == 2 * NMOD * D // 256
STREAM = [("ada", 0, [1] * ADA_FIRST), ("ffn", 0, FFN_ADA_TILES), ("pool", 0, [8]), ("ffn", 1, FFN_ADA_TILES),
          ("ffn", 2, FFN_TILES), ("qkv", 0, [2] * 8 + [4] * 4), ("wo", 0, [2] * 4),
          ("ffn", 3, FFN_TILES), ("ffn", 4, FFN_TILES), ("memkv", 0, [2] * 2), ("a_in", 0, [2] * 11),
          ("a_out", 0, [2] * 4), ("ffn", 5, FFN_TILES), ("kv", 0, [2] * 6), ("ffn", 6, FFN_TILES),
          ("memkv", 1, [2] * 2), ("b_q", 0, [2] * 4), ("b_out", 0, [4] * 2), ("ffn", 7, FFN_TILES)]
FIRST = {}
TILE0 = []
DONE = []
for _kind, _i, _tiles in STREAM:
    FIRST[_kind, _i] = len(DONE)
    for _t in _tiles:
        TILE0.append(TILE0[-1] + _last if TILE0 else 0)
        DONE.append((DONE[-1] if DONE else 0) + max(_t, 1))
        _last = _t
FIRST_AFTER = {key: FIRST[key] + len(t) for key, t in (((k, i), t) for k, i, t in STREAM)}
TOTAL = len(DONE)
PADDED = TOTAL + SLOTS
assert PADDED % SLOTS == 0
BANKS = 4


def freed(tiles):
    return BANKS + tiles


def pack(a):
    def cols(w, width=256):
        return [w[:, c:c + width].reshape(-1, 128, width).transpose(1, 0, 2) for c in range(0, w.shape[1], width)]

    def ffn(w_in, w_out):
        gate, up = cols(w_in[:, :DFF]), cols(w_in[:, DFF:])
        down = [w_out[r:r + 256].reshape(2, 128, D).transpose(1, 0, 2) for r in range(0, DFF, 256)]
        return gate, up, down

    def ffn_order(gate, up, down, ada):
        order = [gate[0], up[0]]
        for i in range(1, GROUPS):
            these = [gate[i], up[i], down[i - 1]]
            for j, c in enumerate(these):
                order += [c] + ([ada[3 * (i - 1) + j]] if ada else [])
        return order + [down[-1]]

    chunks = []
    ada = cols(a["ada_w"][0]) + cols(a["ada_w"][1])
    f1 = [ffn(a["ffn_w_in"][l, s], a["ffn_w_out"][l, s]) for l in range(2) for s in range(2)]
    f2 = [ffn(a[f"ffn_{s}_w_in_2"][l], a[f"ffn_{s}_w_out_2"][l]) for l in range(2) for s in ("pre", "post")]
    for kind, i, _ in STREAM:
        if kind == "ada":
            chunks += ada[:ADA_FIRST]
        elif kind == "ffn":
            chunks += ffn_order(*(f1 + f2)[i], ada[slice(*ADA_PARTS[i + 1])] if i < 2 else None)
        elif kind == "pool":
            chunks.append(a["pool_w"][0].reshape(4, 2, 128, 256).transpose(2, 0, 1, 3))
        elif kind == "memkv":
            chunks += cols(a["mem_w_kv_2"][i])
        elif kind == "b_out":
            chunks += cols(a["b_w_out_2"][0], 512)
        else:
            name = {"qkv": "diff_w_qkv", "wo": "diff_w_o", "a_in": "a_w_in_2", "a_out": "a_w_out_2", "b_q": "b_w_q_2"}.get(kind)
            chunks += cols(a[name][0] if name else a["kv_w_2"])
    w = np.zeros((PADDED, 128, CHUNK), np.float32)
    for n, c in enumerate(chunks):
        w[n] = c.reshape(128, CHUNK)
    at, n = vector_columns()
    vec = np.zeros((128, n), np.float32)
    for name, col in at.items():
        v = a[name].reshape(-1, 64) if name in TWICE else a[name].reshape(-1, 128)
        if name in TWICE:
            v = np.concatenate([v, v], 1)
        vec[:, col:col + len(v)] = v.T

    def fm(v):
        return v.T.reshape(KT, 128, -1).transpose(1, 0, 2)

    arrays = dict(
        W=w.reshape(PADDED * 128, CHUNK),
        XT=np.concatenate([fm(a["x"][0]), fm(a["ctx"][0])], 2), MEMT=fm(a["mem_2"][0]),
        VEC=vec, CST=constants()[1], ICNT=pool_counts(), BT=bias_tables(), REL=a["rel_bias_2"],
        LAM=np.broadcast_to(a["diff_lam"][0].reshape(1, 256), (128, 256)),
        W0B=np.broadcast_to(a["a_w0_2"][0].reshape(1, RW), (128, RW)),
        LORA=np.concatenate([a["a_w_up_2"][0], a["a_a_up_2"][0]], 0), GUP=a["a_g_up_2"][0])
    return {k: np.ascontiguousarray(v) for k, v in arrays.items()}




def build(nc, W, XT, MEMT, VEC, CST, ICNT, BT, REL, LAM, W0B, LORA, GUP, OUT, stop=None):
    f32, f32r = mybir.dt.float32, mybir.dt.float32r
    ACT, ALU, AX = mybir.ActivationFunctionType, mybir.AluOpType, mybir.AxisListType
    add, sub, mult, amax = ALU.add, ALU.subtract, ALU.mult, ALU.max
    vat, nvec = vector_columns()
    cat, _ = constants()
    ncst = CST.shape[1]
    ds = bass.ds
    def ffn_pass(f):
        tiles = FFN_ADA_PASS if f < 2 else FFN_PASS
        n0 = FIRST["ffn", f]
        n = len(tiles)
        gap = n // 3
        ada = [n0 + 2 + gap * j + 1 for j in range(3)] if f < 2 else []
        return n, sum(max(t, 1) for t in tiles), sum(tiles), n0 + 2 + gap, n0 + 2 + 2 * gap, ada, n0 + 2 + n * (GROUPS - 1)


    with ExitStack() as ctx:
        def sb(name, shape, dt=f32):
            return ctx.enter_context(nc.sbuf_tensor(name, shape, dt))

        def sem(name):
            return ctx.enter_context(nc.semaphore(name))

        wraw = sb("wraw", [128, SLOTS, CHUNK])
        whi = sb("whi", [128, SLOTS, CHUNK], f32r)
        wlo = sb("wlo", [128, SLOTS, CHUNK], f32r)
        x = sb("x", [128, KT, NTOK])
        tsq = sb("tsq", [128, KT * NTOK])
        vec = sb("vec", [128, nvec])
        cst = sb("cst", [128, ncst])
        mods = sb("mods", [128, 2, 72, 2])
        sc = sb("sc", [128, 2 * KT])
        cs = sb("cs", [128, KT, 4], f32r)
        acol = sb("acol", [128, 2, 3, KT, 2])
        gcol = sb("gcol", [128, 2, 3, KT, 2])
        rstd = sb("rstd", [128, NTOK])
        lamb = sb("lamb", [128, 256])
        cols = sb("cols", [128, 64])
        with nc.sbuf_tensor("hh", [128, KT, NTOK], f32r) as hh, nc.sbuf_tensor("hl", [128, KT, NTOK], f32r) as hl:
            pass
        big = sb("big", [128, 2 * KT * NTOK])
        with nc.sbuf_tensor("ah", [128, 2, NTOK], f32r) as ah, nc.sbuf_tensor("al", [128, 2, NTOK], f32r) as al:
            pass
        hid = sb("hid", [128, 4 * NTOK])
        scr = sb("scr", [128, 10240])
        ps_g = ctx.enter_context(nc.psum_tensor("ps_g", [128, 2, 512], f32))
        ps_u = ctx.enter_context(nc.psum_tensor("ps_u", [128, 2, 512], f32))
        ps_o = ctx.enter_context(nc.psum_tensor("ps_o", [128, 4, 512], f32))
        bias_rows = nc.dram_tensor("bias_rows", [3 * 4 * 512], f32, kind="Internal")

        def V(name, i=0, n=1):
            return vec[:, vat[name] + i:vat[name] + i + n]

        def C(name, n=128):
            return cst[:, cat[name]:cat[name] + n]

        ident, ones, blk = C("ident"), C("ones"), C("blk")
        BANK = [ps_g[:, 0, :], ps_g[:, 1, :], ps_u[:, 0, :], ps_u[:, 1, :]]
        HALVES = (slice(0, NX), slice(NX, NTOK))

        w_here = [sem(f"w_here{s}") for s in range(SLOTS)]
        w_hi, w_lo = sem("w_hi"), sem("w_lo")
        mm_done = sem("mm_done")
        o_free = sem("o_free")
        c_in, x_in, m_in, ic_in, bt_in, rel_in, lora_in, lam_in = (sem(s) for s in (
            "c_in", "x_in", "m_in", "ic_in", "bt_in", "rel_in", "lora_in", "lam_in"))
        nm_sq, nm_sum, nm_std, nm_rstd = sem("nm_sq"), sem("nm_sum"), sem("nm_std"), sem("nm_rstd")
        nm_t, nm_hi, h_ready = sem("nm_t"), sem("nm_hi"), sem("h_ready")
        g_act, u_mul, a_hi, a_ready = sem("g_act"), sem("u_mul"), sem("a_hi"), sem("a_ready")
        ad_silu, ad_hi, ad_lo, ad_turn, ad_col = (sem(n) for n in ("ad_silu", "ad_hi", "ad_lo", "ad_turn", "ad_col"))
        act_seq, dve_seq = sem("act_seq"), sem("dve_seq")
        y_hi, y_ready = sem("y_hi"), sem("y_ready")
        pl_diff = sem("pl_diff")
        lam_sum, lam_exp = sem("lam_sum"), sem("lam_exp")
        ro_mm, ro_sin, ro_done = sem("ro_mm"), sem("ro_sin"), sem("ro_done")
        sl_sq, sl_sum, sl_std, sl_y = sem("sl_sq"), sem("sl_sum"), sem("sl_std"), sem("sl_y")
        hn_sq, hn_sum, hn_std, hn_done = sem("hn_sq"), sem("hn_sum"), sem("hn_std"), sem("hn_done")
        at_s, at_m, at_e, at_p = sem("at_s"), sem("at_m"), sem("at_e"), sem("at_p")
        at_b = [sem("at_b0"), sem("at_b1")]
        at_t, at_c, at_o, at_y = sem("at_t"), sem("at_c"), sem("at_o"), sem("at_y")
        bi_row, bi_sb, bi_dram = sem("bi_row"), sem("bi_sb"), sem("bi_dram")
        rw = {n: sem("rw_" + n) for n in (
            "shift", "lora", "z", "zb", "zs", "a_mm", "a_act", "a_free", "g_mm", "g_act", "sq", "ss", "std", "kk", "bsq", "bsum", "bon",
            "cum", "dec", "feat", "tp", "tm", "lp", "lmask", "p", "pm", "t", "tt", "mv", "mvx", "tx", "txs", "rp", "rps",
            "gz", "gzs", "s", "ss2", "y", "yout", "mean", "cen", "var", "vstd", "fin")}
        out_done = sem("out_done")
        block = ctx.enter_context(nc.Block())

        def cut(tensor, first, count, pattern=None, **kw):
            v = tensor[:, first:first + count]
            return v.rearrange(pattern, **kw) if pattern else v

        pad = [cut(scr, i * 1088, 1088, "p (a s u) -> p a s u", a=2, s=2) for i in range(3)]
        icnt = cut(scr, 3 * 1088, 16 * NX)
        q_d = cut(scr, 0, 2048, "p (h n) -> p h n", h=8)
        k_d = cut(scr, 2048, 4096, "p (h n) -> p h n", h=8)
        v_d = cut(scr, 6144, 4096, "p (t n) -> p t n", t=4)
        ada_rows = scr[0:4, 0:256 * ADA_FFN]
        y_all = cut(tsq, 0, 2048, "p (k n) -> p k n", n=NX)
        probs = [cut(tsq, 2048 + 1024 * i, 1024) for i in range(2)]
        probs_t = [cut(big, 768 * i, 768, "p (b n) -> p b n", n=128) for i in range(2)]
        mem_x = cut(scr, 0, 2048, "p (k n) -> p k n", n=NX)
        mem_k = cut(scr, 2048, 512, "p (k n) -> p k n", n=NX)
        mem_v = cut(scr, 2560, 512, "p (t n) -> p t n", n=256)
        proj = cut(scr, 3072, 20 * 257, "p (i n) -> p i n", n=257)
        mem_q = {0: cut(scr, 8212, 512, "p (k n) -> p k n", n=NX), 1: cut(scr, 7680, 512, "p (k n) -> p k n", n=NX)}
        r_, k_, v_ = proj[:, 0:6, 1:257], proj[:, 6:12, 1:257], proj[:, 12:18, 1:257]
        shifted = cut(big, 0, 20 * NX, "p (i n) -> p i n", n=NX)
        zs = cut(big, 0, 2 * RW, "p (u n) -> p u n", n=RW)
        aa = cut(big, 1536, 1536, "p (i n) -> p i n", n=NX)
        kk = cut(big, 3072, 1536, "p (i n) -> p i n", n=NX)
        gg = cut(big, 4608, 1536, "p (i n) -> p i n", n=NX)
        bon = cut(big, 6144, 1536, "p (i n) -> p i n", n=NX)
        lora = cut(scr, 0, RW)
        gup = cut(scr, RW, RW)
        w0b = cut(tsq, 2048, RW)
        dec = cut(scr, 8724, 768, "p (e n) -> p e n", n=NX)
        dinc, dexc, dinv = dec[:, 0, :], dec[:, 1, :], dec[:, 2, :]
        gi = cut(scr, 9492, 128, "p (c n) -> p c n", n=64)
        zd = cut(scr, 9620, 192, "p (c n) -> p c n", n=64)
        tmaj = cut(tsq, 2048, 1024, "p (e u n) -> p e u n", e=4, u=2)
        lp = cut(tsq, 3072, 1024, "p (m e n) -> p m e n", m=4, e=2)
        mp = cut(scr, 0, 1024, "p (m e n) -> p m e n", m=4, e=2)
        xs = cut(scr, 1024, 512, "p (m n) -> p m n", m=4)
        tx = cut(scr, 1536, 512, "p (m n) -> p m n", m=4)
        ti = cut(big, 7680, 512, "p (m n) -> p m n", m=4)
        tit = cut(hid, 0, 512, "p (m n) -> p m n", m=4)
        pp = cut(hid, 512, 512, "p (m n) -> p m n", m=4)
        ar = cut(hid, 1024, 512, "p (u e n) -> p u e n", u=2, e=2)
        be = cut(hid, 1536, 256, "p (u n) -> p u n", u=2)
        ka = cut(hid, 1792, 256, "p (u n) -> p u n", u=2)
        rp = cut(rstd, 0, 256, "p (u n) -> p u n", u=2)
        st2 = cut(rstd, 256, 128, "p (c n) -> p c n", n=64)
        k_g = cut(scr, 3072, 1536, "p (k n) -> p k n", n=NX)
        v_g = cut(scr, 4608, 1536, "p (t n) -> p t n", n=RW)
        q_g = cut(scr, 6144, 1536, "p (k n) -> p k n", n=NX)
        bias = [cut(scr, 8192 + 768 * i, 768, "p (g n) -> p g n", g=3) for i in range(2)]
        bt = scr[0:32, 0:3072]
        rowb = scr[0:4, 3072:4608]
        rel = cols[0:32, 40:52]
        lam_col = cols[:, 52:53]
        qgain = cols[:, 53:56]

        two = lambda v: v.rearrange("p (u n) -> p u n", u=2)
        HEADS = lambda h: (h // 2, slice(64 * (h % 2), 64 * (h % 2) + 64))

        def att_diff(g0):
            units = []
            for h in range(DIFF_HEADS):
                for tt in range(2):
                    t = slice(tt * 128, (tt + 1) * 128)
                    units.append(dict(
                        scores=[((slice(0, 128), j, slice(0, 512)), q_d[64 * j:64 * j + 64, h, t], k_d[64 * j:64 * j + 64, h, :])
                                for j in range(2)], width=512, subs=2, nb=4, rows=slice(0, 128),
                        v=[v_d[:, b, h * 128:(h + 1) * 128] for b in range(4)], y=y_all[:, h, t], bias=None))
            return units

        def att_mem(l):
            units = []
            for h in range(4):
                k, r = HEADS(h)
                for tt in range(2):
                    t = slice(tt * 128, (tt + 1) * 128)
                    units.append(dict(
                        scores=[((slice(0, 128), 0, slice(0, 256)), mem_q[l][r, k, t], mem_k[r, k, :])], width=256, subs=1, nb=2,
                        rows=r, v=[mem_v[:, b, h * 64:(h + 1) * 64] for b in range(2)],
                        y=y_all[r, (6 if l == 0 else 2) + k, t], bias=None))
            return units

        def att_dil():
            units = []
            for j in range(4):
                for tt in range(2):
                    t = slice(tt * 128, (tt + 1) * 128)
                    sc_, v = [], []
                    for g in range(3):
                        k, r = HEADS(4 * g + j)
                        sc_.append(((slice(0, 128), g // 2, slice(256 * (g % 2), 256 * (g % 2) + 256)), q_g[r, k, t], k_g[r, k, :]))
                        v += [v_g[:, b, (4 * g + j) * 64:(4 * g + j + 1) * 64] for b in range(2)]
                    k, r = HEADS(j)
                    units.append(dict(scores=sc_, width=768, subs=1, nb=6, rows=r, v=v, y=y_all[r, k, t], bias=(j, tt)))
            return units

        ATT = [att_diff(0), att_mem(0), att_dil(), att_mem(1)]
        AT0 = [sum(len(a) for a in ATT[:i]) for i in range(5)]
        DIL0 = AT0[2]

        @block.sync
        def _(sp):
            sp.dma_start(vec[:], VEC).then_inc(c_in, 16)
            sp.dma_start(cst[:], CST).then_inc(c_in, 16)
            for s in range(SLOTS):
                sp.dma_start(wraw[:, s, :], W[s * 128:(s + 1) * 128, :]).then_inc(w_here[s], 16)
            with sp.Fori(1, PADDED // SLOTS) as i:
                for s in range(SLOTS):
                    sp.wait_ge(w_lo, i * SLOTS + (s + 1 - SLOTS))
                    sp.dma_start(wraw[:, s, :], W[ds(i * (SLOTS * 128) + s * 128, 128), :]).then_inc(w_here[s], 16)
            sp.wait_ge(o_free, freed(TILE0[-1] + KT))
            sp.dma_start(OUT, x[:, :, 0:NX]).then_inc(out_done, 16)
            sp.wait_ge(out_done, 16)

        @block.gpsimd
        def _(pool):
            pool.dma_start(x[:], XT).then_inc(x_in, 16)
            pool.dma_start(lamb[:], LAM).then_inc(lam_in, 16)
            pool.dma_start(rel, REL).then_inc(rel_in, 16)
            pool.wait_ge(ad_turn, 2)
            pool.dma_start(icnt, ICNT).then_inc(ic_in, 16)
            pool.wait_ge(o_free, freed(TILE0[FIRST["ffn", 3]]))
            pool.dma_start(mem_x, MEMT).then_inc(m_in, 16)
            pool.wait_ge(mm_done, DONE[FIRST["a_in", 0] - 1])
            pool.dma_start(lora, LORA).then_inc(lora_in, 16)
            pool.dma_start(gup, GUP).then_inc(lora_in, 16)
            pool.wait_ge(o_free, freed(TILE0[FIRST["a_out", 0]]))
            pool.dma_start(w0b, W0B).then_inc(lora_in, 16)
            pool.wait_ge(o_free, freed(TILE0[FIRST["ffn", 5]]))
            pool.dma_start(bt, BT).then_inc(bt_in, 16)
            pool.wait_ge(bi_sb, 3)
            pool.dma_start(bass.AP(bias_rows, 0, [[512, 4], [2048, 3], [1, 512]]), rowb.rearrange("p (g n) -> p g n", g=3)).then_inc(bi_dram, 16)
            pool.wait_ge(bi_dram, 16)
            pool.dma_start(mem_x, MEMT).then_inc(m_in, 16)
            pool.wait_ge(o_free, freed(TILE0[FIRST["b_out", 0]]))
            for u, unit in enumerate(ATT[2]):
                j, tt = unit["bias"]
                if u >= 2:
                    pool.wait_ge(at_m, DIL0 + u - 1)
                pool.dma_start(bias[u % 2], bass.AP(bias_rows, j * 512 + tt * 128, [[1, 128], [2048, 3], [1, 256]])).then_inc(at_b[u % 2], 16)
            for slot in at_b:
                pool.wait_ge(slot, 16 * (len(ATT[2]) // 2))

        @block.scalar
        def _(act):
            st = {"seq": 0, "k": 0, "t": 0, "h": 0, "hn": 0, "y": 0}

            def link(ins):
                st["seq"] += 1
                ins.then_inc(act_seq, 1)
                act.wait_ge(act_seq, st["seq"])

            def split_hi(n, i=None, step=1, per=SLOTS):
                if n >= PADDED:
                    return
                off = 0 if i is None else i
                act.wait_ge(w_here[n % SLOTS], off * (16 * per // SLOTS) + 16 * (n // SLOTS + 1))
                if n >= SLOTS:
                    act.wait_ge(mm_done, off * step + DONE[n - SLOTS])
                nc.scalar.activation(whi[:, n % SLOTS, :], wraw[:, n % SLOTS, :], ACT.Copy).then_inc(w_hi, 1)

            def norm(src, N, B, mode, ready, n):
                k = st["k"]
                st["k"] += 1
                if st["h"]:
                    act.wait_ge(h_ready, st["h"])
                nc.scalar.activation(cols[:, 61:62], C("eps", 1), ACT.Sqrt)
                for d in range(KT):
                    ready(act, d)
                    nc.scalar.activation(tsq[:, d * NTOK:d * NTOK + N], src(d)[:, 0:N], ACT.Square).then_inc(nm_sq, 1)
                act.wait_ge(nm_sum, k + 1)
                nc.scalar.activation(rstd[:, 0:N], ps_g[:, 0, 0:N], ACT.Sqrt, bias=C("eps", 1), scale=1.0 / D).then_inc(nm_std, 1)
                if n and mode == "split":
                    act.wait_ge(mm_done, DONE[n - 1])
                for d in range(KT):
                    for j in range(N // NX):
                        st["t"] += 1
                        if mode == "final":
                            continue
                        act.wait_ge(nm_t, st["t"])
                        src_t = tsq[:, d * NTOK + j * NX:d * NTOK + (j + 1) * NX]
                        dst = src_t if mode == "plain" else hh[:, d, HALVES[j]]
                        if B is None:
                            nc.scalar.activation(dst, src_t, ACT.Copy).then_inc(nm_hi, 1)
                        else:
                            nc.scalar.activation(dst, src_t, ACT.Identity, bias=B(d, j)).then_inc(nm_hi, 1)
                        st["h"] += mode == "split"

            def after(n):
                return lambda eng, d: eng.wait_ge(o_free, freed(TILE0[n] - KT + d + 1))

            def ffn(f, N):
                n0, g0 = FIRST["ffn", f], f * GROUPS
                sg = tsq[:, 0:1024].rearrange("p (j n) -> p j n", j=2)
                tmp = tsq[:, 1024:2048].rearrange("p (j n) -> p j n", j=2)

                def silu(done, group):
                    act.wait_ge(mm_done, done)
                    if group is not None:
                        act.wait_ge(u_mul, group)
                    nc.scalar.activation(sg[:, :, 0:N], ps_g[:, :, 0:N], ACT.Silu).then_inc(g_act, 1)

                def hidden(group):
                    act.wait_ge(u_mul, group + 1)
                    nc.scalar.activation(ah[:, :, 0:N], tmp[:, :, 0:N], ACT.Copy).then_inc(a_hi, 1)

                per, step, _, _, n_down, _, n_last = ffn_pass(f)
                silu(DONE[n0], g0 or None)
                split_hi(n0 + 3)
                split_hi(n0 + 4)
                hidden(g0)
                with act.Fori(0, GROUPS - 1) as i:
                    split_hi(n0 + 5, i, step, per)
                    silu(i * step + DONE[n0 + 2], i + (g0 + 1))
                    for n in range(n0 + 6, n0 + 5 + per):
                        split_hi(n, i, step, per)
                        if n - SLOTS == n_down:
                            hidden(i + (g0 + 1))
                split_hi(n_last + SLOTS)
                if f < 2:
                    act.wait_ge(ad_col, f + 2)

            def chunks(stage, i):
                n0 = FIRST[stage, i]
                for n in range(n0, FIRST_AFTER[stage, i]):
                    split_hi(n + SLOTS)

            def mod(l, a):
                return lambda d, j: mods[:, l, 24 * a + d, j:j + 1]

            def head_norm(n_banks):
                st["hn"] += 1
                act.wait_ge(hn_sum, st["hn"])
                for b in range(n_banks):
                    ins = nc.scalar.activation(hid[:, b * 512:(b + 1) * 512], BANK[b], ACT.Sqrt, bias=C("eps", 1), scale=1.0 / 64)
                ins.then_inc(hn_std, 1)

            def split_y(src, nt, width=NX):
                nc.scalar.activation(hh[:, 0:nt, 0:width], src, ACT.Copy).then_inc(y_hi, 1)

            def attend(a):
                U = ATT[a]

                def copy(u):
                    g = AT0[a] + u
                    act.wait_ge(at_t, g + 1)
                    if g >= 2:
                        act.wait_ge(at_o, g - 1)
                    nb = U[u]["nb"]
                    for b in range(0, nb, 4):
                        w = min(4, nb - b)
                        ins = nc.scalar.activation(probs_t[g % 2][:, b:b + w, :], ps_o[:, b // 4, 0:w * 128].rearrange("p (b n) -> p b n", n=128), ACT.Copy)
                    ins.then_inc(at_c, 1)

                for u, unit in enumerate(U):
                    g = AT0[a] + u
                    act.wait_ge(at_m, g + 1)
                    if g >= 2:
                        act.wait_ge(at_t, g - 1)
                    bank = ps_g if g % 2 == 0 else ps_u
                    w = unit["width"]
                    for j in range(unit["subs"]):
                        src = bank[:, j, 0:w] if unit["bias"] is None else probs[g % 2][:, 0:w]
                        ins = nc.scalar.activation(probs[g % 2][:, j * w:(j + 1) * w], src, ACT.Exp, bias=cols[:, 4 * (g % 2) + j:4 * (g % 2) + j + 1],
                                                   accum_out=cols[:, 8 + 4 * (g % 2) + j:9 + 4 * (g % 2) + j])
                    ins.then_inc(at_e, 1)
                    if u:
                        copy(u - 1)
                copy(len(U) - 1)

            act.wait_ge(c_in, 32)
            nc.scalar.activation(sc[:], V("c", 0, 16), ACT.Silu).then_inc(ad_silu, 1)
            act.wait_ge(ad_silu, 1)
            nc.scalar.activation(cs[:, :, 0:2], sc[:].rearrange("p (v k) -> p k v", v=2), ACT.Copy).then_inc(ad_hi, 1)
            for n in range(SLOTS):
                split_hi(n)
            for n in range(ADA_FIRST):
                split_hi(n + SLOTS)
            act.wait_ge(ad_col, 1)
            norm(lambda d: x[:, d, :], NTOK, mod(0, 0), "split", lambda eng, d: eng.wait_ge(x_in, 16), FIRST["ffn", 0])
            ffn(0, NTOK)
            norm(lambda d: x[:, d, :], NTOK, mod(0, 1), "plain", after(FIRST["pool", 0]), FIRST["pool", 0])
            for g in range(4):
                act.wait_ge(pl_diff, g + 1)
                nc.scalar.activation(hh[:, 2 * g:2 * g + 2, :], tsq[:, 1024 * g:1024 * (g + 1)].rearrange("p (a n) -> p a n", a=2), ACT.Copy).then_inc(y_hi, 1)
            chunks("pool", 0)
            norm(lambda d: x[:, d, :], NTOK, mod(0, 2), "split", after(FIRST["ffn", 1]), FIRST["ffn", 1])
            ffn(1, NTOK)
            norm(lambda d: x[:, d, :], NTOK, mod(1, 0), "split", after(FIRST["ffn", 2]), FIRST["ffn", 2])
            ffn(2, NTOK)
            norm(lambda d: x[:, d, :], NTOK, mod(1, 1), "split", after(FIRST["qkv", 0]), FIRST["qkv", 0])
            chunks("qkv", 0)
            act.wait_ge(lam_sum, 1)
            nc.scalar.activation(cols[:, 58:60], cols[:, 56:58], ACT.Exp).then_inc(lam_exp, 1)
            attend(0)
            act.wait_ge(sl_sum, 1)
            for b in range(4):
                ins = nc.scalar.activation(big[:, 4096 + 512 * b:4608 + 512 * b], BANK[b], ACT.Sqrt, bias=C("eps", 1), scale=1.0 / 128)
            ins.then_inc(sl_std, 1)
            act.wait_ge(sl_y, 1)
            split_y(y_all, KT)
            chunks("wo", 0)
            norm(lambda d: x[:, d, :], NX, mod(1, 2), "split", after(FIRST["ffn", 3]), FIRST["ffn", 3])
            ffn(3, NX)
            norm(lambda d: x[:, d, :], NX, None, "final", after(FIRST["ffn", 4]), FIRST["ffn", 4])
            t_final = st["t"]
            norm(lambda d: x[:, d, :], NX, None, "split", lambda eng, d: eng.wait_ge(nm_t, t_final), FIRST["ffn", 4])
            ffn(4, NX)
            norm(lambda d: mem_x[:, d, :], NX, None, "split", lambda eng, d: eng.wait_ge(m_in, 16), FIRST["memkv", 0])
            chunks("memkv", 0)
            head_norm(1)
            norm(lambda d: x[:, d, :], NX, None, "split", after(FIRST["memkv", 0]), FIRST["a_in", 0])
            chunks("a_in", 0)
            head_norm(1)
            act.wait_ge(rw["shift"], 1)
            nc.scalar.activation(proj[0:64, 18, 1:257], proj[0:64, 18, 1:257], ACT.Tanh)
            nc.scalar.activation(proj[:, 19, 1:257], proj[:, 19, 1:257], ACT.Sigmoid).then_inc(rw["lora"], 1)
            act.wait_ge(rw["zb"], 1)
            nc.scalar.activation(zs, zs, ACT.Sigmoid).then_inc(rw["zs"], 1)
            for i in range(RT):
                act.wait_ge(rw["a_mm"], i + 1)
                nc.scalar.activation(aa[:, i, :], ps_o[:, i % 2, 0:NX], ACT.Sigmoid, bias=V("a_a0_2", i)).then_inc(rw["a_act"], 1)
            for i in range(RT):
                act.wait_ge(rw["g_mm"], i + 1)
                nc.scalar.activation(gg[:, i, :], ps_o[:, 2 + i % 2, 0:NX], ACT.Copy).then_inc(rw["g_act"], 1)
            act.wait_ge(rw["ss"], 1)
            for b in range(3):
                ins = nc.scalar.activation(hid[:, b * 512:(b + 1) * 512], BANK[b], ACT.Sqrt)
            ins.then_inc(rw["std"], 1)
            c0 = math.exp(-0.5)
            for i in range(RT):
                act.wait_ge(rw["cum"], i + 1)
                if i:
                    act.wait_ge(rw["s"], 2 * i)
                    act.wait_ge(rw["ss2"], 2 * i)
                cum = ps_g[:, :, 0:256].rearrange("p u (e n) -> p u e n", e=2)
                nc.scalar.activation(dinc.rearrange("p (u n) -> p u n", u=2), cum[:, :, 0, :], ACT.Exp, scale=-c0)
                nc.scalar.activation(dexc.rearrange("p (u n) -> p u n", u=2), cum[:, :, 1, :], ACT.Exp, scale=-c0)
                nc.scalar.activation(dinv.rearrange("p (u n) -> p u n", u=2), cum[:, :, 0, :], ACT.Exp, scale=c0).then_inc(rw["dec"], 1)
                act.wait_ge(rw["tp"], i + 1)
                nc.scalar.activation(tmaj[:, 0:2], ps_g[:, 0, :].rearrange("p (e u n) -> p e u n", e=2, u=2), ACT.Copy)
                nc.scalar.activation(tmaj[:, 2:4], ps_g[:, 1, :].rearrange("p (e u n) -> p e u n", e=2, u=2), ACT.Copy)
                al_ = ps_g[:, 1, 256:512].rearrange("p (u q n) -> p q u n", u=2, q=2)
                nc.scalar.activation(xs[:, :, 0:64].rearrange("p (q u) n -> p q u n", q=2), al_, ACT.Copy).then_inc(rw["tm"], 1)
                act.wait_ge(rw["mv"], i + 1)
                nc.scalar.activation(xs[:, :, 64:128], ps_o[:, 3, 0:256].rearrange("p (m n) -> p m n", m=4), ACT.Copy).then_inc(rw["mvx"], 1)
                act.wait_ge(rw["tx"], i + 1)
                nc.scalar.activation(tx, ps_o[:, 0, :].rearrange("p (m n) -> p m n", m=4), ACT.Copy).then_inc(rw["txs"], 1)
            act.wait_ge(rw["var"], 1)
            for b in range(3):
                ins = nc.scalar.activation(hid[:, b * 512:(b + 1) * 512], BANK[b], ACT.Sqrt, bias=C("lnx_eps", 1), scale=1.0 / 64)
            ins.then_inc(rw["vstd"], 1)
            act.wait_ge(rw["fin"], 1)
            attend(1)
            act.wait_ge(at_y, AT0[2])
            split_y(y_all, KT)
            chunks("a_out", 0)
            norm(lambda d: x[:, d, :], NX, None, "split", after(FIRST["ffn", 5]), FIRST["ffn", 5])
            ffn(5, NX)
            norm(lambda d: x[:, d, :], NX, None, "split", after(FIRST["kv", 0]), FIRST["kv", 0])
            chunks("kv", 0)
            head_norm(3)
            norm(lambda d: x[:, d, :], NX, None, "split", lambda eng, d: None, FIRST["ffn", 6])
            ffn(6, NX)
            norm(lambda d: mem_x[:, d, :], NX, None, "split", lambda eng, d: eng.wait_ge(m_in, 32), FIRST["memkv", 1])
            chunks("memkv", 1)
            head_norm(1)
            norm(lambda d: x[:, d, :], NX, None, "split", after(FIRST["memkv", 1]), FIRST["b_q", 0])
            chunks("b_q", 0)
            head_norm(3)
            head_norm(1)
            attend(2)
            attend(3)
            act.wait_ge(at_y, AT0[4])
            split_y(y_all[:, 0:4, :], 4)
            chunks("b_out", 0)
            norm(lambda d: x[:, d, :], NX, None, "split", after(FIRST["ffn", 7]), FIRST["ffn", 7])
            ffn(7, NX)

        @block.vector
        def _(dve):
            st = {"seq": 0, "k": 0, "t": 0, "hi": 0, "hn": 0, "y": 0}
            stt, tt_, ts_ = nc.vector.scalar_tensor_tensor, nc.vector.tensor_tensor, nc.vector.tensor_scalar

            def link(ins):
                st["seq"] += 1
                ins.then_inc(dve_seq, 1)
                dve.wait_ge(dve_seq, st["seq"])

            def split_lo(n, i=None, per=SLOTS):
                if n >= PADDED:
                    return
                dve.wait_ge(w_hi, n + 1 if i is None else i * per + (n + 1))
                tt_(wlo[:, n % SLOTS, :], wraw[:, n % SLOTS, :], whi[:, n % SLOTS, :].bitcast(f32), sub).then_inc(w_lo, 1)

            def norm(src, N, A, B, mode):
                k = st["k"]
                st["k"] += 1
                dve.wait_ge(nm_std, k + 1)
                nc.vector.reciprocal(rstd[:, 0:N], rstd[:, 0:N]).then_inc(nm_rstd, 1)
                dve.wait_ge(nm_rstd, k + 1)
                units = [(d, j) for d in range(KT) for j in range(N // NX)]

                def scaled(d, j):
                    dst = src(d)[:, HALVES[j]] if mode == "final" else tsq[:, d * NTOK + j * NX:d * NTOK + (j + 1) * NX]
                    stt(dst, src(d)[:, HALVES[j]], A(d, j), rstd[:, HALVES[j]], mult, mult).then_inc(nm_t, 1)
                    st["t"] += 1

                def rest(d, j):
                    st["hi"] += 1
                    dve.wait_ge(nm_hi, st["hi"])
                    t = tsq[:, d * NTOK + j * NX:d * NTOK + (j + 1) * NX]
                    up = hh[:, d, HALVES[j]].bitcast(f32)
                    if B is None:
                        tt_(hl[:, d, HALVES[j]], t, up, sub).then_inc(h_ready, 1)
                    else:
                        stt(hl[:, d, HALVES[j]], t, B(d, j), up, add, sub).then_inc(h_ready, 1)

                lag = 3 if mode == "split" else 0
                for q in range(len(units) + lag):
                    if q < len(units):
                        scaled(*units[q])
                    if mode == "split" and q >= lag:
                        rest(*units[q - lag])
                if mode == "plain":
                    st["hi"] += len(units)
                    dve.wait_ge(nm_hi, st["hi"])

            def out_tiles(n):
                for q in range(DONE[n] - (DONE[n - 1])):
                    dve.wait_ge(mm_done, DONE[n - 1] + q + 1)
                    yield ps_o[:, (TILE0[n] + q) % 4, :]

            def residual(src, d, N, gate):
                for j in range(N // NX):
                    ins = stt(x[:, d, HALVES[j]], src[:, HALVES[j]], gate(d, j), x[:, d, HALVES[j]], mult, add)
                ins.then_inc(o_free, 1)

            def ffn(f, N, gate):
                n0, g0 = FIRST["ffn", f], f * GROUPS
                per, step, _, n_up, n_down, n_ada, n_last = ffn_pass(f)
                sg = tsq[:, 0:1024].rearrange("p (j n) -> p j n", j=2)
                tmp = tsq[:, 1024:2048].rearrange("p (j n) -> p j n", j=2)

                def product(group, done, last=True):
                    dve.wait_ge(mm_done, done)
                    if last:
                        dve.wait_ge(a_ready, group)
                    dve.wait_ge(g_act, group + 1)
                    tt_(tmp[:, :, 0:N], sg[:, :, 0:N], ps_u[:, :, 0:N], mult).then_inc(u_mul, 1)

                def hidden(group):
                    dve.wait_ge(a_hi, group + 1)
                    tt_(al[:, :, 0:N], tmp[:, :, 0:N], ah[:, :, 0:N].bitcast(f32), sub).then_inc(a_ready, 1)

                def down(n, done):
                    for d in range(KT):
                        dve.wait_ge(mm_done, done + (d + 1))
                        residual(ps_o[:, (TILE0[n] + d) % BANKS, :], d, N, gate)

                product(g0, DONE[n0 + 1], g0 > 0)
                split_lo(n0 + 3)
                split_lo(n0 + 4)
                hidden(g0)
                with dve.Fori(0, GROUPS - 1) as i:
                    split_lo(n0 + 5, i, per)
                    for n in range(n0 + 3, n0 + 2 + per):
                        if n == n_up:
                            product(i + (g0 + 1), i * step + DONE[n])
                        elif n == n_down:
                            down(n, i * step + DONE[n - 1])
                        else:
                            ada_out(n, n_ada.index(n), i, step)
                        if n == n_down and not n_ada:
                            split_lo(n_up + SLOTS, i, per)
                        if n != n_up or n_ada:
                            split_lo(n + SLOTS, i, per)
                        if n == n_down:
                            hidden(i + (g0 + 1))
                down(n_last, DONE[n_last - 1])
                split_lo(n_last + SLOTS)
                if f < 2:
                    ada_part(f + 1)

            def ada_out(n, c, i=None, step=0):
                off, at = (0, 256 * c) if i is None else (i * step, i * 768 + 256 * c)
                rows = ada_rows[:, at:at + 256] if i is None else ada_rows[:, ds(at, 256)]
                for q in range(DONE[n] - (DONE[n - 1] if n else 0)):
                    dve.wait_ge(mm_done, off + ((DONE[n - 1] if n else 0) + q + 1))
                    part = ps_o[0:4, (TILE0[n] + q) % BANKS, 0:256]
                    if q:
                        dve.wait_ge(o_free, freed(TILE0[n] + q) + (0 if i is None else i * sum(FFN_ADA_PASS)))
                        tt_(rows, rows, part, add).then_inc(o_free, 1)
                    else:
                        nc.vector.tensor_copy(rows, part).then_inc(o_free, 1)

            def ada_part(e):
                c0, c1 = ADA_PARTS[e]
                dve.wait_ge(ad_turn, e + 1)
                flat = mods[:].rearrange("p l t v -> p (l t) v")
                ps = ps_u[:, 0, 0:4 * (c1 - c0)].rearrange("p (t v) -> p t v", v=2)
                tt_(flat[:, 2 * c0:2 * c1, 0], ps[:, :, 0], V("ada_b", 2 * c0, 2 * (c1 - c0)), add)
                link(tt_(flat[:, 2 * c0:2 * c1, 1], ps[:, :, 1], V("ada_b", 2 * c0, 2 * (c1 - c0)), add))
                for l, first, last in (((0, 0, 1),), ((0, 1, 3),), ((1, 0, 3),))[e]:
                  m = mods[:, l]
                  for v in range(2):
                    for a in range(first, last):
                        stt(acol[:, l, a, :, v], m[:, 24 * a + 8:24 * a + 16, v], 1.0, V("norm_g", 24 * l + 8 * a, 8), add, mult)
                        gate = m[:, 24 * a + 16:24 * a + 24, v]
                        if a == 1 and l == 0:
                            tt_(gcol[:, l, a, :, v], gate, V("pool_scale", 0, 8), mult)
                        else:
                            ts_(gcol[:, l, a, :, v], gate, 1.0 if a == 1 else 0.5, None, mult)
                nc.vector.memset(cols[:, 60:61], 0.0).then_inc(ad_col, 1)
                dve.wait_ge(ad_col, e + 1)

            def chunks_out(stage, i, take):
                n0 = FIRST[stage, i]
                for n in range(n0, FIRST_AFTER[stage, i]):
                    for q, tile in enumerate(out_tiles(n)):
                        take(n - n0, q, tile)
                    split_lo(n + SLOTS)

            def add_to_x(N, gate, per):
                return lambda c, q, tile: residual(tile, c * per + q, N, gate)

            def head_norm(buf, nt, gain):
                st["hn"] += 1
                sq = hid[:, 0:nt * NX].rearrange("p (k n) -> p k n", n=NX)
                dve.wait_ge(o_free, freed(st["tiles"]))
                if st["hn"] > 1:
                    dve.wait_ge(hn_done, st["hn"] - 1)
                tt_(sq, buf, buf, mult).then_inc(hn_sq, 1)
                dve.wait_ge(hn_std, st["hn"])
                link(nc.vector.reciprocal(sq, sq))
                stt(buf, buf, gain, sq, mult, mult).then_inc(hn_done, 1)

            def rest_y(src, nt, width=NX):
                st["y"] += 1
                dve.wait_ge(y_hi, st["y"])
                tt_(hl[:, 0:nt, 0:width], src, hh[:, 0:nt, 0:width].bitcast(f32), sub).then_inc(y_ready, 1)

            def attend(a):
                U = ATT[a]

                def maximum(u):
                    g, unit = AT0[a] + u, U[u]
                    dve.wait_ge(at_s, g + 1)
                    if g >= 2:
                        dve.wait_ge(at_p, g - 1)
                    bank = ps_g if g % 2 == 0 else ps_u
                    w = unit["width"]
                    nm = cols[:, 4 * (g % 2):4 * (g % 2) + unit["subs"]]
                    if unit["bias"] is None:
                        nc.vector.reduce_max(nm, bank[:, 0:unit["subs"], 0:w], AX.X, negate=True).then_inc(at_m, 1)
                        return
                    dve.wait_ge(at_b[u % 2], 16 * (u // 2 + 1))
                    if g >= 2:
                        dve.wait_ge(at_t, g - 1)
                    s = probs[g % 2][:, 0:w]
                    by_group = "p (g n) -> p g n"
                    tt_(s[:, 0:512].rearrange(by_group, g=2), bank[:, 0, :].rearrange(by_group, g=2), bias[u % 2][:, 0:2, ::-1], add)
                    link(tt_(s[:, 512:768], bank[:, 1, 0:256], bias[u % 2][:, 2, ::-1], add))
                    nc.vector.reduce_max(nm, s, AX.X, negate=True).then_inc(at_m, 1)

                def normalise(u):
                    g, unit = AT0[a] + u, U[u]
                    dve.wait_ge(at_e, g + 1)
                    w = unit["width"]
                    su = cols[:, 8 + 4 * (g % 2):8 + 4 * (g % 2) + unit["subs"]]
                    r = cols[:, 16 + 4 * (g % 2):16 + 4 * (g % 2) + unit["subs"]]
                    link(nc.vector.reciprocal(r, su))
                    p = probs[g % 2]
                    if unit["subs"] == 1:
                        ts_(p[:, 0:w], p[:, 0:w], r[:, 0:1], None, mult).then_inc(at_p, 1)
                    else:
                        link(tt_(r[:, 1:2], r[:, 1:2], lam_col, mult))
                        link(ts_(p[:, w:2 * w], p[:, w:2 * w], r[:, 1:2], None, mult))
                        stt(p[:, 0:w], p[:, 0:w], r[:, 0:1], p[:, w:2 * w], mult, add).then_inc(at_p, 1)

                def result(u):
                    g, unit = AT0[a] + u, U[u]
                    dve.wait_ge(at_o, g + 1)
                    nc.vector.tensor_copy(unit["y"], ps_o[unit["rows"], 2 + g % 2, 0:128]).then_inc(at_y, 1)

                for u in range(len(U) + 2):
                    if u < len(U):
                        maximum(u)
                    if 1 <= u <= len(U):
                        normalise(u - 1)
                    if u >= 2:
                        result(u - 2)

            def xs_(d):
                return x[:, d, :]

            def A_mod(l, a):
                return lambda d, j: acol[:, l, a, d, j:j + 1]

            def B_mod(l, a):
                return lambda d, j: mods[:, l, 24 * a + d, j:j + 1]

            def gate(l, a):
                return lambda d, j: gcol[:, l, a, d, j:j + 1]

            def gain(name, l=0):
                return lambda d, j: V(name, KT * l + d)

            half = lambda d, j: 0.5
            one = lambda d, j: 1.0

            dve.sem_inc(o_free, BANKS)
            dve.wait_ge(ad_hi, 1)
            tt_(cs[:, :, 2:4], sc[:].rearrange("p (v k) -> p k v", v=2), cs[:, :, 0:2].bitcast(f32), sub).then_inc(ad_lo, 1)
            for n in range(SLOTS):
                split_lo(n)
            for n in range(ADA_FIRST):
                ada_out(n, n)
                split_lo(n + SLOTS)
            ada_part(0)
            norm(xs_, NTOK, A_mod(0, 0), B_mod(0, 0), "split")
            ffn(0, NTOK, gate(0, 0))
            link(nc.vector.memset(scr[:, 0:1088], 0.0))
            norm(xs_, NTOK, A_mod(0, 1), None, "plain")
            dve.wait_ge(ic_in, 16)
            for g in range(4):
                h4 = tsq[:, 1024 * g:1024 * (g + 1)].rearrange("p (a s n) -> p a s n", a=2, s=2)
                link(nc.vector.tensor_copy(pad[0][:, :, :, 8:264], h4))
                link(tt_(pad[1][:, :, :, 1:272], pad[0][:, :, :, 0:271], pad[0][:, :, :, 1:272], add))
                cur, lo = 1, 1
                for e in range(g):
                    b, nxt = 1 << e, 3 - cur
                    lo2 = lo + b
                    hi2 = 272 - (2 * b - 1)
                    link(tt_(pad[nxt][:, :, :, lo2:hi2], pad[cur][:, :, :, lo2 - b:hi2 - b], pad[cur][:, :, :, lo2 + b:hi2 + b], add))
                    cur, lo = nxt, lo2
                mean = cut(scr, (3 - cur) * 1088, 1024, "p (a s n) -> p a s n", a=2, s=2)
                link(tt_(mean, pad[cur][:, :, :, 8:264], icnt[:, g * 1024:(g + 1) * 1024].rearrange("p (a s n) -> p a s n", a=2, s=2), mult))
                tt_(h4, mean, h4, sub).then_inc(pl_diff, 1)
            for g in range(4):
                st["y"] += 1
                dve.wait_ge(y_hi, st["y"])
                tt_(hl[:, 2 * g:2 * g + 2, :], tsq[:, 1024 * g:1024 * (g + 1)].rearrange("p (a n) -> p a n", a=2),
                    hh[:, 2 * g:2 * g + 2, :].bitcast(f32), sub).then_inc(y_ready, 1)
            chunks_out("pool", 0, add_to_x(NTOK, gate(0, 1), 8))
            norm(xs_, NTOK, A_mod(0, 2), B_mod(0, 2), "split")
            ffn(1, NTOK, gate(0, 2))
            norm(xs_, NTOK, A_mod(1, 0), B_mod(1, 0), "split")
            ffn(2, NTOK, gate(1, 0))
            norm(xs_, NTOK, A_mod(1, 1), B_mod(1, 1), "split")

            def take_qkv(c, q, tile):
                if c < 4:
                    ts_(q_d[:, 2 * c + q, :], tile[:, 0:NX], 0.125, None, mult).then_inc(o_free, 1)
                elif c < 8:
                    nc.vector.tensor_copy(k_d[:, 2 * (c - 4) + q, :], tile).then_inc(o_free, 1)
                else:
                    nc.vector.tensor_copy(v_d[:, q, 256 * (c - 8):256 * (c - 7)], tile[:, 0:256]).then_inc(o_free, 1)

            chunks_out("qkv", 0, take_qkv)
            for r in range(8):
                z = q_d[:, 2 * r:2 * r + 2, :] if r < 4 else k_d[:, 2 * (r - 4):2 * (r - 4) + 2, 0:NX]
                t = tsq[:, 512 * (r % 4):512 * (r % 4) + 512].rearrange("p (a n) -> p a n", a=2)
                dve.wait_ge(ro_mm, r + 1)
                tt_(t, BANK[r % 4].rearrange("p (a n) -> p a n", a=2), C("sin", 512).rearrange("p (a n) -> p a n", a=2), mult).then_inc(ro_sin, 1)
                link(tt_(z, z, C("cos", 512).rearrange("p (a n) -> p a n", a=2), mult))
                tt_(z, z, t, add).then_inc(ro_done, 1)
            dve.wait_ge(lam_in, 16)
            for j in range(2):
                link(tt_(lamb[:, 128 * j:128 * j + 64], lamb[:, 128 * j:128 * j + 64], lamb[:, 128 * j + 64:128 * j + 128], mult))
            nc.vector.reduce_sum(cols[:, 56:58], lamb[:].rearrange("p (j n) -> p j n", j=2)[:, :, 0:64], AX.X).then_inc(lam_sum, 1)
            dve.wait_ge(lam_exp, 1)
            link(tt_(lam_col, cols[:, 59:60], cols[:, 58:59], sub))
            link(ts_(lam_col, lam_col, -LAM_INIT, None, add))
            attend(0)
            dve.wait_ge(at_y, AT0[1])
            tt_(big[:, 2048:4096], tsq[:, 0:2048], tsq[:, 0:2048], mult).then_inc(sl_sq, 1)
            dve.wait_ge(sl_std, 1)
            link(nc.vector.reciprocal(big[:, 4096:6144], big[:, 4096:6144]))
            link(tt_(tsq[:, 0:2048], tsq[:, 0:2048], big[:, 4096:6144], mult))
            ts_(tsq[:, 0:2048], tsq[:, 0:2048], V("diff_subln_g"), 1.0 - LAM_INIT, mult, mult).then_inc(sl_y, 1)
            rest_y(y_all, KT)
            chunks_out("wo", 0, add_to_x(NX, gate(1, 1), 2))
            norm(xs_, NX, A_mod(1, 2), B_mod(1, 2), "split")
            ffn(3, NX, gate(1, 2))
            norm(xs_, NX, gain("final_g"), None, "final")
            dve.wait_ge(nm_t, st["t"])
            norm(xs_, NX, gain("ffn_pre_norm_2", 0), None, "split")
            ffn(4, NX, half)

            def take_memkv(c, q, tile):
                nc.vector.tensor_copy(mem_k[:, q, :] if c == 0 else mem_v[:, q, :], tile[:, 0:256]).then_inc(o_free, 1)

            norm(lambda d: mem_x[:, d, :], NX, gain("mem_norm_2", 0), None, "split")
            chunks_out("memkv", 0, take_memkv)
            st["tiles"] = TILE0[FIRST["a_in", 0]]
            head_norm(mem_k, 2, V("mem_k_norm_2", 0))
            norm(xs_, NX, gain("mix_norm_2", 0), None, "split")

            def take_in(c, q, tile):
                i = 2 * c + q
                dst = proj[:, i, 1:257] if i < 20 else mem_q[0][:, i - 20, :]
                nc.vector.tensor_copy(dst, tile[:, 0:NX]).then_inc(o_free, 1)

            link(nc.vector.memset(proj[:, :, 0:1], 0.0))
            chunks_out("a_in", 0, take_in)
            link(ts_(qgain, vec[:, vat["mem_q_norm_2"]:vat["mem_q_norm_2"] + 3], 0.125, None, mult))
            st["tiles"] = TILE0[FIRST["a_out", 0]]
            head_norm(mem_q[0], 2, qgain[:, 0:1])
            link(tt_(shifted, proj[:, :, 0:256], proj[:, :, 1:257], sub))
            for i in range(20):
                ins = stt(proj[:, i, 1:257], shifted[:, i, :], V("a_shift_mu_2", i), proj[:, i, 1:257], mult, add)
                if i < 19:
                    link(ins)
            ins.then_inc(rw["shift"], 1)
            dve.wait_ge(rw["shift"], 1)
            dve.wait_ge(lora_in, 48)
            dve.wait_ge(rw["z"], 1)
            for u in range(2):
                bank = ps_g if u == 0 else ps_u
                tt_(zs[:, u, 0:512], bank[:, 0, :], w0b[:, 0:512], add)
                ins = tt_(zs[:, u, 512:768], bank[:, 1, 0:256], w0b[:, 512:768], add)
            ins.then_inc(rw["zb"], 1)
            for i in range(RT):
                link(ts_(kk[:, i, :], k_[:, i, :], V("a_kk_scale_2", i), None, mult))
            tt_(bon, kk, kk, mult).then_inc(rw["sq"], 1)
            sq3 = hid[:, 0:1536].rearrange("p (i n) -> p i n", n=NX)
            dve.wait_ge(rw["std"], 1)
            link(ts_(sq3, sq3, 1e-12, None, amax))
            link(nc.vector.reciprocal(sq3, sq3))
            link(tt_(kk, kk, sq3, mult))
            dve.wait_ge(rw["a_act"], RT)
            for i in range(RT):
                link(ts_(sq3[:, i, :], aa[:, i, :], 1.0, V("a_k_a_2", i), sub, mult))
                link(stt(k_[:, i, :], sq3[:, i, :], 1.0, k_[:, i, :], add, mult))
                ins = stt(bon[:, i, :], r_[:, i, :], V("a_r_k_2", i), k_[:, i, :], mult, mult)
                if i < RT - 1:
                    link(ins)
            ins.then_inc(rw["bsq"], 1)
            link(tt_(aa, aa, kk, mult))
            dve.wait_ge(rw["bsum"], 1)
            dve.wait_ge(rw["bsq"], 1)
            for b in range(3):
                link(tt_(bon[:, 2 * b:2 * b + 2, :], BANK[b].rearrange("p (i n) -> p i n", n=NX), v_[:, 2 * b:2 * b + 2, :], mult))
            nc.vector.memset(cols[:, 60:61], 0.0).then_inc(rw["bon"], 1)
            for i in range(RT):
                dve.wait_ge(rw["dec"], i + 1)
                stt(ar[:, :, 0, :], two(kk[:, i, :]), -1.0, two(dexc), mult, mult)
                tt_(ar[:, :, 1, :], two(r_[:, i, :]), two(dinc), mult)
                tt_(be, two(aa[:, i, :]), two(dinv), mult)
                tt_(ka, two(k_[:, i, :]), two(dinv), mult).then_inc(rw["feat"], 1)
                dve.wait_ge(rw["lp"], i + 1)
                m256 = C("lp_mask", 256).rearrange("p (e n) -> p e n", e=2)
                for m in range(4):
                    b = (m % 2) * 256
                    bk = slice(b, b + 256)
                    tt_(lp[:, m], (ps_u[:, m // 2, bk]).rearrange("p (e n) -> p e n", e=2), m256, mult)
                    tt_(mp[:, m], (ps_o[:, m // 2, bk]).rearrange("p (e n) -> p e n", e=2), m256, mult)
                for m in range(4):
                    link(tt_(ti[:, m, :], ps_o[:, 2 + m // 2, 128 * (m % 2):128 * (m % 2) + 128], C("m1"), mult))
                    link(tt_(ti[:, m, :], ti[:, m, :], ident, add))
                    link(tt_(tit[:, m, :], lp[:, m, 0, :], C("m1t"), mult))
                    ins = tt_(tit[:, m, :], tit[:, m, :], ident, add)
                    if m < 3:
                        link(ins)
                ins.then_inc(rw["lmask"], 1)
                for l, b in enumerate((2, 4, 8, 16, 32)):
                    e = 5 * i + l
                    dve.wait_ge(rw["p"], e + 1)
                    for m in range(4):
                        ins = tt_(pp[:, m, :], ps_o[:, 0, m * 128:(m + 1) * 128], C(f"m{b}"), mult)
                    ins.then_inc(rw["pm"], 1)
                    dve.wait_ge(rw["t"], e + 1)
                    if b < 32:
                        tt_(ti, ti, ps_o[:, 1, :].rearrange("p (m n) -> p m n", m=4), add)
                    tt_(tit, tit, ps_o[:, 2, :].rearrange("p (m n) -> p m n", m=4), add).then_inc(rw["tt"], 1)
                dve.wait_ge(rw["rp"], i + 1)
                tt_(rp, ar[:, :, 1, :], two(ps_o[:, 1, 0:256]), add).then_inc(rw["rps"], 1)
                dve.wait_ge(rw["gz"], i + 1)
                for c in (1, 2):
                    tt_(gi[:, c - 1, :], ps_g[:, c % 2, 64 * (c // 2):64 * (c // 2) + 64], C("ident64", 64), add)
                for c in range(3):
                    end = dinc[:, CH * (c + 1) - 1:CH * (c + 1)]
                    ins = ts_(zd[:, c, :], ps_g[:, c % 2, 128 + 64 * (c // 2):192 + 64 * (c // 2)], end, None, mult)
                ins.then_inc(rw["gzs"], 1)
                dve.wait_ge(rw["gzs"], i + 1)
                for c in range(2):
                    end = dinc[:, CH * (c + 2) - 1:CH * (c + 2)]
                    dve.wait_ge(rw["s"], 2 * i + c + 1)
                    stt(st2[:, c, :], ps_g[:, 1, 256 + 64 * c:320 + 64 * c], end, zd[:, c + 1, :], mult, add).then_inc(rw["ss2"], 1)
                dve.wait_ge(rw["y"], i + 1)
                for u in range(2):
                    ins = nc.vector.tensor_copy(y_all[:, i, u * 128:(u + 1) * 128], ps_u[:, u, 0:128])
                ins.then_inc(rw["yout"], 1)
            y6 = y_all[:, 0:6, :]
            dve.wait_ge(rw["mean"], 1)
            for b in range(3):
                link(stt(y6[:, 2 * b:2 * b + 2, :], BANK[b].rearrange("p (i n) -> p i n", n=NX), -1.0 / 64, y6[:, 2 * b:2 * b + 2, :], mult, add))
            tt_(sq3, y6, y6, mult).then_inc(rw["cen"], 1)
            dve.wait_ge(rw["vstd"], 1)
            link(nc.vector.reciprocal(sq3, sq3))
            link(tt_(y6, y6, sq3, mult))
            for i in range(RT):
                link(ts_(y6[:, i, :], y6[:, i, :], V("a_lnx_g_2", i), V("a_lnx_b_2", i), mult, add))
            link(tt_(y6, y6, bon, add))
            dve.wait_ge(rw["g_act"], RT)
            tt_(y6, y6, gg, mult).then_inc(rw["fin"], 1)
            attend(1)
            rest_y(y_all, KT)
            chunks_out("a_out", 0, add_to_x(NX, one, 2))
            norm(xs_, NX, gain("ffn_post_norm_2", 0), None, "split")
            ffn(5, NX, half)
            dve.wait_ge(bi_row, 1)
            for g in range(3):
                tt_(rowb[:, 512 * g:512 * (g + 1)], BANK[1 + g][0:4, :], bt[0:4, 1536 + 512 * g:2048 + 512 * g], add).then_inc(bi_sb, 1)
            norm(xs_, NX, gain("kv_norm_2"), None, "split")

            def take_kv(c, q, tile):
                if c < 3:
                    nc.vector.tensor_copy(k_g[:, 2 * c + q, :], tile[:, 0:NX]).then_inc(o_free, 1)
                else:
                    nc.vector.tensor_copy(v_g[:, q, 256 * (c - 3):256 * (c - 2)], tile[:, 0:256]).then_inc(o_free, 1)

            dve.wait_ge(bi_dram, 16)
            chunks_out("kv", 0, take_kv)
            st["tiles"] = TILE0[FIRST["ffn", 6]]
            head_norm(k_g, 6, V("kv_k_norm_2"))
            norm(xs_, NX, gain("ffn_pre_norm_2", 1), None, "split")
            ffn(6, NX, half)
            norm(lambda d: mem_x[:, d, :], NX, gain("mem_norm_2", 1), None, "split")
            chunks_out("memkv", 1, take_memkv)
            st["tiles"] = TILE0[FIRST["b_q", 0]]
            head_norm(mem_k, 2, V("mem_k_norm_2", 1))
            norm(xs_, NX, gain("mix_norm_2", 1), None, "split")

            def take_q(c, q, tile):
                i = 2 * c + q
                nc.vector.tensor_copy(q_g[:, i, :] if i < 6 else mem_q[1][:, i - 6, :], tile[:, 0:NX]).then_inc(o_free, 1)

            chunks_out("b_q", 0, take_q)
            st["tiles"] = TILE0[FIRST["b_out", 0]]
            head_norm(q_g, 6, qgain[:, 2:3])
            head_norm(mem_q[1], 2, qgain[:, 1:2])
            attend(2)
            attend(3)
            rest_y(y_all[:, 0:4, :], 4)
            chunks_out("b_out", 0, add_to_x(NX, one, 4))
            norm(xs_, NX, gain("ffn_post_norm_2", 1), None, "split")
            ffn(7, NX, half)

        @block.tensor
        def _(pe):
            st = {"k": 0, "h": 0, "hn": 0, "y": 0}
            mm = nc.tensor.matmul

            def chunk(n, i=None, per=SLOTS):
                pe.wait_ge(w_lo, n + 1 if i is None else i * per + (n + 1))
                return n % SLOTS

            def weights(s, cols_):
                return (whi[:, s, :].rearrange("p (k n) -> p k n", n=cols_), wlo[:, s, :].rearrange("p (k n) -> p k n", n=cols_))

            def mm3(out, a, b, first, last):
                mm(out, a[1], b[0], start=first, stop=False)
                mm(out, a[0], b[1], start=False, stop=False)
                return mm(out, a[0], b[0], start=False, stop=last)

            def norm(N, split=True):
                st["k"] += 1
                for d in range(KT):
                    pe.wait_ge(nm_sq, (st["k"] - 1) * KT + d + 1)
                    ins = mm(ps_g[:, 0, 0:N], ones, tsq[:, d * NTOK:d * NTOK + N], start=d == 0, stop=d == KT - 1)
                ins.then_inc(nm_sum, 1)
                if split:
                    st["h"] += KT * (N // NX)

            def tile(n, q):
                T = TILE0[n] + q
                pe.wait_ge(o_free, T + 1)
                return ps_o[:, T % 4, :]

            def split_input(N):
                h0, per = st["h"] - KT * (N // NX), N // NX
                return lambda k: pe.wait_ge(h_ready, h0 + (k + 1) * per)

            def project(n, N, rows=KT, width=256, k0=0, w0=0, ready=lambda k: None, q0=0):
                w = weights(chunk(n), width)
                for j in range(width // 128):
                    out = tile(n, q0 + j)
                    for k in range(rows):
                        ready(k)
                        c = slice(j * 128, (j + 1) * 128)
                        ins = mm3(out[:, 0:N], (w[0][:, w0 + k, c], w[1][:, w0 + k, c]), (hh[:, k0 + k, 0:N], hl[:, k0 + k, 0:N]), k == 0, k == rows - 1)
                    ins.then_inc(mm_done, 1)

            def project_first(n, N, of=None):
                ready = split_input(of or N)
                w = [weights(chunk(n + b), 256) for b in range(2)]
                out = [tile(n + b, j)[:, 0:N] for b in range(2) for j in range(2)]
                for k in range(KT):
                    ready(k)
                    for b in range(2):
                        for j in range(2):
                            c = slice(j * 128, (j + 1) * 128)
                            ins = mm3(out[2 * b + j], (w[b][0][:, k, c], w[b][1][:, k, c]), (hh[:, k, 0:N], hl[:, k, 0:N]), k == 0, k == KT - 1)
                            if k == KT - 1:
                                ins.then_inc(mm_done, 1)

            def project_tokens(n, ntok):
                w = weights(chunk(n), 256)
                for q in range(ntok // 128):
                    out, c = tile(n, q), slice(q * 128, (q + 1) * 128)
                    for k in range(KT):
                        ins = mm3(out[:, 0:256], (hh[:, k, c], hl[:, k, c]), (w[0][:, k, :], w[1][:, k, :]), k == 0, k == KT - 1)
                    ins.then_inc(mm_done, 1)

            def ffn(f, N):
                n0, g0 = FIRST["ffn", f], f * GROUPS
                per, _, tiles, n_up, n_down, n_ada, n_last = ffn_pass(f)
                ready = split_input(N)

                def first_halves():
                    w = [weights(chunk(n), 256) for n in (n0, n0 + 1)]
                    for k in range(KT):
                        ready(k)
                        for b, bank in enumerate((ps_g, ps_u)):
                            for j in range(2):
                                c = slice(j * 128, (j + 1) * 128)
                                ins = mm3(bank[:, j, 0:N], (w[b][0][:, k, c], w[b][1][:, k, c]), (hh[:, k, 0:N], hl[:, k, 0:N]), k == 0, k == KT - 1)
                            if k == KT - 1:
                                ins.then_inc(mm_done, 1)

                def half(bank, n, i=None):
                    w = weights(chunk(n, i, per), 256)
                    for j in range(2):
                        for k in range(KT):
                            c = slice(j * 128, (j + 1) * 128)
                            ins = mm3(bank[:, j, 0:N], (w[0][:, k, c], w[1][:, k, c]), (hh[:, k, 0:N], hl[:, k, 0:N]), k == 0, k == KT - 1)
                    ins.then_inc(mm_done, 1)

                def down(n, T, group, i=None):
                    w = weights(chunk(n, i, per), D)
                    pe.wait_ge(a_ready, group + 1)
                    for d in range(KT):
                        pe.wait_ge(o_free, T + (d + 1))
                        for k in range(2):
                            c = slice(d * 128, (d + 1) * 128)
                            ins = mm3(ps_o[:, (TILE0[n] + d) % BANKS, 0:N], (w[0][:, k, c], w[1][:, k, c]), (ah[:, k, 0:N], al[:, k, 0:N]), k == 0, k == 1)
                        ins.then_inc(mm_done, 1)

                first_halves()
                with pe.Fori(0, GROUPS - 1) as i:
                    pe.wait_ge(g_act, i + (g0 + 1))
                    half(ps_g, n0 + 2, i)
                    for n in range(n0 + 3, n0 + 2 + per):
                        if n == n_up:
                            pe.wait_ge(u_mul, i + (g0 + 1))
                            half(ps_u, n, i)
                        elif n == n_down:
                            down(n, i * tiles + TILE0[n], i + g0, i)
                        else:
                            ada(n, i)
                down(n_last, TILE0[n_last], g0 + GROUPS - 1)
                if f < 2:
                    ada_turn(f + 1)

            def ada(n, i=None):
                w = weights(chunk(n, i, len(FFN_ADA_PASS)), 256)
                parts = DONE[n] - (DONE[n - 1] if n else 0)
                for q in range(parts):
                    T = TILE0[n] + q
                    pe.wait_ge(o_free, T + 1 if i is None else i * sum(FFN_ADA_PASS) + (T + 1))
                    rows = range(q * KT // parts, (q + 1) * KT // parts)
                    for k in rows:
                        out = ps_o[0:4, T % BANKS, 0:256]
                        mm(out, cs[:, k, :], w[1][:, k, :], start=k == rows[0], stop=False)
                        ins = mm(out, cs[:, k, :], w[0][:, k, :], start=False, stop=k == rows[-1])
                    ins.then_inc(mm_done, 1)

            def ada_turn(e):
                c0, c1 = ADA_PARTS[e]
                n_last = [FIRST["ada", 0] + ADA_FIRST, FIRST["ffn", 0] + 2 + 6 * (GROUPS - 1), FIRST["ffn", 1] + 2 + 6 * (GROUPS - 1)][e]
                pe.wait_ge(o_free, freed(TILE0[n_last]))
                for t in range(2 * (c1 - c0)):
                    ins = mm(ps_u[:, 0, 2 * t:2 * t + 2], ada_rows[:, 128 * t:128 * (t + 1)], C("pick", 2)[0:4], start=True, stop=True)
                ins.then_inc(ad_turn, 1)

            def head_norm(nt):
                st["hn"] += 1
                pe.wait_ge(hn_sq, st["hn"])
                for b in range((nt + 1) // 2):
                    ins = mm(BANK[b], blk, hid[:, 512 * b:512 * (b + 1)], start=True, stop=True)
                ins.then_inc(hn_sum, 1)

            def attend(a):
                U = ATT[a]

                def scores(u):
                    g, unit = AT0[a] + u, U[u]
                    if g >= 2:
                        pe.wait_ge(at_e, g - 1)
                    bank = ps_g if g % 2 == 0 else ps_u
                    for (rows, b, c), q, k in unit["scores"]:
                        ins = mm(bank[rows, b, c], q, k, start=True, stop=True)
                    ins.then_inc(at_s, 1)

                def flip(u):
                    g, unit = AT0[a] + u, U[u]
                    pe.wait_ge(at_p, g + 1)
                    if g:
                        pe.wait_ge(at_c, g)
                    for b in range(unit["nb"]):
                        ins = nc.tensor.transpose(ps_o[:, b // 4, (b % 4) * 128:(b % 4 + 1) * 128], probs[g % 2][:, b * 128:(b + 1) * 128], ident)
                    ins.then_inc(at_t, 1)

                def values(u):
                    g, unit = AT0[a] + u, U[u]
                    pe.wait_ge(at_c, g + 1)
                    if g >= 2:
                        pe.wait_ge(at_y, g - 1)
                    nb = unit["nb"]
                    for b in range(nb):
                        ins = mm(ps_o[unit["rows"], 2 + g % 2, 0:128], unit["v"][b], probs_t[g % 2][:, b, :], start=b == 0, stop=b == nb - 1)
                    ins.then_inc(at_o, 1)

                scores(0)
                for u in range(len(U)):
                    if u + 1 < len(U):
                        scores(u + 1)
                    if u:
                        values(u - 1)
                    flip(u)
                values(len(U) - 1)

            def y_split():
                st["y"] += 1
                pe.wait_ge(y_ready, st["y"])

            pe.wait_ge(ad_lo, 1)
            for n in range(ADA_FIRST):
                ada(n)
            ada_turn(0)
            norm(NTOK)
            ffn(0, NTOK)
            norm(NTOK, False)
            n = FIRST["pool", 0]
            w = weights(chunk(n), 256)
            for g in range(4):
                y_split()
                for j in range(2):
                    out, c = tile(n, 2 * g + j), slice(j * 128, (j + 1) * 128)
                    for k in range(2):
                        ins = mm3(out, (w[0][:, 2 * g + k, c], w[1][:, 2 * g + k, c]), (hh[:, 2 * g + k, :], hl[:, 2 * g + k, :]), k == 0, k == 1)
                    ins.then_inc(mm_done, 1)
            norm(NTOK)
            ffn(1, NTOK)
            norm(NTOK)
            ffn(2, NTOK)
            norm(NTOK)
            n = FIRST["qkv", 0]
            project_first(n, NX, of=NTOK)
            for c in range(2, 12):
                if c < 8:
                    project(n + c, NX if c < 4 else NTOK)
                else:
                    project_tokens(n + c, NTOK)
            pe.wait_ge(o_free, freed(TILE0[n + 8]))
            for r in range(8):
                z = q_d[:, 2 * r:2 * r + 2, :] if r < 4 else k_d[:, 2 * (r - 4):2 * (r - 4) + 2, 0:NX]
                if r >= 4:
                    pe.wait_ge(ro_sin, r - 3)
                mm(BANK[r % 4].rearrange("p (a n) -> p a n", a=2), C("perm"), z, start=True, stop=True).then_inc(ro_mm, 1)
            pe.wait_ge(ro_done, 8)
            pe.wait_ge(o_free, freed(TILE0[n + 12]))
            attend(0)
            pe.wait_ge(sl_sq, 1)
            for b in range(4):
                ins = mm(BANK[b], ones, big[:, 2048 + 512 * b:2560 + 512 * b], start=True, stop=True)
            ins.then_inc(sl_sum, 1)
            y_split()
            for c in range(4):
                project(FIRST["wo", 0] + c, NX)
            norm(NX)
            ffn(3, NX)
            norm(NX, False)
            norm(NX)
            ffn(4, NX)

            def mem_kv(l):
                norm(NX)
                project(FIRST["memkv", l], NX, ready=split_input(NX))
                project_tokens(FIRST["memkv", l] + 1, NX)
                head_norm(2)

            mem_kv(0)
            norm(NX)
            project_first(FIRST["a_in", 0], NX)
            for c in range(2, 11):
                project(FIRST["a_in", 0] + c, NX)
            head_norm(2)
            pe.wait_ge(hn_done, st["hn"])
            pe.wait_ge(lora_in, 48)
            pe.wait_ge(rw["lora"], 1)
            for u in range(2):
                bank = ps_g if u == 0 else ps_u
                lhs = proj[0:64, 18, 1 + 128 * u:129 + 128 * u]
                mm(bank[:, 0, :], lhs, lora[0:64, 0:512], start=True, stop=True)
                ins = mm(bank[:, 1, 0:256], lhs, lora[0:64, 512:768], start=True, stop=True)
            ins.then_inc(rw["z"], 1)
            for i in range(RT):
                if i >= 2:
                    pe.wait_ge(rw["a_act"], i - 1)
                mm(ps_o[:, i % 2, 0:NX], lora[64:128, 128 * i:128 * (i + 1)], proj[64:128, 18, 1:257], start=True, stop=True).then_inc(rw["a_mm"], 1)
            for i in range(RT):
                if i >= 2:
                    pe.wait_ge(rw["g_act"], i - 1)
                mm(ps_o[:, 2 + i % 2, 0:NX], gup[:, 128 * i:128 * (i + 1)], proj[:, 19, 1:257], start=True, stop=True).then_inc(rw["g_mm"], 1)
            pe.wait_ge(rw["sq"], 1)
            for b in range(3):
                ins = mm(BANK[b], blk, bon[:, 2 * b:2 * b + 2, :], start=True, stop=True)
            ins.then_inc(rw["ss"], 1)
            pe.wait_ge(rw["std"], 1)
            pe.wait_ge(rw["bsq"], 1)
            for b in range(3):
                ins = mm(BANK[b], blk, bon[:, 2 * b:2 * b + 2, :], start=True, stop=True)
            ins.then_inc(rw["bsum"], 1)
            pe.wait_ge(rw["zs"], 1)
            pe.wait_ge(rw["bon"], 1)
            pe.wait_ge(rw["a_act"], RT)
            pe.wait_ge(rw["g_act"], RT)
            R = [slice(0, 64), slice(64, 128)]
            for i in range(RT):
                if i:
                    pe.wait_ge(rw["yout"], i)
                for u in range(2):
                    ins = mm(ps_g[:, u, 0:256], zs[:, u, 128 * i:128 * (i + 1)], C("cum", 256), start=True, stop=True)
                ins.then_inc(rw["cum"], 1)
                pe.wait_ge(rw["feat"], i + 1)
                for e, src in enumerate((two(v_[:, i, :]), be, ka, ar[:, :, 0, :])):
                    for u in range(2):
                        at = (e % 2) * 256 + u * 128
                        ins = nc.tensor.transpose(ps_g[:, e // 2, at:at + 128], src[:, u, :], ident)
                ins.then_inc(rw["tp"], 1)
                for m in range(4):
                    q, u = m // 2, m % 2
                    rhs = ar[R[q], u, :, :]
                    b = (m % 2) * 256
                    mm(ps_u[:, m // 2, b:b + 256].rearrange("p (e n) -> p e n", e=2), be[R[q], u, :], rhs, start=True, stop=True)
                    mm(ps_o[:, m // 2, b:b + 256].rearrange("p (e n) -> p e n", e=2), ka[R[q], u, :], rhs, start=True, stop=True)
                    ins = mm(ps_o[:, 2 + q, 128 * u:128 * (u + 1)], ar[R[q], u, 0, :], be[R[q], u, :], start=True, stop=True)
                ins.then_inc(rw["lp"], 1)
                pe.wait_ge(rw["lmask"], i + 1)
                for l in range(5):
                    e = 5 * i + l
                    if l:
                        pe.wait_ge(rw["tt"], e)
                    for m in range(4):
                        ins = mm(ps_o[:, 0, 128 * m:128 * (m + 1)], lp[:, m, 0, :], ti[:, m, :], start=True, stop=True)
                    ins.then_inc(rw["p"], 1)
                    pe.wait_ge(rw["pm"], e + 1)
                    for m in range(4):
                        c = slice(128 * m, 128 * (m + 1))
                        if l < 4:
                            mm(ps_o[:, 1, c], tit[:, m, :], pp[:, m, :], start=True, stop=True)
                        ins = mm(ps_o[:, 2, c], pp[:, m, :], tit[:, m, :], start=True, stop=True)
                    ins.then_inc(rw["t"], 1)
                pe.wait_ge(rw["tm"], i + 1)

                def tok(e, m):
                    return tmaj[:, e, m % 2, 64 * (m // 2):64 * (m // 2) + 64]

                for m in range(4):
                    ins = mm(ps_o[:, 3, 64 * m:64 * (m + 1)], mp[:, m, 0, :], tok(0, m), start=True, stop=True)
                ins.then_inc(rw["mv"], 1)
                pe.wait_ge(rw["mvx"], i + 1)
                pe.wait_ge(rw["tt"], 5 * (i + 1))
                for m in range(4):
                    ins = mm(ps_o[:, 0, 128 * m:128 * (m + 1)], tit[:, m, :], xs[:, m, :], start=True, stop=True)
                ins.then_inc(rw["tx"], 1)
                pe.wait_ge(rw["txs"], i + 1)
                for m in range(4):
                    q, u = m // 2, m % 2
                    ins = mm(ps_o[R[q], 1, 128 * u:128 * (u + 1)], tx[:, m, 0:64], lp[:, m, 1, :], start=True, stop=True)
                ins.then_inc(rw["rp"], 1)
                for m in range(4):
                    q, u = m // 2, m % 2
                    for e in range(2):
                        c = 2 * u + e
                        if c in (1, 2):
                            mm(ps_g[R[q], e, 64 * u:64 * (u + 1)], tx[R[e], m, 0:64], tok(1, m)[R[e]], start=True, stop=True)
                        if c < 3:
                            o = ps_g[R[q], e, 128 + 64 * u:192 + 64 * u]
                            mm(o, tok(1, m)[R[e]], tx[R[e], m, 64:128], start=True, stop=False)
                            ins = mm(o, tok(2, m)[R[e]], tok(0, m)[R[e]], start=False, stop=True)
                ins.then_inc(rw["gz"], 1)
                state = [None, zd[:, 0, :], st2[:, 0, :], st2[:, 1, :]]
                for c in range(2):
                    if c == 0:
                        pe.wait_ge(rw["gzs"], i + 1)
                    else:
                        pe.wait_ge(rw["ss2"], 2 * i + 1)
                    for q in range(2):
                        ins = mm(ps_g[R[q], 1, 256 + 64 * c:320 + 64 * c], gi[R[q], c, :], state[c + 1][R[q]], start=True, stop=True)
                    ins.then_inc(rw["s"], 1)
                pe.wait_ge(rw["rps"], i + 1)
                pe.wait_ge(rw["ss2"], 2 * i + 2)
                for u in range(2):
                    for q in range(2):
                        m = 2 * q + u
                        o = ps_u[R[q], u, 0:128]
                        mm(o, tx[:, m, 64:128], lp[:, m, 1, :], start=True, stop=False)
                        mm(o, tok(0, m), mp[:, m, 1, :], start=False, stop=True)
                        for e in range(2):
                            c = 2 * u + e
                            if c:
                                ins = mm(ps_u[R[q], u, 64 * e:64 * e + 64], state[c][R[q]], rp[R[q], u, 64 * e:64 * e + 64], start=False, stop=True,
                                         skip_group_check=True)
                ins.then_inc(rw["y"], 1)
            pe.wait_ge(rw["yout"], RT)
            for b in range(3):
                ins = mm(BANK[b], blk, y_all[:, 2 * b:2 * b + 2, :], start=True, stop=True)
            ins.then_inc(rw["mean"], 1)
            pe.wait_ge(rw["cen"], 1)
            for b in range(3):
                ins = mm(BANK[b], blk, hid[:, 512 * b:512 * (b + 1)], start=True, stop=True)
            ins.then_inc(rw["var"], 1)
            pe.wait_ge(rw["fin"], 1)
            attend(1)
            y_split()
            for c in range(4):
                project(FIRST["a_out", 0] + c, NX)
            norm(NX)
            ffn(5, NX)
            pe.wait_ge(bt_in, 16)
            pe.wait_ge(rel_in, 16)
            for g in range(3):
                ins = mm(BANK[1 + g][0:4, :], rel[:, 4 * g:4 * g + 4], bt[:, 512 * g:512 * (g + 1)], start=True, stop=True)
            ins.then_inc(bi_row, 1)
            norm(NX)
            pe.wait_ge(bi_sb, 3)
            project_first(FIRST["kv", 0], NX)
            for c in range(2, 6):
                if c < 3:
                    project(FIRST["kv", 0] + c, NX)
                else:
                    project_tokens(FIRST["kv", 0] + c, NX)
            head_norm(6)
            norm(NX)
            ffn(6, NX)
            mem_kv(1)
            norm(NX)
            project_first(FIRST["b_q", 0], NX)
            for c in range(2, 4):
                project(FIRST["b_q", 0] + c, NX)
            head_norm(6)
            head_norm(2)
            pe.wait_ge(hn_done, st["hn"])
            attend(2)
            attend(3)
            y_split()
            for c in range(2):
                project(FIRST["b_out", 0] + c, NX, rows=4, width=512)
            norm(NX)
            ffn(7, NX)


def kernel(**inputs):
    import concourse.bacc as _bacc
    from concourse.bass_utils import run_bass_kernel_spmd as _run

    a = {k: np.asarray(v) for k, v in inputs.items()}
    arrays = pack(a)
    nc = _bacc.Bacc("TRN2", target_bir_lowering=False, num_devices=1)
    args = [nc.dram_tensor("in_" + k, v.shape, mybir.dt.from_np(v.dtype), kind="ExternalInput").ap() for k, v in arrays.items()]
    out = nc.dram_tensor("out", (128, KT, NX), mybir.dt.float32, kind="ExternalOutput").ap()
    build(nc, *args, out)
    r = _run(nc, [{"in_" + k: v for k, v in arrays.items()}], core_ids=[0])
    return np.ascontiguousarray(np.asarray(r.results[0]["out"]).transpose(2, 1, 0)).reshape(1, NX, D)
```

```python
import math
from contextlib import ExitStack

import numpy as np

import concourse.bass as bass
from concourse import mybir

D = 1024
KT = D // 128
NX = 256
NTOK = 512
DFF = 2816
GROUPS = DFF // 256
CHUNK = 2048
SLOTS = 3
NMOD = 9
POOL_WINDOWS = (2, 4, 8, 16)
DIFF_HEADS = 8
RW = 768
RT = RW // 128
CH = 64
DIL = ((128, 1), (512, 4), (2048, 16))
NUM_BUCKETS, MAX_DISTANCE = 32, 2048
LAM_INIT = 0.8 - 0.6 * math.exp(-0.3)
NEG = -1e30


def vector_columns():
    sizes = [("ada_b", 144), ("norm_g", 48), ("pool_scale", 8), ("final_g", 8), ("ffn_pre_norm_2", 16),
             ("mix_norm_2", 16), ("ffn_post_norm_2", 16), ("mem_norm_2", 16), ("a_shift_mu_2", 20),
             ("a_w0_2", 6), ("a_a0_2", 6), ("a_kk_scale_2", 6), ("a_k_a_2", 6), ("a_r_k_2", 6),
             ("a_lnx_g_2", 6), ("a_lnx_b_2", 6), ("kv_norm_2", 8), ("c", 8), ("c_ctx", 8),
             ("diff_subln_g", 1), ("mem_q_norm_2", 2), ("b_q_norm_2", 1), ("mem_k_norm_2", 2),
             ("kv_k_norm_2", 1)]
    at, col = {}, 0
    for name, n in sizes:
        at[name] = col
        col += n
    return at, col


TWICE = ("mem_q_norm_2", "mem_k_norm_2", "b_q_norm_2", "kv_k_norm_2")


def constants():
    p = np.arange(128)
    half = p // 64
    same = half[:, None] == half[None, :]
    parts = {}
    parts["ident"] = np.eye(128)
    parts["ones"] = np.ones((128, 128))
    parts["blk"] = same.astype(float)
    perm = np.zeros((128, 128))
    for f in range(128):
        perm[f ^ 16, f] = 1.0
    parts["perm"] = perm
    t = np.arange(NX)
    inv = 10000.0 ** (-np.arange(0, 32, 2, dtype=np.float32) / np.float32(32))
    f32_ = np.float32
    ang = np.zeros((128, NX), f32_)
    for f in range(128):
        pos = (t // 64) if (f % 64) < 32 else (t % 64)
        ang[f] = pos.astype(f32_) * inv[f % 16].astype(f32_)
    sign = np.where((p % 32) < 16, -1.0, 1.0)[:, None]
    parts["cos"] = np.tile(np.cos(ang), 2)
    parts["sin"] = np.tile(np.sin(ang) * sign, 2)
    s_, t_ = p[:, None], p[None, :]
    parts["cum"] = np.concatenate([same & (s_ <= t_), same & (s_ < t_)], 1).astype(float)
    parts["lp_mask"] = np.concatenate([same & (s_ < t_), same & (s_ <= t_)], 1).astype(float)
    def level(b):
        return ((s_ // (2 * b) == t_ // (2 * b)) & (s_ // b % 2 == 1) & (t_ // b % 2 == 0)).astype(float)
    parts["m1"], parts["m1t"] = level(1), level(1).T
    for b in (2, 4, 8, 16, 32):
        parts[f"m{b}"] = level(b)
    parts["pick"] = np.eye(128)[:, 0:2] + np.eye(128, k=-2)[:, 0:2]
    parts["ident64"] = np.concatenate([np.eye(64), np.eye(64)], 0)
    parts["eps"] = np.full((128, 1), 1e-6)
    parts["lnx_eps"] = np.full((128, 1), 64e-5)
    at, col, cols = {}, 0, []
    for name, a in parts.items():
        at[name] = col
        col += a.shape[1]
        cols.append(np.asarray(a, f32_))
    return at, np.ascontiguousarray(np.concatenate(cols, 1))


def pool_counts():
    t = np.arange(NX)
    rows = [1.0 / (np.clip(t - w // 2 + w - 1, 0, NX - 1) - np.clip(t - w // 2, 0, NX - 1) + 1) for w in POOL_WINDOWS]
    return np.ascontiguousarray(np.broadcast_to(np.concatenate([np.tile(r, 4) for r in rows]).astype(np.float32), (128, 16 * NX)))


def bias_tables():
    u = np.arange(512)
    dist = u - 255
    exact = NUM_BUCKETS // 2
    large = exact + (np.log(np.maximum(dist, 1).astype(np.float32) / exact) / math.log(MAX_DISTANCE / exact)
                     * (NUM_BUCKETS - exact)).astype(np.int32)
    bucket = np.where(dist < exact, dist, np.minimum(large, NUM_BUCKETS - 1))
    hot = np.zeros((32, 3, 512), np.float32)
    add = np.zeros((32, 3, 512), np.float32)
    for g, (window, dil) in enumerate(DIL):
        ok = (dist >= 0) & (dist % dil == 0) & (dist <= window)
        for k in range(512):
            if ok[k]:
                hot[bucket[k], g, k] = 1.0
        add[:, g] = np.where(ok, 0.0, NEG)
    return np.ascontiguousarray(np.concatenate([hot.reshape(32, -1), add.reshape(32, -1)], 1))


FFN_PASS = [0, 0, KT]
FFN_ADA_PASS = [0, 1, 0, 1, KT, 2]
FFN_TILES = [0, 0] + FFN_PASS * (GROUPS - 1) + [KT]
FFN_ADA_TILES = [0, 0] + FFN_ADA_PASS * (GROUPS - 1) + [KT]
ADA_FIRST = 12
ADA_FFN = 3 * (GROUPS - 1)
ADA_PARTS = [(0, ADA_FIRST), (ADA_FIRST, ADA_FIRST + ADA_FFN), (ADA_FIRST + ADA_FFN, ADA_FIRST + 2 * ADA_FFN)]
assert ADA_PARTS[-1][1] == 2 * NMOD * D // 256
STREAM = [("ada", 0, [1] * ADA_FIRST), ("ffn", 0, FFN_ADA_TILES), ("pool", 0, [8]), ("ffn", 1, FFN_ADA_TILES),
          ("ffn", 2, FFN_TILES), ("qkv", 0, [2] * 8 + [4] * 4), ("wo", 0, [2] * 4),
          ("ffn", 3, FFN_TILES), ("ffn", 4, FFN_TILES), ("memkv", 0, [2] * 2), ("a_in", 0, [2] * 11),
          ("a_out", 0, [2] * 4), ("ffn", 5, FFN_TILES), ("kv", 0, [2] * 6), ("ffn", 6, FFN_TILES),
          ("memkv", 1, [2] * 2), ("b_q", 0, [2] * 4), ("b_out", 0, [4] * 2), ("ffn", 7, FFN_TILES)]
FIRST = {}
TILE0 = []
DONE = []
for _kind, _i, _tiles in STREAM:
    FIRST[_kind, _i] = len(DONE)
    for _t in _tiles:
        TILE0.append(TILE0[-1] + _last if TILE0 else 0)
        DONE.append((DONE[-1] if DONE else 0) + max(_t, 1))
        _last = _t
FIRST_AFTER = {key: FIRST[key] + len(t) for key, t in (((k, i), t) for k, i, t in STREAM)}
TOTAL = len(DONE)
PADDED = TOTAL + SLOTS
assert PADDED % SLOTS == 0
BANKS = 4


def freed(tiles):
    return BANKS + tiles


def pack(a):
    def cols(w, width=256):
        return [w[:, c:c + width].reshape(-1, 128, width).transpose(1, 0, 2) for c in range(0, w.shape[1], width)]

    def ffn(w_in, w_out):
        gate, up = cols(w_in[:, :DFF]), cols(w_in[:, DFF:])
        down = [w_out[r:r + 256].reshape(2, 128, D).transpose(1, 0, 2) for r in range(0, DFF, 256)]
        return gate, up, down

    def ffn_order(gate, up, down, ada):
        order = [gate[0], up[0]]
        for i in range(1, GROUPS):
            these = [gate[i], up[i], down[i - 1]]
            for j, c in enumerate(these):
                order += [c] + ([ada[3 * (i - 1) + j]] if ada else [])
        return order + [down[-1]]

    chunks = []
    ada = cols(a["ada_w"][0]) + cols(a["ada_w"][1])
    f1 = [ffn(a["ffn_w_in"][l, s], a["ffn_w_out"][l, s]) for l in range(2) for s in range(2)]
    f2 = [ffn(a[f"ffn_{s}_w_in_2"][l], a[f"ffn_{s}_w_out_2"][l]) for l in range(2) for s in ("pre", "post")]
    for kind, i, _ in STREAM:
        if kind == "ada":
            chunks += ada[:ADA_FIRST]
        elif kind == "ffn":
            chunks += ffn_order(*(f1 + f2)[i], ada[slice(*ADA_PARTS[i + 1])] if i < 2 else None)
        elif kind == "pool":
            chunks.append(a["pool_w"][0].reshape(4, 2, 128, 256).transpose(2, 0, 1, 3))
        elif kind == "memkv":
            chunks += cols(a["mem_w_kv_2"][i])
        elif kind == "b_out":
            chunks += cols(a["b_w_out_2"][0], 512)
        else:
            name = {"qkv": "diff_w_qkv", "wo": "diff_w_o", "a_in": "a_w_in_2", "a_out": "a_w_out_2", "b_q": "b_w_q_2"}.get(kind)
            chunks += cols(a[name][0] if name else a["kv_w_2"])
    w = np.zeros((PADDED, 128, CHUNK), np.float32)
    for n, c in enumerate(chunks):
        w[n] = c.reshape(128, CHUNK)
    at, n = vector_columns()
    vec = np.zeros((128, n), np.float32)
    for name, col in at.items():
        v = a[name].reshape(-1, 64) if name in TWICE else a[name].reshape(-1, 128)
        if name in TWICE:
            v = np.concatenate([v, v], 1)
        vec[:, col:col + len(v)] = v.T

    def fm(v):
        return v.T.reshape(KT, 128, -1).transpose(1, 0, 2)

    arrays = dict(
        W=w.reshape(PADDED * 128, CHUNK),
        XT=np.concatenate([fm(a["x"][0]), fm(a["ctx"][0])], 2), MEMT=fm(a["mem_2"][0]),
        VEC=vec, CST=constants()[1], ICNT=pool_counts(), BT=bias_tables(), REL=a["rel_bias_2"],
        LAM=np.broadcast_to(a["diff_lam"][0].reshape(1, 256), (128, 256)),
        W0B=np.broadcast_to(a["a_w0_2"][0].reshape(1, RW), (128, RW)),
        LORA=np.concatenate([a["a_w_up_2"][0], a["a_a_up_2"][0]], 0), GUP=a["a_g_up_2"][0])
    return {k: np.ascontiguousarray(v) for k, v in arrays.items()}




def build(nc, W, XT, MEMT, VEC, CST, ICNT, BT, REL, LAM, W0B, LORA, GUP, OUT, stop=None):
    f32, f32r = mybir.dt.float32, mybir.dt.float32r
    ACT, ALU, AX = mybir.ActivationFunctionType, mybir.AluOpType, mybir.AxisListType
    add, sub, mult, amax = ALU.add, ALU.subtract, ALU.mult, ALU.max
    vat, nvec = vector_columns()
    cat, _ = constants()
    ncst = CST.shape[1]
    ds = bass.ds
    def ffn_pass(f):
        tiles = FFN_ADA_PASS if f < 2 else FFN_PASS
        n0 = FIRST["ffn", f]
        n = len(tiles)
        gap = n // 3
        ada = [n0 + 2 + gap * j + 1 for j in range(3)] if f < 2 else []
        return n, sum(max(t, 1) for t in tiles), sum(tiles), n0 + 2 + gap, n0 + 2 + 2 * gap, ada, n0 + 2 + n * (GROUPS - 1)


    with ExitStack() as ctx:
        def sb(name, shape, dt=f32):
            return ctx.enter_context(nc.sbuf_tensor(name, shape, dt))

        def sem(name):
            return ctx.enter_context(nc.semaphore(name))

        wraw = sb("wraw", [128, SLOTS, CHUNK])
        whi = sb("whi", [128, SLOTS, CHUNK], f32r)
        wlo = sb("wlo", [128, SLOTS, CHUNK], f32r)
        x = sb("x", [128, KT, NTOK])
        tsq = sb("tsq", [128, KT * NTOK])
        vec = sb("vec", [128, nvec])
        cst = sb("cst", [128, ncst])
        mods = sb("mods", [128, 2, 72, 2])
        sc = sb("sc", [128, 2 * KT])
        cs = sb("cs", [128, KT, 4], f32r)
        acol = sb("acol", [128, 2, 3, KT, 2])
        gcol = sb("gcol", [128, 2, 3, KT, 2])
        rstd = sb("rstd", [128, NTOK])
        lamb = sb("lamb", [128, 256])
        cols = sb("cols", [128, 64])
        with nc.sbuf_tensor("hh", [128, KT, NTOK], f32r) as hh, nc.sbuf_tensor("hl", [128, KT, NTOK], f32r) as hl:
            pass
        big = sb("big", [128, 2 * KT * NTOK])
        with nc.sbuf_tensor("ah", [128, 2, NTOK], f32r) as ah, nc.sbuf_tensor("al", [128, 2, NTOK], f32r) as al:
            pass
        hid = sb("hid", [128, 4 * NTOK])
        scr = sb("scr", [128, 10240])
        ps_g = ctx.enter_context(nc.psum_tensor("ps_g", [128, 2, 512], f32))
        ps_u = ctx.enter_context(nc.psum_tensor("ps_u", [128, 2, 512], f32))
        ps_o = ctx.enter_context(nc.psum_tensor("ps_o", [128, 4, 512], f32))
        bias_rows = nc.dram_tensor("bias_rows", [3 * 4 * 512], f32, kind="Internal")

        def V(name, i=0, n=1):
            return vec[:, vat[name] + i:vat[name] + i + n]

        def C(name, n=128):
            return cst[:, cat[name]:cat[name] + n]

        ident, ones, blk = C("ident"), C("ones"), C("blk")
        BANK = [ps_g[:, 0, :], ps_g[:, 1, :], ps_u[:, 0, :], ps_u[:, 1, :]]
        HALVES = (slice(0, NX), slice(NX, NTOK))

        w_here = [sem(f"w_here{s}") for s in range(SLOTS)]
        w_hi, w_lo = sem("w_hi"), sem("w_lo")
        mm_done = sem("mm_done")
        o_free = sem("o_free")
        c_in, x_in, m_in, ic_in, bt_in, rel_in, lora_in, lam_in = (sem(s) for s in (
            "c_in", "x_in", "m_in", "ic_in", "bt_in", "rel_in", "lora_in", "lam_in"))
        nm_sq, nm_sum, nm_std, nm_rstd = sem("nm_sq"), sem("nm_sum"), sem("nm_std"), sem("nm_rstd")
        nm_t, nm_hi, h_ready = sem("nm_t"), sem("nm_hi"), sem("h_ready")
        g_act, u_mul, a_hi, a_ready = sem("g_act"), sem("u_mul"), sem("a_hi"), sem("a_ready")
        ad_silu, ad_hi, ad_lo, ad_turn, ad_col = (sem(n) for n in ("ad_silu", "ad_hi", "ad_lo", "ad_turn", "ad_col"))
        act_seq, dve_seq = sem("act_seq"), sem("dve_seq")
        y_hi, y_ready = sem("y_hi"), sem("y_ready")
        pl_diff = sem("pl_diff")
        lam_sum, lam_exp = sem("lam_sum"), sem("lam_exp")
        ro_mm, ro_sin, ro_done = sem("ro_mm"), sem("ro_sin"), sem("ro_done")
        sl_sq, sl_sum, sl_std, sl_y = sem("sl_sq"), sem("sl_sum"), sem("sl_std"), sem("sl_y")
        hn_sq, hn_sum, hn_std, hn_done = sem("hn_sq"), sem("hn_sum"), sem("hn_std"), sem("hn_done")
        at_s, at_m, at_e, at_p = sem("at_s"), sem("at_m"), sem("at_e"), sem("at_p")
        at_b = [sem("at_b0"), sem("at_b1")]
        at_t, at_c, at_o, at_y = sem("at_t"), sem("at_c"), sem("at_o"), sem("at_y")
        bi_row, bi_sb, bi_dram = sem("bi_row"), sem("bi_sb"), sem("bi_dram")
        rw = {n: sem("rw_" + n) for n in (
            "shift", "lora", "z", "zb", "zs", "a_mm", "a_act", "a_free", "g_mm", "g_act", "sq", "ss", "std", "kk", "bsq", "bsum", "bon",
            "cum", "dec", "feat", "tp", "tm", "lp", "lmask", "p", "pm", "t", "tt", "mv", "mvx", "tx", "txs", "rp", "rps",
            "lpm", "mp", "mpm", "tib", "gz", "gzs", "s", "ss2", "y", "y_in", "yout", "mean", "cen", "var", "vstd", "fin")}
        out_done = sem("out_done")
        block = ctx.enter_context(nc.Block())

        def cut(tensor, first, count, pattern=None, **kw):
            v = tensor[:, first:first + count]
            return v.rearrange(pattern, **kw) if pattern else v

        pad = [cut(scr, i * 1088, 1088, "p (a s u) -> p a s u", a=2, s=2) for i in range(3)]
        icnt = cut(scr, 3 * 1088, 16 * NX)
        q_d = cut(scr, 0, 2048, "p (h n) -> p h n", h=8)
        k_d = cut(scr, 2048, 4096, "p (h n) -> p h n", h=8)
        v_d = cut(scr, 6144, 4096, "p (t n) -> p t n", t=4)
        ada_rows = scr[0:4, 0:256 * ADA_FFN]
        y_all = cut(tsq, 0, 2048, "p (k n) -> p k n", n=NX)
        probs = [cut(tsq, 2048 + 1024 * i, 1024) for i in range(2)]
        probs_t = [cut(big, 768 * i, 768, "p (b n) -> p b n", n=128) for i in range(2)]
        mem_x = cut(scr, 0, 2048, "p (k n) -> p k n", n=NX)
        mem_k = cut(scr, 2048, 512, "p (k n) -> p k n", n=NX)
        mem_v = cut(scr, 2560, 512, "p (t n) -> p t n", n=256)
        proj = cut(scr, 3072, 20 * 257, "p (i n) -> p i n", n=257)
        mem_q = {0: cut(scr, 8212, 512, "p (k n) -> p k n", n=NX), 1: cut(scr, 7680, 512, "p (k n) -> p k n", n=NX)}
        r_, k_, v_ = proj[:, 0:6, 1:257], proj[:, 6:12, 1:257], proj[:, 12:18, 1:257]
        shifted = cut(big, 0, 20 * NX, "p (i n) -> p i n", n=NX)
        zs = cut(big, 0, 2 * RW, "p (u n) -> p u n", n=RW)
        aa = cut(big, 1536, 1536, "p (i n) -> p i n", n=NX)
        kk = cut(big, 3072, 1536, "p (i n) -> p i n", n=NX)
        gg = cut(big, 4608, 1536, "p (i n) -> p i n", n=NX)
        bon = cut(big, 6144, 1536, "p (i n) -> p i n", n=NX)
        lora = cut(scr, 0, RW)
        gup = cut(scr, RW, RW)
        w0b = cut(tsq, 2048, RW)
        dec = cut(scr, 8724, 768, "p (e n) -> p e n", n=NX)
        dinc, dexc, dinv = dec[:, 0, :], dec[:, 1, :], dec[:, 2, :]
        gi = cut(scr, 9492, 128, "p (c n) -> p c n", n=64)
        zd = cut(scr, 9620, 192, "p (c n) -> p c n", n=64)
        xc = x[:, :, NX:NTOK]
        tmaj = [cut(tsq, 2048, 768, "p (e u n) -> p e u n", e=3, u=2), xc[:, 0:3, :].rearrange("p e (u n) -> p e u n", u=2)]
        lp = [cut(tsq, 3072, 1024, "p (m e n) -> p m e n", m=4, e=2), xc[:, 4:8, :].rearrange("p m (e n) -> p m e n", e=2)]
        mp = [cut(scr, 0, 1024, "p (m e n) -> p m e n", m=4, e=2),
              cst[:, cat["cos"]:cat["cos"] + 1024].rearrange("p (m e n) -> p m e n", m=4, e=2)]
        xs = [cut(scr, 1024 + 1024 * j, 512, "p (m n) -> p m n", m=4) for j in range(2)]
        tx = cut(scr, 1536, 512, "p (m n) -> p m n", m=4)
        ti = cut(big, 7680, 512, "p (m n) -> p m n", m=4)
        tit = [cut(hid, 0, 512, "p (m n) -> p m n", m=4), cut(scr, 8212, 512, "p (m n) -> p m n", m=4)]
        pp = cut(hid, 512, 512, "p (m n) -> p m n", m=4)
        ar = [cut(t, at, 512, "p (u e n) -> p u e n", u=2, e=2) for t, at in ((hid, 1024), (scr, 2560))]
        ends = cols[:, 24:36].rearrange("p (j c) -> p j c", j=3)
        INV, FREE = [ps_o[:, b, :] for b in range(3)], [ps_o[:, 3, :], ps_g[:, 0, :], ps_u[:, 0, :], ps_u[:, 1, :], ps_g[:, 1, :]]
        be = cut(hid, 1536, 256, "p (u n) -> p u n", u=2)
        ka = cut(hid, 1792, 256, "p (u n) -> p u n", u=2)
        rp = cut(rstd, 0, 256, "p (u n) -> p u n", u=2)
        st2 = cut(rstd, 256, 128, "p (c n) -> p c n", n=64)
        k_g = cut(scr, 3072, 1536, "p (k n) -> p k n", n=NX)
        v_g = cut(scr, 4608, 1536, "p (t n) -> p t n", n=RW)
        q_g = cut(scr, 6144, 1536, "p (k n) -> p k n", n=NX)
        bias = [cut(scr, 8192 + 768 * i, 768, "p (g n) -> p g n", g=3) for i in range(2)]
        bt = scr[0:32, 0:3072]
        rowb = scr[0:4, 3072:4608]
        rel = cols[0:32, 40:52]
        lam_col = cols[:, 52:53]
        qgain = cols[:, 53:56]

        def over(v, n):
            return v.unsqueeze(1).broadcast_to([v.shape[0], n] + list(v.shape[1:]))

        two = lambda v: v.rearrange("p (u n) -> p u n", u=2)
        HEADS = lambda h: (h // 2, slice(64 * (h % 2), 64 * (h % 2) + 64))

        def att_diff(g0):
            units = []
            for h in range(DIFF_HEADS):
                for tt in range(2):
                    t = slice(tt * 128, (tt + 1) * 128)
                    units.append(dict(
                        scores=[((slice(0, 128), j, slice(0, 512)), q_d[64 * j:64 * j + 64, h, t], k_d[64 * j:64 * j + 64, h, :])
                                for j in range(2)], width=512, subs=2, nb=4, rows=slice(0, 128),
                        v=[v_d[:, b, h * 128:(h + 1) * 128] for b in range(4)], y=y_all[:, h, t], bias=None))
            return units

        def att_mem(l):
            units = []
            for h in range(4):
                k, r = HEADS(h)
                for tt in range(2):
                    t = slice(tt * 128, (tt + 1) * 128)
                    units.append(dict(
                        scores=[((slice(0, 128), 0, slice(0, 256)), mem_q[l][r, k, t], mem_k[r, k, :])], width=256, subs=1, nb=2,
                        rows=r, v=[mem_v[:, b, h * 64:(h + 1) * 64] for b in range(2)],
                        y=y_all[r, (6 if l == 0 else 2) + k, t], bias=None))
            return units

        def att_dil():
            units = []
            for j in range(4):
                for tt in range(2):
                    t = slice(tt * 128, (tt + 1) * 128)
                    sc_, v = [], []
                    for g in range(3):
                        k, r = HEADS(4 * g + j)
                        sc_.append(((slice(0, 128), g // 2, slice(256 * (g % 2), 256 * (g % 2) + 256)), q_g[r, k, t], k_g[r, k, :]))
                        v += [v_g[:, b, (4 * g + j) * 64:(4 * g + j + 1) * 64] for b in range(2)]
                    k, r = HEADS(j)
                    units.append(dict(scores=sc_, width=768, subs=1, nb=6, rows=r, v=v, y=y_all[r, k, t], bias=(j, tt)))
            return units

        ATT = [att_diff(0), att_mem(0), att_dil(), att_mem(1)]
        AT0 = [sum(len(a) for a in ATT[:i]) for i in range(5)]
        DIL0 = AT0[2]

        @block.sync
        def _(sp):
            sp.dma_start(vec[:], VEC).then_inc(c_in, 16)
            sp.dma_start(cst[:], CST).then_inc(c_in, 16)
            for s in range(SLOTS):
                sp.dma_start(wraw[:, s, :], W[s * 128:(s + 1) * 128, :]).then_inc(w_here[s], 16)
            with sp.Fori(1, PADDED // SLOTS) as i:
                for s in range(SLOTS):
                    sp.wait_ge(w_lo, i * SLOTS + (s + 1 - SLOTS))
                    sp.dma_start(wraw[:, s, :], W[ds(i * (SLOTS * 128) + s * 128, 128), :]).then_inc(w_here[s], 16)
            sp.wait_ge(o_free, freed(TILE0[-1] + KT))
            sp.dma_start(OUT, x[:, :, 0:NX]).then_inc(out_done, 16)
            sp.wait_ge(out_done, 16)

        @block.gpsimd
        def _(pool):
            pool.dma_start(x[:], XT).then_inc(x_in, 16)
            pool.dma_start(lamb[:], LAM).then_inc(lam_in, 16)
            pool.dma_start(rel, REL).then_inc(rel_in, 16)
            pool.wait_ge(ad_turn, 2)
            pool.dma_start(icnt, ICNT).then_inc(ic_in, 16)
            pool.wait_ge(o_free, freed(TILE0[FIRST["ffn", 3]]))
            pool.dma_start(mem_x, MEMT).then_inc(m_in, 16)
            pool.wait_ge(mm_done, DONE[FIRST["a_in", 0] - 1])
            pool.dma_start(lora, LORA).then_inc(lora_in, 16)
            pool.dma_start(gup, GUP).then_inc(lora_in, 16)
            pool.wait_ge(at_y, AT0[2])
            pool.dma_start(w0b, W0B).then_inc(lora_in, 16)
            pool.wait_ge(o_free, freed(TILE0[FIRST["ffn", 5]]))
            pool.dma_start(bt, BT).then_inc(bt_in, 16)
            pool.wait_ge(bi_sb, 3)
            pool.dma_start(bass.AP(bias_rows, 0, [[512, 4], [2048, 3], [1, 512]]), rowb.rearrange("p (g n) -> p g n", g=3)).then_inc(bi_dram, 16)
            pool.wait_ge(bi_dram, 16)
            pool.dma_start(mem_x, MEMT).then_inc(m_in, 16)
            pool.wait_ge(o_free, freed(TILE0[FIRST["b_out", 0]]))
            for u, unit in enumerate(ATT[2]):
                j, tt = unit["bias"]
                if u >= 2:
                    pool.wait_ge(at_m, DIL0 + u - 1)
                pool.dma_start(bias[u % 2], bass.AP(bias_rows, j * 512 + tt * 128, [[1, 128], [2048, 3], [1, 256]])).then_inc(at_b[u % 2], 16)
            for slot in at_b:
                pool.wait_ge(slot, 16 * (len(ATT[2]) // 2))

        @block.scalar
        def _(act):
            st = {"seq": 0, "k": 0, "t": 0, "h": 0, "hn": 0, "y": 0}

            def link(ins):
                st["seq"] += 1
                ins.then_inc(act_seq, 1)
                act.wait_ge(act_seq, st["seq"])

            def split_hi(n, i=None, step=1, per=SLOTS):
                if n >= PADDED:
                    return
                off = 0 if i is None else i
                act.wait_ge(w_here[n % SLOTS], off * (16 * per // SLOTS) + 16 * (n // SLOTS + 1))
                if n >= SLOTS:
                    act.wait_ge(mm_done, off * step + DONE[n - SLOTS])
                nc.scalar.activation(whi[:, n % SLOTS, :], wraw[:, n % SLOTS, :], ACT.Copy).then_inc(w_hi, 1)

            def norm(src, N, B, mode, ready, n):
                k = st["k"]
                st["k"] += 1
                if st["h"]:
                    act.wait_ge(h_ready, st["h"])
                nc.scalar.activation(cols[:, 61:62], C("eps", 1), ACT.Sqrt)
                for d in range(KT):
                    ready(act, d)
                    nc.scalar.activation(tsq[:, d * NTOK:d * NTOK + N], src(d)[:, 0:N], ACT.Square).then_inc(nm_sq, 1)
                act.wait_ge(nm_sum, k + 1)
                nc.scalar.activation(rstd[:, 0:N], ps_g[:, 0, 0:N], ACT.Sqrt, bias=C("eps", 1), scale=1.0 / D).then_inc(nm_std, 1)
                if n and mode == "split":
                    act.wait_ge(mm_done, DONE[n - 1])
                for d in range(KT):
                    for j in range(N // NX):
                        st["t"] += 1
                        if mode == "final":
                            continue
                        act.wait_ge(nm_t, st["t"])
                        src_t = tsq[:, d * NTOK + j * NX:d * NTOK + (j + 1) * NX]
                        dst = src_t if mode == "plain" else hh[:, d, HALVES[j]]
                        if B is None:
                            nc.scalar.activation(dst, src_t, ACT.Copy).then_inc(nm_hi, 1)
                        else:
                            nc.scalar.activation(dst, src_t, ACT.Identity, bias=B(d, j)).then_inc(nm_hi, 1)
                        st["h"] += mode == "split"

            def after(n):
                return lambda eng, d: eng.wait_ge(o_free, freed(TILE0[n] - KT + d + 1))

            def ffn(f, N):
                n0, g0 = FIRST["ffn", f], f * GROUPS
                sg = tsq[:, 0:1024].rearrange("p (j n) -> p j n", j=2)
                tmp = tsq[:, 1024:2048].rearrange("p (j n) -> p j n", j=2)

                def silu(done, group):
                    act.wait_ge(mm_done, done)
                    if group is not None:
                        act.wait_ge(u_mul, group)
                    nc.scalar.activation(sg[:, :, 0:N], ps_g[:, :, 0:N], ACT.Silu).then_inc(g_act, 1)

                def hidden(group):
                    act.wait_ge(u_mul, group + 1)
                    nc.scalar.activation(ah[:, :, 0:N], tmp[:, :, 0:N], ACT.Copy).then_inc(a_hi, 1)

                per, step, _, _, n_down, _, n_last = ffn_pass(f)
                silu(DONE[n0], g0 or None)
                split_hi(n0 + 3)
                split_hi(n0 + 4)
                hidden(g0)
                with act.Fori(0, GROUPS - 1) as i:
                    split_hi(n0 + 5, i, step, per)
                    silu(i * step + DONE[n0 + 2], i + (g0 + 1))
                    for n in range(n0 + 6, n0 + 5 + per):
                        split_hi(n, i, step, per)
                        if n - SLOTS == n_down:
                            hidden(i + (g0 + 1))
                split_hi(n_last + SLOTS)
                if f < 2:
                    act.wait_ge(ad_col, f + 2)

            def chunks(stage, i):
                n0 = FIRST[stage, i]
                for n in range(n0, FIRST_AFTER[stage, i]):
                    split_hi(n + SLOTS)

            def mod(l, a):
                return lambda d, j: mods[:, l, 24 * a + d, j:j + 1]

            def head_norm(n_banks):
                st["hn"] += 1
                act.wait_ge(hn_sum, st["hn"])
                for b in range(n_banks):
                    ins = nc.scalar.activation(hid[:, b * 512:(b + 1) * 512], BANK[b], ACT.Sqrt, bias=C("eps", 1), scale=1.0 / 64)
                ins.then_inc(hn_std, 1)

            def split_y(src, nt, width=NX):
                nc.scalar.activation(hh[:, 0:nt, 0:width], src, ACT.Copy).then_inc(y_hi, 1)

            def attend(a):
                U = ATT[a]

                def copy(u):
                    g = AT0[a] + u
                    act.wait_ge(at_t, g + 1)
                    if g >= 2:
                        act.wait_ge(at_o, g - 1)
                    nb = U[u]["nb"]
                    for b in range(0, nb, 4):
                        w = min(4, nb - b)
                        ins = nc.scalar.activation(probs_t[g % 2][:, b:b + w, :], ps_o[:, b // 4, 0:w * 128].rearrange("p (b n) -> p b n", n=128), ACT.Copy)
                    ins.then_inc(at_c, 1)

                for u, unit in enumerate(U):
                    g = AT0[a] + u
                    act.wait_ge(at_m, g + 1)
                    if g >= 2:
                        act.wait_ge(at_t, g - 1)
                    bank = ps_g if g % 2 == 0 else ps_u
                    w = unit["width"]
                    for j in range(unit["subs"]):
                        src = bank[:, j, 0:w] if unit["bias"] is None else probs[g % 2][:, 0:w]
                        ins = nc.scalar.activation(probs[g % 2][:, j * w:(j + 1) * w], src, ACT.Exp, bias=cols[:, 4 * (g % 2) + j:4 * (g % 2) + j + 1],
                                                   accum_out=cols[:, 8 + 4 * (g % 2) + j:9 + 4 * (g % 2) + j])
                    ins.then_inc(at_e, 1)
                    if u:
                        copy(u - 1)
                copy(len(U) - 1)

            act.wait_ge(c_in, 32)
            nc.scalar.activation(sc[:], V("c", 0, 16), ACT.Silu).then_inc(ad_silu, 1)
            act.wait_ge(ad_silu, 1)
            nc.scalar.activation(cs[:, :, 0:2], sc[:].rearrange("p (v k) -> p k v", v=2), ACT.Copy).then_inc(ad_hi, 1)
            for n in range(SLOTS):
                split_hi(n)
            for n in range(ADA_FIRST):
                split_hi(n + SLOTS)
            act.wait_ge(ad_col, 1)
            norm(lambda d: x[:, d, :], NTOK, mod(0, 0), "split", lambda eng, d: eng.wait_ge(x_in, 16), FIRST["ffn", 0])
            ffn(0, NTOK)
            norm(lambda d: x[:, d, :], NTOK, mod(0, 1), "plain", after(FIRST["pool", 0]), FIRST["pool", 0])
            for g in range(4):
                act.wait_ge(pl_diff, g + 1)
                nc.scalar.activation(hh[:, 2 * g:2 * g + 2, :], tsq[:, 1024 * g:1024 * (g + 1)].rearrange("p (a n) -> p a n", a=2), ACT.Copy).then_inc(y_hi, 1)
            chunks("pool", 0)
            norm(lambda d: x[:, d, :], NTOK, mod(0, 2), "split", after(FIRST["ffn", 1]), FIRST["ffn", 1])
            ffn(1, NTOK)
            norm(lambda d: x[:, d, :], NTOK, mod(1, 0), "split", after(FIRST["ffn", 2]), FIRST["ffn", 2])
            ffn(2, NTOK)
            norm(lambda d: x[:, d, :], NTOK, mod(1, 1), "split", after(FIRST["qkv", 0]), FIRST["qkv", 0])
            chunks("qkv", 0)
            act.wait_ge(lam_sum, 1)
            nc.scalar.activation(cols[:, 58:60], cols[:, 56:58], ACT.Exp).then_inc(lam_exp, 1)
            attend(0)
            act.wait_ge(sl_sum, 1)
            for b in range(4):
                ins = nc.scalar.activation(big[:, 4096 + 512 * b:4608 + 512 * b], BANK[b], ACT.Sqrt, bias=C("eps", 1), scale=1.0 / 128)
            ins.then_inc(sl_std, 1)
            act.wait_ge(sl_y, 1)
            split_y(y_all, KT)
            chunks("wo", 0)
            norm(lambda d: x[:, d, :], NX, mod(1, 2), "split", after(FIRST["ffn", 3]), FIRST["ffn", 3])
            ffn(3, NX)
            norm(lambda d: x[:, d, :], NX, None, "final", after(FIRST["ffn", 4]), FIRST["ffn", 4])
            t_final = st["t"]
            norm(lambda d: x[:, d, :], NX, None, "split", lambda eng, d: eng.wait_ge(nm_t, t_final), FIRST["ffn", 4])
            ffn(4, NX)
            norm(lambda d: mem_x[:, d, :], NX, None, "split", lambda eng, d: eng.wait_ge(m_in, 16), FIRST["memkv", 0])
            chunks("memkv", 0)
            head_norm(1)
            norm(lambda d: x[:, d, :], NX, None, "split", after(FIRST["memkv", 0]), FIRST["a_in", 0])
            chunks("a_in", 0)
            head_norm(1)
            attend(1)
            act.wait_ge(rw["shift"], 1)
            nc.scalar.activation(proj[0:64, 18, 1:257], proj[0:64, 18, 1:257], ACT.Tanh)
            nc.scalar.activation(proj[:, 19, 1:257], proj[:, 19, 1:257], ACT.Sigmoid).then_inc(rw["lora"], 1)
            act.wait_ge(rw["zb"], 1)
            nc.scalar.activation(zs, zs, ACT.Sigmoid).then_inc(rw["zs"], 1)
            for i in range(RT):
                act.wait_ge(rw["a_mm"], i + 1)
                nc.scalar.activation(aa[:, i, :], ps_o[:, i % 2, 0:NX], ACT.Sigmoid, bias=V("a_a0_2", i)).then_inc(rw["a_act"], 1)
            for i in range(RT):
                act.wait_ge(rw["g_mm"], i + 1)
                nc.scalar.activation(gg[:, i, :], ps_o[:, 2 + i % 2, 0:NX], ACT.Copy).then_inc(rw["g_act"], 1)
            act.wait_ge(rw["ss"], 1)
            for b in range(3):
                ins = nc.scalar.activation(hid[:, b * 512:(b + 1) * 512], BANK[b], ACT.Sqrt)
            ins.then_inc(rw["std"], 1)
            c0 = math.exp(-0.5)
            quarters = "p (m n) -> p m n"

            def decays(i):
                act.wait_ge(rw["cum"], i + 1)
                if i:
                    act.wait_ge(rw["feat"], i)
                cum = FREE[1].rearrange("p (u e n) -> p u e n", u=2, e=2)
                nc.scalar.activation(dinc.rearrange("p (u n) -> p u n", u=2), cum[:, :, 0, :], ACT.Exp, scale=-c0)
                nc.scalar.activation(dexc.rearrange("p (u n) -> p u n", u=2), cum[:, :, 1, :], ACT.Exp, scale=-c0)
                nc.scalar.activation(dinv.rearrange("p (u n) -> p u n", u=2), cum[:, :, 0, :], ACT.Exp, scale=c0).then_inc(rw["dec"], 1)

            def token_major(i):
                act.wait_ge(rw["tp"], i + 1)
                nc.scalar.activation(tmaj[i % 2][:, 0:2], FREE[1].rearrange("p (e u n) -> p e u n", e=2, u=2), ACT.Copy)
                nc.scalar.activation(tmaj[i % 2][:, 2, :, :], FREE[4][:, 0:256].rearrange("p (u n) -> p u n", u=2), ACT.Copy)
                al_ = FREE[4][:, 256:512].rearrange("p (u q n) -> p q u n", u=2, q=2)
                nc.scalar.activation(xs[i % 2][:, :, 0:64].rearrange("p (q u) n -> p q u n", q=2), al_, ACT.Copy).then_inc(rw["tm"], 1)

            def mv_out(i):
                act.wait_ge(rw["mv"], i + 1)
                nc.scalar.activation(xs[i % 2][:, :, 64:128], FREE[4][:, 0:256].rearrange(quarters, m=4), ACT.Copy).then_inc(rw["mvx"], 1)

            def tx_out(i):
                act.wait_ge(rw["tx"], i + 1)
                nc.scalar.activation(tx, FREE[0].rearrange(quarters, m=4), ACT.Copy).then_inc(rw["txs"], 1)

            decays(0)
            token_major(0)
            mv_out(0)
            for i in range(RT + 1):
                if i:
                    tx_out(i - 1)
                if i + 1 < RT:
                    decays(i + 1)
                if i + 1 < RT:
                    token_major(i + 1)
                if i + 1 < RT:
                    mv_out(i + 1)
            act.wait_ge(rw["var"], 1)
            for b in range(3):
                ins = nc.scalar.activation(hid[:, b * 512:(b + 1) * 512], BANK[b], ACT.Sqrt, bias=C("lnx_eps", 1), scale=1.0 / 64)
            ins.then_inc(rw["vstd"], 1)
            act.wait_ge(rw["fin"], 1)
            act.wait_ge(at_y, AT0[2])
            split_y(y_all, KT)
            chunks("a_out", 0)
            norm(lambda d: x[:, d, :], NX, None, "split", after(FIRST["ffn", 5]), FIRST["ffn", 5])
            ffn(5, NX)
            norm(lambda d: x[:, d, :], NX, None, "split", after(FIRST["kv", 0]), FIRST["kv", 0])
            chunks("kv", 0)
            head_norm(3)
            norm(lambda d: x[:, d, :], NX, None, "split", lambda eng, d: None, FIRST["ffn", 6])
            ffn(6, NX)
            norm(lambda d: mem_x[:, d, :], NX, None, "split", lambda eng, d: eng.wait_ge(m_in, 32), FIRST["memkv", 1])
            chunks("memkv", 1)
            head_norm(1)
            norm(lambda d: x[:, d, :], NX, None, "split", after(FIRST["memkv", 1]), FIRST["b_q", 0])
            chunks("b_q", 0)
            head_norm(3)
            head_norm(1)
            attend(2)
            attend(3)
            act.wait_ge(at_y, AT0[4])
            split_y(y_all[:, 0:4, :], 4)
            chunks("b_out", 0)
            norm(lambda d: x[:, d, :], NX, None, "split", after(FIRST["ffn", 7]), FIRST["ffn", 7])
            ffn(7, NX)

        @block.vector
        def _(dve):
            st = {"seq": 0, "k": 0, "t": 0, "hi": 0, "hn": 0, "y": 0}
            stt, tt_, ts_ = nc.vector.scalar_tensor_tensor, nc.vector.tensor_tensor, nc.vector.tensor_scalar

            def link(ins):
                st["seq"] += 1
                ins.then_inc(dve_seq, 1)
                dve.wait_ge(dve_seq, st["seq"])

            def split_lo(n, i=None, per=SLOTS):
                if n >= PADDED:
                    return
                dve.wait_ge(w_hi, n + 1 if i is None else i * per + (n + 1))
                tt_(wlo[:, n % SLOTS, :], wraw[:, n % SLOTS, :], whi[:, n % SLOTS, :].bitcast(f32), sub).then_inc(w_lo, 1)

            def norm(src, N, A, B, mode):
                k = st["k"]
                st["k"] += 1
                dve.wait_ge(nm_std, k + 1)
                nc.vector.reciprocal(rstd[:, 0:N], rstd[:, 0:N]).then_inc(nm_rstd, 1)
                dve.wait_ge(nm_rstd, k + 1)
                units = [(d, j) for d in range(KT) for j in range(N // NX)]

                def scaled(d, j):
                    dst = src(d)[:, HALVES[j]] if mode == "final" else tsq[:, d * NTOK + j * NX:d * NTOK + (j + 1) * NX]
                    stt(dst, src(d)[:, HALVES[j]], A(d, j), rstd[:, HALVES[j]], mult, mult).then_inc(nm_t, 1)
                    st["t"] += 1

                def rest(d, j):
                    st["hi"] += 1
                    dve.wait_ge(nm_hi, st["hi"])
                    t = tsq[:, d * NTOK + j * NX:d * NTOK + (j + 1) * NX]
                    up = hh[:, d, HALVES[j]].bitcast(f32)
                    if B is None:
                        tt_(hl[:, d, HALVES[j]], t, up, sub).then_inc(h_ready, 1)
                    else:
                        stt(hl[:, d, HALVES[j]], t, B(d, j), up, add, sub).then_inc(h_ready, 1)

                lag = 3 if mode == "split" else 0
                for q in range(len(units) + lag):
                    if q < len(units):
                        scaled(*units[q])
                    if mode == "split" and q >= lag:
                        rest(*units[q - lag])
                if mode == "plain":
                    st["hi"] += len(units)
                    dve.wait_ge(nm_hi, st["hi"])

            def out_tiles(n):
                for q in range(DONE[n] - (DONE[n - 1])):
                    dve.wait_ge(mm_done, DONE[n - 1] + q + 1)
                    yield ps_o[:, (TILE0[n] + q) % 4, :]

            def residual(src, d, N, gate):
                for j in range(N // NX):
                    ins = stt(x[:, d, HALVES[j]], src[:, HALVES[j]], gate(d, j), x[:, d, HALVES[j]], mult, add)
                ins.then_inc(o_free, 1)

            def ffn(f, N, gate):
                n0, g0 = FIRST["ffn", f], f * GROUPS
                per, step, _, n_up, n_down, n_ada, n_last = ffn_pass(f)
                sg = tsq[:, 0:1024].rearrange("p (j n) -> p j n", j=2)
                tmp = tsq[:, 1024:2048].rearrange("p (j n) -> p j n", j=2)

                def product(group, done, last=True):
                    dve.wait_ge(mm_done, done)
                    if last:
                        dve.wait_ge(a_ready, group)
                    dve.wait_ge(g_act, group + 1)
                    tt_(tmp[:, :, 0:N], sg[:, :, 0:N], ps_u[:, :, 0:N], mult).then_inc(u_mul, 1)

                def hidden(group):
                    dve.wait_ge(a_hi, group + 1)
                    tt_(al[:, :, 0:N], tmp[:, :, 0:N], ah[:, :, 0:N].bitcast(f32), sub).then_inc(a_ready, 1)

                def down(n, done):
                    for d in range(KT):
                        dve.wait_ge(mm_done, done + (d + 1))
                        residual(ps_o[:, (TILE0[n] + d) % BANKS, :], d, N, gate)

                product(g0, DONE[n0 + 1], g0 > 0)
                split_lo(n0 + 3)
                split_lo(n0 + 4)
                hidden(g0)
                with dve.Fori(0, GROUPS - 1) as i:
                    split_lo(n0 + 5, i, per)
                    for n in range(n0 + 3, n0 + 2 + per):
                        if n == n_up:
                            product(i + (g0 + 1), i * step + DONE[n])
                        elif n == n_down:
                            down(n, i * step + DONE[n - 1])
                        else:
                            ada_out(n, n_ada.index(n), i, step)
                        if n == n_down and not n_ada:
                            split_lo(n_up + SLOTS, i, per)
                        if n != n_up or n_ada:
                            split_lo(n + SLOTS, i, per)
                        if n == n_down:
                            hidden(i + (g0 + 1))
                down(n_last, DONE[n_last - 1])
                split_lo(n_last + SLOTS)
                if f < 2:
                    ada_part(f + 1)

            def ada_out(n, c, i=None, step=0):
                off, at = (0, 256 * c) if i is None else (i * step, i * 768 + 256 * c)
                rows = ada_rows[:, at:at + 256] if i is None else ada_rows[:, ds(at, 256)]
                for q in range(DONE[n] - (DONE[n - 1] if n else 0)):
                    dve.wait_ge(mm_done, off + ((DONE[n - 1] if n else 0) + q + 1))
                    part = ps_o[0:4, (TILE0[n] + q) % BANKS, 0:256]
                    if q:
                        dve.wait_ge(o_free, freed(TILE0[n] + q) + (0 if i is None else i * sum(FFN_ADA_PASS)))
                        tt_(rows, rows, part, add).then_inc(o_free, 1)
                    else:
                        nc.vector.tensor_copy(rows, part).then_inc(o_free, 1)

            def ada_part(e):
                c0, c1 = ADA_PARTS[e]
                dve.wait_ge(ad_turn, e + 1)
                flat = mods[:].rearrange("p l t v -> p (l t) v")
                ps = ps_u[:, 0, 0:4 * (c1 - c0)].rearrange("p (t v) -> p t v", v=2)
                tt_(flat[:, 2 * c0:2 * c1, 0], ps[:, :, 0], V("ada_b", 2 * c0, 2 * (c1 - c0)), add)
                link(tt_(flat[:, 2 * c0:2 * c1, 1], ps[:, :, 1], V("ada_b", 2 * c0, 2 * (c1 - c0)), add))
                for l, first, last in (((0, 0, 1),), ((0, 1, 3),), ((1, 0, 3),))[e]:
                  m = mods[:, l]
                  for v in range(2):
                    for a in range(first, last):
                        stt(acol[:, l, a, :, v], m[:, 24 * a + 8:24 * a + 16, v], 1.0, V("norm_g", 24 * l + 8 * a, 8), add, mult)
                        gate = m[:, 24 * a + 16:24 * a + 24, v]
                        if a == 1 and l == 0:
                            tt_(gcol[:, l, a, :, v], gate, V("pool_scale", 0, 8), mult)
                        else:
                            ts_(gcol[:, l, a, :, v], gate, 1.0 if a == 1 else 0.5, None, mult)
                nc.vector.memset(cols[:, 60:61], 0.0).then_inc(ad_col, 1)
                dve.wait_ge(ad_col, e + 1)

            def chunks_out(stage, i, take):
                n0 = FIRST[stage, i]
                for n in range(n0, FIRST_AFTER[stage, i]):
                    for q, tile in enumerate(out_tiles(n)):
                        take(n - n0, q, tile)
                    split_lo(n + SLOTS)

            def add_to_x(N, gate, per):
                return lambda c, q, tile: residual(tile, c * per + q, N, gate)

            def head_norm(buf, nt, gain):
                st["hn"] += 1
                sq = hid[:, 0:nt * NX].rearrange("p (k n) -> p k n", n=NX)
                dve.wait_ge(o_free, freed(st["tiles"]))
                if st["hn"] > 1:
                    dve.wait_ge(hn_done, st["hn"] - 1)
                tt_(sq, buf, buf, mult).then_inc(hn_sq, 1)
                dve.wait_ge(hn_std, st["hn"])
                link(nc.vector.reciprocal(sq, sq))
                stt(buf, buf, gain, sq, mult, mult).then_inc(hn_done, 1)

            def rest_y(src, nt, width=NX):
                st["y"] += 1
                dve.wait_ge(y_hi, st["y"])
                tt_(hl[:, 0:nt, 0:width], src, hh[:, 0:nt, 0:width].bitcast(f32), sub).then_inc(y_ready, 1)

            def attend(a):
                U = ATT[a]

                def maximum(u):
                    g, unit = AT0[a] + u, U[u]
                    dve.wait_ge(at_s, g + 1)
                    if g >= 2:
                        dve.wait_ge(at_p, g - 1)
                    bank = ps_g if g % 2 == 0 else ps_u
                    w = unit["width"]
                    nm = cols[:, 4 * (g % 2):4 * (g % 2) + unit["subs"]]
                    if unit["bias"] is None:
                        nc.vector.reduce_max(nm, bank[:, 0:unit["subs"], 0:w], AX.X, negate=True).then_inc(at_m, 1)
                        return
                    dve.wait_ge(at_b[u % 2], 16 * (u // 2 + 1))
                    if g >= 2:
                        dve.wait_ge(at_t, g - 1)
                    s = probs[g % 2][:, 0:w]
                    by_group = "p (g n) -> p g n"
                    tt_(s[:, 0:512].rearrange(by_group, g=2), bank[:, 0, :].rearrange(by_group, g=2), bias[u % 2][:, 0:2, ::-1], add)
                    link(tt_(s[:, 512:768], bank[:, 1, 0:256], bias[u % 2][:, 2, ::-1], add))
                    nc.vector.reduce_max(nm, s, AX.X, negate=True).then_inc(at_m, 1)

                def normalise(u):
                    g, unit = AT0[a] + u, U[u]
                    dve.wait_ge(at_e, g + 1)
                    w = unit["width"]
                    su = cols[:, 8 + 4 * (g % 2):8 + 4 * (g % 2) + unit["subs"]]
                    r = cols[:, 16 + 4 * (g % 2):16 + 4 * (g % 2) + unit["subs"]]
                    link(nc.vector.reciprocal(r, su))
                    p = probs[g % 2]
                    if unit["subs"] == 1:
                        ts_(p[:, 0:w], p[:, 0:w], r[:, 0:1], None, mult).then_inc(at_p, 1)
                    else:
                        link(tt_(r[:, 1:2], r[:, 1:2], lam_col, mult))
                        link(ts_(p[:, w:2 * w], p[:, w:2 * w], r[:, 1:2], None, mult))
                        stt(p[:, 0:w], p[:, 0:w], r[:, 0:1], p[:, w:2 * w], mult, add).then_inc(at_p, 1)

                def result(u):
                    g, unit = AT0[a] + u, U[u]
                    dve.wait_ge(at_o, g + 1)
                    nc.vector.tensor_copy(unit["y"], ps_o[unit["rows"], 2 + g % 2, 0:128]).then_inc(at_y, 1)

                for u in range(len(U) + 2):
                    if u < len(U):
                        maximum(u)
                    if 1 <= u <= len(U):
                        normalise(u - 1)
                    if u >= 2:
                        result(u - 2)

            def xs_(d):
                return x[:, d, :]

            def A_mod(l, a):
                return lambda d, j: acol[:, l, a, d, j:j + 1]

            def B_mod(l, a):
                return lambda d, j: mods[:, l, 24 * a + d, j:j + 1]

            def gate(l, a):
                return lambda d, j: gcol[:, l, a, d, j:j + 1]

            def gain(name, l=0):
                return lambda d, j: V(name, KT * l + d)

            half = lambda d, j: 0.5
            one = lambda d, j: 1.0

            dve.sem_inc(o_free, BANKS)
            dve.wait_ge(ad_hi, 1)
            tt_(cs[:, :, 2:4], sc[:].rearrange("p (v k) -> p k v", v=2), cs[:, :, 0:2].bitcast(f32), sub).then_inc(ad_lo, 1)
            for n in range(SLOTS):
                split_lo(n)
            for n in range(ADA_FIRST):
                ada_out(n, n)
                split_lo(n + SLOTS)
            ada_part(0)
            norm(xs_, NTOK, A_mod(0, 0), B_mod(0, 0), "split")
            ffn(0, NTOK, gate(0, 0))
            link(nc.vector.memset(scr[:, 0:1088], 0.0))
            norm(xs_, NTOK, A_mod(0, 1), None, "plain")
            dve.wait_ge(ic_in, 16)
            for g in range(4):
                h4 = tsq[:, 1024 * g:1024 * (g + 1)].rearrange("p (a s n) -> p a s n", a=2, s=2)
                link(nc.vector.tensor_copy(pad[0][:, :, :, 8:264], h4))
                link(tt_(pad[1][:, :, :, 1:272], pad[0][:, :, :, 0:271], pad[0][:, :, :, 1:272], add))
                cur, lo = 1, 1
                for e in range(g):
                    b, nxt = 1 << e, 3 - cur
                    lo2 = lo + b
                    hi2 = 272 - (2 * b - 1)
                    link(tt_(pad[nxt][:, :, :, lo2:hi2], pad[cur][:, :, :, lo2 - b:hi2 - b], pad[cur][:, :, :, lo2 + b:hi2 + b], add))
                    cur, lo = nxt, lo2
                mean = cut(scr, (3 - cur) * 1088, 1024, "p (a s n) -> p a s n", a=2, s=2)
                link(tt_(mean, pad[cur][:, :, :, 8:264], icnt[:, g * 1024:(g + 1) * 1024].rearrange("p (a s n) -> p a s n", a=2, s=2), mult))
                tt_(h4, mean, h4, sub).then_inc(pl_diff, 1)
            for g in range(4):
                st["y"] += 1
                dve.wait_ge(y_hi, st["y"])
                tt_(hl[:, 2 * g:2 * g + 2, :], tsq[:, 1024 * g:1024 * (g + 1)].rearrange("p (a n) -> p a n", a=2),
                    hh[:, 2 * g:2 * g + 2, :].bitcast(f32), sub).then_inc(y_ready, 1)
            chunks_out("pool", 0, add_to_x(NTOK, gate(0, 1), 8))
            norm(xs_, NTOK, A_mod(0, 2), B_mod(0, 2), "split")
            ffn(1, NTOK, gate(0, 2))
            norm(xs_, NTOK, A_mod(1, 0), B_mod(1, 0), "split")
            ffn(2, NTOK, gate(1, 0))
            norm(xs_, NTOK, A_mod(1, 1), B_mod(1, 1), "split")

            def take_qkv(c, q, tile):
                if c < 4:
                    ts_(q_d[:, 2 * c + q, :], tile[:, 0:NX], 0.125, None, mult).then_inc(o_free, 1)
                elif c < 8:
                    nc.vector.tensor_copy(k_d[:, 2 * (c - 4) + q, :], tile).then_inc(o_free, 1)
                else:
                    nc.vector.tensor_copy(v_d[:, q, 256 * (c - 8):256 * (c - 7)], tile[:, 0:256]).then_inc(o_free, 1)

            chunks_out("qkv", 0, take_qkv)
            for r in range(8):
                z = q_d[:, 2 * r:2 * r + 2, :] if r < 4 else k_d[:, 2 * (r - 4):2 * (r - 4) + 2, 0:NX]
                t = tsq[:, 512 * (r % 4):512 * (r % 4) + 512].rearrange("p (a n) -> p a n", a=2)
                dve.wait_ge(ro_mm, r + 1)
                tt_(t, BANK[r % 4].rearrange("p (a n) -> p a n", a=2), C("sin", 512).rearrange("p (a n) -> p a n", a=2), mult).then_inc(ro_sin, 1)
                link(tt_(z, z, C("cos", 512).rearrange("p (a n) -> p a n", a=2), mult))
                tt_(z, z, t, add).then_inc(ro_done, 1)
            dve.wait_ge(lam_in, 16)
            for j in range(2):
                link(tt_(lamb[:, 128 * j:128 * j + 64], lamb[:, 128 * j:128 * j + 64], lamb[:, 128 * j + 64:128 * j + 128], mult))
            nc.vector.reduce_sum(cols[:, 56:58], lamb[:].rearrange("p (j n) -> p j n", j=2)[:, :, 0:64], AX.X).then_inc(lam_sum, 1)
            dve.wait_ge(lam_exp, 1)
            link(tt_(lam_col, cols[:, 59:60], cols[:, 58:59], sub))
            link(ts_(lam_col, lam_col, -LAM_INIT, None, add))
            attend(0)
            dve.wait_ge(at_y, AT0[1])
            tt_(big[:, 2048:4096], tsq[:, 0:2048], tsq[:, 0:2048], mult).then_inc(sl_sq, 1)
            dve.wait_ge(sl_std, 1)
            link(nc.vector.reciprocal(big[:, 4096:6144], big[:, 4096:6144]))
            link(tt_(tsq[:, 0:2048], tsq[:, 0:2048], big[:, 4096:6144], mult))
            ts_(tsq[:, 0:2048], tsq[:, 0:2048], V("diff_subln_g"), 1.0 - LAM_INIT, mult, mult).then_inc(sl_y, 1)
            rest_y(y_all, KT)
            chunks_out("wo", 0, add_to_x(NX, gate(1, 1), 2))
            norm(xs_, NX, A_mod(1, 2), B_mod(1, 2), "split")
            ffn(3, NX, gate(1, 2))
            norm(xs_, NX, gain("final_g"), None, "final")
            dve.wait_ge(nm_t, st["t"])
            norm(xs_, NX, gain("ffn_pre_norm_2", 0), None, "split")
            ffn(4, NX, half)

            def take_memkv(c, q, tile):
                nc.vector.tensor_copy(mem_k[:, q, :] if c == 0 else mem_v[:, q, :], tile[:, 0:256]).then_inc(o_free, 1)

            norm(lambda d: mem_x[:, d, :], NX, gain("mem_norm_2", 0), None, "split")
            chunks_out("memkv", 0, take_memkv)
            st["tiles"] = TILE0[FIRST["a_in", 0]]
            head_norm(mem_k, 2, V("mem_k_norm_2", 0))
            norm(xs_, NX, gain("mix_norm_2", 0), None, "split")

            def take_in(c, q, tile):
                i = 2 * c + q
                dst = proj[:, i, 1:257] if i < 20 else mem_q[0][:, i - 20, :]
                nc.vector.tensor_copy(dst, tile[:, 0:NX]).then_inc(o_free, 1)

            link(nc.vector.memset(proj[:, :, 0:1], 0.0))
            chunks_out("a_in", 0, take_in)
            link(ts_(qgain, vec[:, vat["mem_q_norm_2"]:vat["mem_q_norm_2"] + 3], 0.125, None, mult))
            st["tiles"] = TILE0[FIRST["a_out", 0]]
            head_norm(mem_q[0], 2, qgain[:, 0:1])
            attend(1)
            link(tt_(shifted, proj[:, :, 0:256], proj[:, :, 1:257], sub))
            for i in (18, 19, *range(18)):
                ins = stt(proj[:, i, 1:257], shifted[:, i, :], V("a_shift_mu_2", i), proj[:, i, 1:257], mult, add)
            ins.then_inc(rw["shift"], 1)
            dve.wait_ge(rw["shift"], 1)
            dve.wait_ge(lora_in, 48)
            dve.wait_ge(rw["z"], 1)
            for u in range(2):
                bank = ps_g if u == 0 else ps_u
                tt_(zs[:, u, 0:512], bank[:, 0, :], w0b[:, 0:512], add)
                ins = tt_(zs[:, u, 512:768], bank[:, 1, 0:256], w0b[:, 512:768], add)
            ins.then_inc(rw["zb"], 1)
            for i in range(RT):
                ins = ts_(kk[:, i, :], k_[:, i, :], V("a_kk_scale_2", i), None, mult)
            link(ins)
            tt_(bon, kk, kk, mult).then_inc(rw["sq"], 1)
            sq3 = hid[:, 0:1536].rearrange("p (i n) -> p i n", n=NX)
            dve.wait_ge(rw["std"], 1)
            link(ts_(sq3, sq3, 1e-12, None, amax))
            link(nc.vector.reciprocal(sq3, sq3))
            link(tt_(kk, kk, sq3, mult))
            dve.wait_ge(rw["a_act"], RT)
            for i in range(RT):
                ins = ts_(sq3[:, i, :], aa[:, i, :], 1.0, V("a_k_a_2", i), sub, mult)
            link(ins)
            link(stt(k_, sq3, 1.0, k_, add, mult))
            for i in range(RT):
                ins = stt(bon[:, i, :], r_[:, i, :], V("a_r_k_2", i), k_[:, i, :], mult, mult)
            ins.then_inc(rw["bsq"], 1)
            link(tt_(aa, aa, kk, mult))
            dve.wait_ge(rw["bsum"], 1)
            dve.wait_ge(rw["bsq"], 1)
            for b in range(3):
                link(tt_(bon[:, 2 * b:2 * b + 2, :], BANK[b].rearrange("p (i n) -> p i n", n=NX), v_[:, 2 * b:2 * b + 2, :], mult))
            nc.vector.memset(cols[:, 60:61], 0.0).then_inc(rw["bon"], 1)
            m256 = C("lp_mask", 256).rearrange("p (e n) -> p e n", e=2)
            by_unit = "p (m n) -> p m n"

            def features(i):
                dve.wait_ge(rw["dec"], i + 1)
                if i >= 2:
                    dve.wait_ge(rw["rps"], i - 1)
                a = ar[i % 2]
                stt(a[:, :, 0, :], two(kk[:, i, :]), -1.0, two(dexc), mult, mult)
                tt_(a[:, :, 1, :], two(r_[:, i, :]), two(dinc), mult)
                tt_(be, two(aa[:, i, :]), two(dinv), mult)
                nc.vector.tensor_copy(ends[:, i % 3, :], dinc.rearrange("p (c n) -> p c n", n=CH)[:, :, CH - 1])
                tt_(ka, two(k_[:, i, :]), two(dinv), mult).then_inc(rw["feat"], 1)

            def pairs(i, q, which, buf, bank, done):
                dve.wait_ge(rw[which], 2 * i + q + 1)
                tt_(buf[i % 2][:, 2 * q:2 * q + 2], bank.rearrange("p (m e n) -> p m e n", m=2, e=2), over(m256, 2), mult).then_inc(rw[done], 1)

            def start_inverse(i):
                dve.wait_ge(rw["tib"], i + 1)
                dve.wait_ge(rw["lpm"], 2 * i + 2)
                for q, bank in enumerate((FREE[1], FREE[3])):
                    tt_(ti[:, 2 * q:2 * q + 2, :], bank[:, 0:256].rearrange(by_unit, m=2), over(C("m1"), 2), mult)
                link(tt_(tit[i % 2], lp[i % 2][:, :, 0, :], over(C("m1t"), 4), mult))
                tt_(ti, ti, over(ident, 4), add)
                tt_(tit[i % 2], tit[i % 2], over(ident, 4), add).then_inc(rw["lmask"], 1)

            def mask_p(i, l):
                dve.wait_ge(rw["p"], 5 * i + l + 1)
                tt_(pp, INV[0].rearrange(by_unit, m=4), over(C(f"m{2 << l}"), 4), mult).then_inc(rw["pm"], 1)

            def grow(i, l):
                dve.wait_ge(rw["t"], 5 * i + l + 1)
                if l < 4:
                    tt_(ti, ti, INV[1].rearrange(by_unit, m=4), add)
                t = tit[i % 2]
                tt_(t, t, INV[2].rearrange(by_unit, m=4), add).then_inc(rw["tt"], 1)

            def readout(i):
                dve.wait_ge(rw["rp"], i + 1)
                tt_(rp, ar[i % 2][:, :, 1, :], two(FREE[0][:, 0:256]), add).then_inc(rw["rps"], 1)

            def transitions(i):
                dve.wait_ge(rw["gz"], i + 1)
                for c in (1, 2):
                    tt_(gi[:, c - 1, :], FREE[2 + c % 2][:, 64 * (c // 2):64 * (c // 2) + 64], C("ident64", 64), add)
                for c in range(3):
                    ins = ts_(zd[:, c, :], FREE[2 + c % 2][:, 128 + 64 * (c // 2):192 + 64 * (c // 2)], ends[:, i % 3, c:c + 1], None, mult)
                ins.then_inc(rw["gzs"], 1)
                nc.vector.tensor_copy(y_all[:, i, :], FREE[2][:, 256:512]).then_inc(rw["y_in"], 1)

            def state(i, c):
                dve.wait_ge(rw["gzs"], i + 1)
                dve.wait_ge(rw["s"], 2 * i + c + 1)
                stt(st2[:, c, :], FREE[3][:, 256 + 64 * c:320 + 64 * c], ends[:, i % 3, c + 1:c + 2], zd[:, c + 1, :], mult, add).then_inc(rw["ss2"], 1)

            def output(i):
                dve.wait_ge(rw["y_in"], i + 1)
                dve.wait_ge(rw["y"], i + 1)
                y = y_all[:, i, CH:NX]
                tt_(y, y, FREE[2][:, CH:NX], add).then_inc(rw["yout"], 1)

            features(0)
            for q in range(2):
                pairs(0, q, "lp", lp, FREE[q], "lpm")
            for q, b in enumerate((4, 0)):
                pairs(0, q, "mp", mp, FREE[b], "mpm")
            start_inverse(0)
            for i in range(RT + 1):
                inv, post, pre = i < RT, i > 0, i + 1 < RT
                if inv:
                    mask_p(i, 0)
                    grow(i, 0)
                    mask_p(i, 1)
                if post:
                    readout(i - 1)
                if pre:
                    features(i + 1)
                if post:
                    transitions(i - 1)
                if inv:
                    grow(i, 1)
                    mask_p(i, 2)
                if post:
                    state(i - 1, 0)
                if inv:
                    grow(i, 2)
                if post:
                    state(i - 1, 1)
                if pre:
                    pairs(i + 1, 0, "lp", lp, FREE[0], "lpm")
                if inv:
                    mask_p(i, 3)
                if pre:
                    pairs(i + 1, 1, "lp", lp, FREE[1], "lpm")
                if inv:
                    grow(i, 3)
                if post:
                    output(i - 1)
                if pre:
                    pairs(i + 1, 0, "mp", mp, FREE[4], "mpm")
                if inv:
                    mask_p(i, 4)
                if pre:
                    pairs(i + 1, 1, "mp", mp, FREE[0], "mpm")
                if inv:
                    grow(i, 4)
                if pre:
                    start_inverse(i + 1)
            y6 = y_all[:, 0:6, :]
            dve.wait_ge(rw["mean"], 1)
            for b in range(3):
                ins = stt(y6[:, 2 * b:2 * b + 2, :], BANK[b].rearrange("p (i n) -> p i n", n=NX), -1.0 / 64, y6[:, 2 * b:2 * b + 2, :], mult, add)
            link(ins)
            tt_(sq3, y6, y6, mult).then_inc(rw["cen"], 1)
            dve.wait_ge(rw["vstd"], 1)
            link(nc.vector.reciprocal(sq3, sq3))
            link(tt_(y6, y6, sq3, mult))
            for i in range(RT):
                ins = ts_(y6[:, i, :], y6[:, i, :], V("a_lnx_g_2", i), V("a_lnx_b_2", i), mult, add)
            link(ins)
            link(tt_(y6, y6, bon, add))
            dve.wait_ge(rw["g_act"], RT)
            tt_(y6, y6, gg, mult).then_inc(rw["fin"], 1)
            rest_y(y_all, KT)
            chunks_out("a_out", 0, add_to_x(NX, one, 2))
            norm(xs_, NX, gain("ffn_post_norm_2", 0), None, "split")
            ffn(5, NX, half)
            dve.wait_ge(bi_row, 1)
            for g in range(3):
                tt_(rowb[:, 512 * g:512 * (g + 1)], BANK[1 + g][0:4, :], bt[0:4, 1536 + 512 * g:2048 + 512 * g], add).then_inc(bi_sb, 1)
            norm(xs_, NX, gain("kv_norm_2"), None, "split")

            def take_kv(c, q, tile):
                if c < 3:
                    nc.vector.tensor_copy(k_g[:, 2 * c + q, :], tile[:, 0:NX]).then_inc(o_free, 1)
                else:
                    nc.vector.tensor_copy(v_g[:, q, 256 * (c - 3):256 * (c - 2)], tile[:, 0:256]).then_inc(o_free, 1)

            dve.wait_ge(bi_dram, 16)
            chunks_out("kv", 0, take_kv)
            st["tiles"] = TILE0[FIRST["ffn", 6]]
            head_norm(k_g, 6, V("kv_k_norm_2"))
            norm(xs_, NX, gain("ffn_pre_norm_2", 1), None, "split")
            ffn(6, NX, half)
            norm(lambda d: mem_x[:, d, :], NX, gain("mem_norm_2", 1), None, "split")
            chunks_out("memkv", 1, take_memkv)
            st["tiles"] = TILE0[FIRST["b_q", 0]]
            head_norm(mem_k, 2, V("mem_k_norm_2", 1))
            norm(xs_, NX, gain("mix_norm_2", 1), None, "split")

            def take_q(c, q, tile):
                i = 2 * c + q
                nc.vector.tensor_copy(q_g[:, i, :] if i < 6 else mem_q[1][:, i - 6, :], tile[:, 0:NX]).then_inc(o_free, 1)

            chunks_out("b_q", 0, take_q)
            st["tiles"] = TILE0[FIRST["b_out", 0]]
            head_norm(q_g, 6, qgain[:, 2:3])
            head_norm(mem_q[1], 2, qgain[:, 1:2])
            attend(2)
            attend(3)
            rest_y(y_all[:, 0:4, :], 4)
            chunks_out("b_out", 0, add_to_x(NX, one, 4))
            norm(xs_, NX, gain("ffn_post_norm_2", 1), None, "split")
            ffn(7, NX, half)

        @block.tensor
        def _(pe):
            st = {"k": 0, "h": 0, "hn": 0, "y": 0}
            mm = nc.tensor.matmul

            def chunk(n, i=None, per=SLOTS):
                pe.wait_ge(w_lo, n + 1 if i is None else i * per + (n + 1))
                return n % SLOTS

            def weights(s, cols_):
                return (whi[:, s, :].rearrange("p (k n) -> p k n", n=cols_), wlo[:, s, :].rearrange("p (k n) -> p k n", n=cols_))

            def mm3(out, a, b, first, last):
                mm(out, a[1], b[0], start=first, stop=False)
                mm(out, a[0], b[1], start=False, stop=False)
                return mm(out, a[0], b[0], start=False, stop=last)

            def norm(N, split=True):
                st["k"] += 1
                for d in range(KT):
                    pe.wait_ge(nm_sq, (st["k"] - 1) * KT + d + 1)
                    ins = mm(ps_g[:, 0, 0:N], ones, tsq[:, d * NTOK:d * NTOK + N], start=d == 0, stop=d == KT - 1)
                ins.then_inc(nm_sum, 1)
                if split:
                    st["h"] += KT * (N // NX)

            def tile(n, q):
                T = TILE0[n] + q
                pe.wait_ge(o_free, T + 1)
                return ps_o[:, T % 4, :]

            def split_input(N):
                h0, per = st["h"] - KT * (N // NX), N // NX
                return lambda k: pe.wait_ge(h_ready, h0 + (k + 1) * per)

            def project(n, N, rows=KT, width=256, k0=0, w0=0, ready=lambda k: None, q0=0):
                w = weights(chunk(n), width)
                for j in range(width // 128):
                    out = tile(n, q0 + j)
                    for k in range(rows):
                        ready(k)
                        c = slice(j * 128, (j + 1) * 128)
                        ins = mm3(out[:, 0:N], (w[0][:, w0 + k, c], w[1][:, w0 + k, c]), (hh[:, k0 + k, 0:N], hl[:, k0 + k, 0:N]), k == 0, k == rows - 1)
                    ins.then_inc(mm_done, 1)

            def project_first(n, N, of=None):
                ready = split_input(of or N)
                w = [weights(chunk(n + b), 256) for b in range(2)]
                out = [tile(n + b, j)[:, 0:N] for b in range(2) for j in range(2)]
                for k in range(KT):
                    ready(k)
                    for b in range(2):
                        for j in range(2):
                            c = slice(j * 128, (j + 1) * 128)
                            ins = mm3(out[2 * b + j], (w[b][0][:, k, c], w[b][1][:, k, c]), (hh[:, k, 0:N], hl[:, k, 0:N]), k == 0, k == KT - 1)
                            if k == KT - 1:
                                ins.then_inc(mm_done, 1)

            def project_tokens(n, ntok):
                w = weights(chunk(n), 256)
                for q in range(ntok // 128):
                    out, c = tile(n, q), slice(q * 128, (q + 1) * 128)
                    for k in range(KT):
                        ins = mm3(out[:, 0:256], (hh[:, k, c], hl[:, k, c]), (w[0][:, k, :], w[1][:, k, :]), k == 0, k == KT - 1)
                    ins.then_inc(mm_done, 1)

            def ffn(f, N):
                n0, g0 = FIRST["ffn", f], f * GROUPS
                per, _, tiles, n_up, n_down, n_ada, n_last = ffn_pass(f)
                ready = split_input(N)

                def first_halves():
                    w = [weights(chunk(n), 256) for n in (n0, n0 + 1)]
                    for k in range(KT):
                        ready(k)
                        for b, bank in enumerate((ps_g, ps_u)):
                            for j in range(2):
                                c = slice(j * 128, (j + 1) * 128)
                                ins = mm3(bank[:, j, 0:N], (w[b][0][:, k, c], w[b][1][:, k, c]), (hh[:, k, 0:N], hl[:, k, 0:N]), k == 0, k == KT - 1)
                            if k == KT - 1:
                                ins.then_inc(mm_done, 1)

                def half(bank, n, i=None):
                    w = weights(chunk(n, i, per), 256)
                    for j in range(2):
                        for k in range(KT):
                            c = slice(j * 128, (j + 1) * 128)
                            ins = mm3(bank[:, j, 0:N], (w[0][:, k, c], w[1][:, k, c]), (hh[:, k, 0:N], hl[:, k, 0:N]), k == 0, k == KT - 1)
                    ins.then_inc(mm_done, 1)

                def down(n, T, group, i=None):
                    w = weights(chunk(n, i, per), D)
                    pe.wait_ge(a_ready, group + 1)
                    for d in range(KT):
                        pe.wait_ge(o_free, T + (d + 1))
                        for k in range(2):
                            c = slice(d * 128, (d + 1) * 128)
                            ins = mm3(ps_o[:, (TILE0[n] + d) % BANKS, 0:N], (w[0][:, k, c], w[1][:, k, c]), (ah[:, k, 0:N], al[:, k, 0:N]), k == 0, k == 1)
                        ins.then_inc(mm_done, 1)

                first_halves()
                with pe.Fori(0, GROUPS - 1) as i:
                    pe.wait_ge(g_act, i + (g0 + 1))
                    half(ps_g, n0 + 2, i)
                    for n in range(n0 + 3, n0 + 2 + per):
                        if n == n_up:
                            pe.wait_ge(u_mul, i + (g0 + 1))
                            half(ps_u, n, i)
                        elif n == n_down:
                            down(n, i * tiles + TILE0[n], i + g0, i)
                        else:
                            ada(n, i)
                down(n_last, TILE0[n_last], g0 + GROUPS - 1)
                if f < 2:
                    ada_turn(f + 1)

            def ada(n, i=None):
                w = weights(chunk(n, i, len(FFN_ADA_PASS)), 256)
                parts = DONE[n] - (DONE[n - 1] if n else 0)
                for q in range(parts):
                    T = TILE0[n] + q
                    pe.wait_ge(o_free, T + 1 if i is None else i * sum(FFN_ADA_PASS) + (T + 1))
                    rows = range(q * KT // parts, (q + 1) * KT // parts)
                    for k in rows:
                        out = ps_o[0:4, T % BANKS, 0:256]
                        mm(out, cs[:, k, :], w[1][:, k, :], start=k == rows[0], stop=False)
                        ins = mm(out, cs[:, k, :], w[0][:, k, :], start=False, stop=k == rows[-1])
                    ins.then_inc(mm_done, 1)

            def ada_turn(e):
                c0, c1 = ADA_PARTS[e]
                n_last = [FIRST["ada", 0] + ADA_FIRST, FIRST["ffn", 0] + 2 + 6 * (GROUPS - 1), FIRST["ffn", 1] + 2 + 6 * (GROUPS - 1)][e]
                pe.wait_ge(o_free, freed(TILE0[n_last]))
                for t in range(2 * (c1 - c0)):
                    ins = mm(ps_u[:, 0, 2 * t:2 * t + 2], ada_rows[:, 128 * t:128 * (t + 1)], C("pick", 2)[0:4], start=True, stop=True)
                ins.then_inc(ad_turn, 1)

            def head_norm(nt):
                st["hn"] += 1
                pe.wait_ge(hn_sq, st["hn"])
                for b in range((nt + 1) // 2):
                    ins = mm(BANK[b], blk, hid[:, 512 * b:512 * (b + 1)], start=True, stop=True)
                ins.then_inc(hn_sum, 1)

            def attend(a):
                U = ATT[a]

                def scores(u):
                    g, unit = AT0[a] + u, U[u]
                    if g >= 2:
                        pe.wait_ge(at_e, g - 1)
                    bank = ps_g if g % 2 == 0 else ps_u
                    for (rows, b, c), q, k in unit["scores"]:
                        ins = mm(bank[rows, b, c], q, k, start=True, stop=True)
                    ins.then_inc(at_s, 1)

                def flip(u):
                    g, unit = AT0[a] + u, U[u]
                    pe.wait_ge(at_p, g + 1)
                    if g:
                        pe.wait_ge(at_c, g)
                    for b in range(unit["nb"]):
                        ins = nc.tensor.transpose(ps_o[:, b // 4, (b % 4) * 128:(b % 4 + 1) * 128], probs[g % 2][:, b * 128:(b + 1) * 128], ident)
                    ins.then_inc(at_t, 1)

                def values(u):
                    g, unit = AT0[a] + u, U[u]
                    pe.wait_ge(at_c, g + 1)
                    if g >= 2:
                        pe.wait_ge(at_y, g - 1)
                    nb = unit["nb"]
                    for b in range(nb):
                        ins = mm(ps_o[unit["rows"], 2 + g % 2, 0:128], unit["v"][b], probs_t[g % 2][:, b, :], start=b == 0, stop=b == nb - 1)
                    ins.then_inc(at_o, 1)

                scores(0)
                for u in range(len(U)):
                    if u + 1 < len(U):
                        scores(u + 1)
                    if u:
                        values(u - 1)
                    flip(u)
                values(len(U) - 1)

            def y_split():
                st["y"] += 1
                pe.wait_ge(y_ready, st["y"])

            pe.wait_ge(ad_lo, 1)
            for n in range(ADA_FIRST):
                ada(n)
            ada_turn(0)
            norm(NTOK)
            ffn(0, NTOK)
            norm(NTOK, False)
            n = FIRST["pool", 0]
            w = weights(chunk(n), 256)
            for g in range(4):
                y_split()
                for j in range(2):
                    out, c = tile(n, 2 * g + j), slice(j * 128, (j + 1) * 128)
                    for k in range(2):
                        ins = mm3(out, (w[0][:, 2 * g + k, c], w[1][:, 2 * g + k, c]), (hh[:, 2 * g + k, :], hl[:, 2 * g + k, :]), k == 0, k == 1)
                    ins.then_inc(mm_done, 1)
            norm(NTOK)
            ffn(1, NTOK)
            norm(NTOK)
            ffn(2, NTOK)
            norm(NTOK)
            n = FIRST["qkv", 0]
            project_first(n, NX, of=NTOK)
            for c in range(2, 12):
                if c < 8:
                    project(n + c, NX if c < 4 else NTOK)
                else:
                    project_tokens(n + c, NTOK)
            pe.wait_ge(o_free, freed(TILE0[n + 8]))
            for r in range(8):
                z = q_d[:, 2 * r:2 * r + 2, :] if r < 4 else k_d[:, 2 * (r - 4):2 * (r - 4) + 2, 0:NX]
                if r >= 4:
                    pe.wait_ge(ro_sin, r - 3)
                mm(BANK[r % 4].rearrange("p (a n) -> p a n", a=2), C("perm"), z, start=True, stop=True).then_inc(ro_mm, 1)
            pe.wait_ge(ro_done, 8)
            pe.wait_ge(o_free, freed(TILE0[n + 12]))
            attend(0)
            pe.wait_ge(sl_sq, 1)
            for b in range(4):
                ins = mm(BANK[b], ones, big[:, 2048 + 512 * b:2560 + 512 * b], start=True, stop=True)
            ins.then_inc(sl_sum, 1)
            y_split()
            for c in range(4):
                project(FIRST["wo", 0] + c, NX)
            norm(NX)
            ffn(3, NX)
            norm(NX, False)
            norm(NX)
            ffn(4, NX)

            def mem_kv(l):
                norm(NX)
                project(FIRST["memkv", l], NX, ready=split_input(NX))
                project_tokens(FIRST["memkv", l] + 1, NX)
                head_norm(2)

            mem_kv(0)
            norm(NX)
            project_first(FIRST["a_in", 0], NX)
            for c in range(2, 11):
                project(FIRST["a_in", 0] + c, NX)
            head_norm(2)
            pe.wait_ge(hn_done, st["hn"])
            attend(1)
            pe.wait_ge(lora_in, 48)
            pe.wait_ge(rw["lora"], 1)
            for u in range(2):
                bank = ps_g if u == 0 else ps_u
                lhs = proj[0:64, 18, 1 + 128 * u:129 + 128 * u]
                mm(bank[:, 0, :], lhs, lora[0:64, 0:512], start=True, stop=True)
                ins = mm(bank[:, 1, 0:256], lhs, lora[0:64, 512:768], start=True, stop=True)
            ins.then_inc(rw["z"], 1)
            for i in range(RT):
                if i >= 2:
                    pe.wait_ge(rw["a_act"], i - 1)
                mm(ps_o[:, i % 2, 0:NX], lora[64:128, 128 * i:128 * (i + 1)], proj[64:128, 18, 1:257], start=True, stop=True).then_inc(rw["a_mm"], 1)
            for i in range(RT):
                if i >= 2:
                    pe.wait_ge(rw["g_act"], i - 1)
                mm(ps_o[:, 2 + i % 2, 0:NX], gup[:, 128 * i:128 * (i + 1)], proj[:, 19, 1:257], start=True, stop=True).then_inc(rw["g_mm"], 1)
            pe.wait_ge(rw["sq"], 1)
            for b in range(3):
                ins = mm(BANK[b], blk, bon[:, 2 * b:2 * b + 2, :], start=True, stop=True)
            ins.then_inc(rw["ss"], 1)
            pe.wait_ge(rw["std"], 1)
            pe.wait_ge(rw["bsq"], 1)
            for b in range(3):
                ins = mm(BANK[b], blk, bon[:, 2 * b:2 * b + 2, :], start=True, stop=True)
            ins.then_inc(rw["bsum"], 1)
            pe.wait_ge(rw["zs"], 1)
            pe.wait_ge(rw["bon"], 1)
            pe.wait_ge(rw["a_act"], RT)
            pe.wait_ge(rw["g_act"], RT)
            R = [slice(0, 64), slice(64, 128)]
            def tok(i, e, m):
                return tmaj[i % 2][:, e, m % 2, 64 * (m // 2):64 * (m // 2) + 64]

            def decay_sums(i):
                for u in range(2):
                    ins = mm(FREE[1][:, 256 * u:256 * u + 256], zs[:, u, 128 * i:128 * (i + 1)], C("cum", 256), start=True, stop=True)
                ins.then_inc(rw["cum"], 1)

            def to_tokens(i):
                pe.wait_ge(rw["feat"], i + 1)
                if i:
                    pe.wait_ge(rw["mvx"], i)
                for e, src in enumerate((two(v_[:, i, :]), be, ka, ar[i % 2][:, :, 0, :])):
                    for u in range(2):
                        at = (e % 2) * 256 + u * 128
                        ins = nc.tensor.transpose(FREE[1 + 3 * (e // 2)][:, at:at + 128], src[:, u, :], ident)
                ins.then_inc(rw["tp"], 1)

            def pairs(i, q, lhs, bank, done):
                for u in range(2):
                    ins = mm(bank[:, 256 * u:256 * u + 256].rearrange("p (e n) -> p e n", e=2), lhs[R[q], u, :], ar[i % 2][R[q], u, :, :], start=True, stop=True)
                ins.then_inc(rw[done], 1)

            def pairs_lp(i, q):
                if q:
                    pe.wait_ge(rw["tm"], i + 1)
                elif i >= 2:
                    pe.wait_ge(rw["rps"], i - 1)
                pairs(i, q, be, FREE[q], "lp")

            def pairs_mp(i, q):
                if q:
                    pe.wait_ge(rw["lpm"], 2 * i + 1)
                else:
                    pe.wait_ge(rw["tm"], i + 1)
                pairs(i, q, ka, FREE[4 * (1 - q)], "mp")

            def pairs_ti(i):
                pe.wait_ge(rw["lpm"], 2 * i + 2)
                if i >= 2:
                    pe.wait_ge(rw["ss2"], 2 * (i - 1))
                for q in range(2):
                    for u in range(2):
                        ins = mm(FREE[1 + 2 * q][:, 128 * u:128 * (u + 1)], ar[i % 2][R[q], u, 0, :], be[R[q], u, :], start=True, stop=True)
                ins.then_inc(rw["tib"], 1)

            def mix_values(i):
                pe.wait_ge(rw["mpm"], 2 * i + 2)
                for m in range(4):
                    ins = mm(FREE[4][:, 64 * m:64 * (m + 1)], mp[i % 2][:, m, 0, :], tok(i, 0, m), start=True, stop=True)
                ins.then_inc(rw["mv"], 1)

            def level_p(i, l):
                if l:
                    pe.wait_ge(rw["tt"], 5 * i + l)
                else:
                    pe.wait_ge(rw["lmask"], i + 1)
                for m in range(4):
                    ins = mm(INV[0][:, 128 * m:128 * (m + 1)], lp[i % 2][:, m, 0, :], ti[:, m, :], start=True, stop=True)
                ins.then_inc(rw["p"], 1)

            def level_t(i, l):
                pe.wait_ge(rw["pm"], 5 * i + l + 1)
                for m in range(4):
                    c = slice(128 * m, 128 * (m + 1))
                    if l < 4:
                        mm(INV[1][:, c], tit[i % 2][:, m, :], pp[:, m, :], start=True, stop=True)
                    ins = mm(INV[2][:, c], pp[:, m, :], tit[i % 2][:, m, :], start=True, stop=True)
                ins.then_inc(rw["t"], 1)

            def solve(i):
                pe.wait_ge(rw["mvx"], i + 1)
                pe.wait_ge(rw["tt"], 5 * (i + 1))
                if i + 1 < RT:
                    pe.wait_ge(rw["mpm"], 2 * (i + 2))
                for m in range(4):
                    ins = mm(FREE[0][:, 128 * m:128 * (m + 1)], tit[i % 2][:, m, :], xs[i % 2][:, m, :], start=True, stop=True)
                ins.then_inc(rw["tx"], 1)

            def read_out(i):
                pe.wait_ge(rw["txs"], i + 1)
                if i:
                    pe.wait_ge(rw["yout"], i)
                for m in range(4):
                    q, u = m // 2, m % 2
                    ins = mm(FREE[0][R[q], 128 * u:128 * (u + 1)], tx[:, m, 0:64], lp[i % 2][:, m, 1, :], start=True, stop=True)
                ins.then_inc(rw["rp"], 1)
                for u in range(2):
                    for q in range(2):
                        m = 2 * q + u
                        o = FREE[2][R[q], 256 + 128 * u:384 + 128 * u]
                        mm(o, tx[:, m, 64:128], lp[i % 2][:, m, 1, :], start=True, stop=False)
                        mm(o, tok(i, 0, m), mp[i % 2][:, m, 1, :], start=False, stop=True)
                for m in range(4):
                    q, u = m // 2, m % 2
                    for e in range(2):
                        c = 2 * u + e
                        if c in (1, 2):
                            mm(FREE[2 + e][R[q], 64 * u:64 * (u + 1)], tx[R[e], m, 0:64], tok(i, 1, m)[R[e]], start=True, stop=True)
                        if c < 3:
                            o = FREE[2 + e][R[q], 128 + 64 * u:192 + 64 * u]
                            mm(o, tok(i, 1, m)[R[e]], tx[R[e], m, 64:128], start=True, stop=False)
                            ins = mm(o, tok(i, 2, m)[R[e]], tok(i, 0, m)[R[e]], start=False, stop=True)
                ins.then_inc(rw["gz"], 1)

            states = [None, zd[:, 0, :], st2[:, 0, :], st2[:, 1, :]]

            def carry(i, c):
                if c == 0:
                    pe.wait_ge(rw["gzs"], i + 1)
                else:
                    pe.wait_ge(rw["ss2"], 2 * i + 1)
                for q in range(2):
                    ins = mm(FREE[3][R[q], 256 + 64 * c:320 + 64 * c], gi[R[q], c, :], states[c + 1][R[q]], start=True, stop=True)
                ins.then_inc(rw["s"], 1)

            def output(i):
                pe.wait_ge(rw["rps"], i + 1)
                pe.wait_ge(rw["ss2"], 2 * i + 2)
                for c in range(1, 4):
                    for q in range(2):
                        u, e = c // 2, c % 2
                        ins = mm(FREE[2][R[q], CH * c:CH * (c + 1)], states[c][R[q]], rp[R[q], u, 64 * e:64 * e + 64], start=True, stop=True)
                ins.then_inc(rw["y"], 1)

            decay_sums(0)
            to_tokens(0)
            pairs_lp(0, 0)
            pairs_lp(0, 1)
            pairs_mp(0, 0)
            pairs_mp(0, 1)
            pairs_ti(0)
            mix_values(0)
            for i in range(RT + 1):
                inv, post, pre = i < RT, i > 0, i + 1 < RT
                if inv:
                    level_p(i, 0)
                if post:
                    solve(i - 1)
                if inv:
                    level_t(i, 0)
                if pre:
                    decay_sums(i + 1)
                if inv:
                    level_p(i, 1)
                if post:
                    read_out(i - 1)
                if inv:
                    level_t(i, 1)
                if pre:
                    to_tokens(i + 1)
                if inv:
                    level_p(i, 2)
                if post:
                    carry(i - 1, 0)
                if pre:
                    pairs_lp(i + 1, 0)
                if inv:
                    level_t(i, 2)
                if post:
                    carry(i - 1, 1)
                if pre:
                    pairs_lp(i + 1, 1)
                if inv:
                    level_p(i, 3)
                if post:
                    output(i - 1)
                if pre:
                    pairs_mp(i + 1, 0)
                if inv:
                    level_t(i, 3)
                if pre:
                    pairs_mp(i + 1, 1)
                if inv:
                    level_p(i, 4)
                if pre:
                    pairs_ti(i + 1)
                if inv:
                    level_t(i, 4)
                if pre:
                    mix_values(i + 1)
            pe.wait_ge(rw["yout"], RT)
            for b in range(3):
                ins = mm(BANK[b], blk, y_all[:, 2 * b:2 * b + 2, :], start=True, stop=True)
            ins.then_inc(rw["mean"], 1)
            pe.wait_ge(rw["cen"], 1)
            for b in range(3):
                ins = mm(BANK[b], blk, hid[:, 512 * b:512 * (b + 1)], start=True, stop=True)
            ins.then_inc(rw["var"], 1)
            y_split()
            for c in range(4):
                project(FIRST["a_out", 0] + c, NX)
            norm(NX)
            ffn(5, NX)
            pe.wait_ge(bt_in, 16)
            pe.wait_ge(rel_in, 16)
            for g in range(3):
                ins = mm(BANK[1 + g][0:4, :], rel[:, 4 * g:4 * g + 4], bt[:, 512 * g:512 * (g + 1)], start=True, stop=True)
            ins.then_inc(bi_row, 1)
            norm(NX)
            pe.wait_ge(bi_sb, 3)
            project_first(FIRST["kv", 0], NX)
            for c in range(2, 6):
                if c < 3:
                    project(FIRST["kv", 0] + c, NX)
                else:
                    project_tokens(FIRST["kv", 0] + c, NX)
            head_norm(6)
            norm(NX)
            ffn(6, NX)
            mem_kv(1)
            norm(NX)
            project_first(FIRST["b_q", 0], NX)
            for c in range(2, 4):
                project(FIRST["b_q", 0] + c, NX)
            head_norm(6)
            head_norm(2)
            pe.wait_ge(hn_done, st["hn"])
            attend(2)
            attend(3)
            y_split()
            for c in range(2):
                project(FIRST["b_out", 0] + c, NX, rows=4, width=512)
            norm(NX)
            ffn(7, NX)


def kernel(**inputs):
    import concourse.bacc as _bacc
    from concourse.bass_utils import run_bass_kernel_spmd as _run

    a = {k: np.asarray(v) for k, v in inputs.items()}
    arrays = pack(a)
    nc = _bacc.Bacc("TRN2", target_bir_lowering=False, num_devices=1)
    args = [nc.dram_tensor("in_" + k, v.shape, mybir.dt.from_np(v.dtype), kind="ExternalInput").ap() for k, v in arrays.items()]
    out = nc.dram_tensor("out", (128, KT, NX), mybir.dt.float32, kind="ExternalOutput").ap()
    build(nc, *args, out)
    r = _run(nc, [{"in_" + k: v for k, v in arrays.items()}], core_ids=[0])
    return np.ascontiguousarray(np.asarray(r.results[0]["out"]).transpose(2, 1, 0)).reshape(1, NX, D)
```

```python
import math
from contextlib import ExitStack

import numpy as np

import concourse.bass as bass
from concourse import mybir

D = 1024
KT = D // 128
NX = 256
NTOK = 512
DFF = 2816
GROUPS = DFF // 256
CHUNK = 2048
SLOTS = 3
NMOD = 9
POOL_WINDOWS = (2, 4, 8, 16)
DIFF_HEADS = 8
RW = 768
RT = RW // 128
CH = 64
DIL = ((128, 1), (512, 4), (2048, 16))
NUM_BUCKETS, MAX_DISTANCE = 32, 2048
LAM_INIT = 0.8 - 0.6 * math.exp(-0.3)
NEG = -1e30


def vector_columns():
    sizes = [("ada_b", 144), ("norm_g", 48), ("pool_scale", 8), ("final_g", 8), ("ffn_pre_norm_2", 16),
             ("mix_norm_2", 16), ("ffn_post_norm_2", 16), ("mem_norm_2", 16), ("a_shift_mu_2", 20),
             ("a_w0_2", 6), ("a_a0_2", 6), ("a_kk_scale_2", 6), ("a_k_a_2", 6), ("a_r_k_2", 6),
             ("a_lnx_g_2", 6), ("a_lnx_b_2", 6), ("kv_norm_2", 8), ("c", 8), ("c_ctx", 8),
             ("diff_subln_g", 1), ("mem_q_norm_2", 2), ("b_q_norm_2", 1), ("mem_k_norm_2", 2),
             ("kv_k_norm_2", 1)]
    at, col = {}, 0
    for name, n in sizes:
        at[name] = col
        col += n
    return at, col


TWICE = ("mem_q_norm_2", "mem_k_norm_2", "b_q_norm_2", "kv_k_norm_2")


def constants():
    p = np.arange(128)
    half = p // 64
    same = half[:, None] == half[None, :]
    parts = {}
    parts["ident"] = np.eye(128)
    parts["ones"] = np.ones((128, 128))
    parts["blk"] = same.astype(float)
    perm = np.zeros((128, 128))
    for f in range(128):
        perm[f ^ 16, f] = 1.0
    parts["perm"] = perm
    s_, t_ = p[:, None], p[None, :]
    pick = np.zeros((128, 6))
    for c, row in enumerate(ADA_ROWS):
        for v in range(2):
            pick[[row + v, row + 2 + v], 2 * c + v] = 1.0
    parts["pick"] = pick
    parts["eps"] = np.full((128, 1), 1e-6)
    parts["lnx_eps"] = np.full((128, 1), 64e-5)
    t = np.arange(NX)
    inv = 10000.0 ** (-np.arange(0, 32, 2, dtype=np.float32) / np.float32(32))
    f32_ = np.float32
    ang = np.zeros((128, NX), f32_)
    for f in range(128):
        pos = (t // 64) if (f % 64) < 32 else (t % 64)
        ang[f] = pos.astype(f32_) * inv[f % 16].astype(f32_)
    sign = np.where((p % 32) < 16, -1.0, 1.0)[:, None]
    parts["cos"] = np.tile(np.cos(ang), 2)
    parts["sin"] = np.tile(np.sin(ang) * sign, 2)
    parts["cum"] = np.concatenate([same & (s_ <= t_), same & (s_ < t_)], 1).astype(float)
    parts["lp_mask"] = np.concatenate([same & (s_ < t_), same & (s_ <= t_)], 1).astype(float)
    def level(b):
        return ((s_ // (2 * b) == t_ // (2 * b)) & (s_ // b % 2 == 1) & (t_ // b % 2 == 0)).astype(float)
    parts["m1"], parts["m1t"] = level(1), level(1).T
    for b in (2, 4, 8, 16, 32):
        parts[f"m{b}"] = level(b)
    parts["sel"] = np.zeros((128, 32))
    parts["sel"][p, 16 + half] = 1.0
    parts["sel8"] = np.zeros((128, 47))
    parts["sel8"][:, 39] = 1.0
    parts["spread"] = np.zeros((128, 8, 128))
    for i in range(8):
        parts["spread"][2 * i + half, i, p] = 1.0
        parts["spread"][32 + i, i] = 1.0
    parts["spread"] = parts["spread"].reshape(128, 1024)
    parts["ident64"] = np.concatenate([np.eye(64), np.eye(64)], 0)
    at, col, cols = {}, 0, []
    for name, a in parts.items():
        at[name] = col
        col += a.shape[1]
        cols.append(np.asarray(a, f32_))
    return at, np.ascontiguousarray(np.concatenate(cols, 1))


def pool_counts():
    t = np.arange(NX)
    rows = [1.0 / (np.clip(t - w // 2 + w - 1, 0, NX - 1) - np.clip(t - w // 2, 0, NX - 1) + 1) for w in POOL_WINDOWS]
    return np.ascontiguousarray(np.broadcast_to(np.concatenate([np.tile(r, 4) for r in rows]).astype(np.float32), (128, 16 * NX)))


def bias_tables():
    u = np.arange(512)
    dist = u - 255
    exact = NUM_BUCKETS // 2
    large = exact + (np.log(np.maximum(dist, 1).astype(np.float32) / exact) / math.log(MAX_DISTANCE / exact)
                     * (NUM_BUCKETS - exact)).astype(np.int32)
    bucket = np.where(dist < exact, dist, np.minimum(large, NUM_BUCKETS - 1))
    hot = np.zeros((32, 3, 512), np.float32)
    add = np.zeros((32, 3, 512), np.float32)
    for g, (window, dil) in enumerate(DIL):
        ok = (dist >= 0) & (dist % dil == 0) & (dist <= window)
        for k in range(512):
            if ok[k]:
                hot[bucket[k], g, k] = 1.0
        add[:, g] = np.where(ok, 0.0, NEG)
    return np.ascontiguousarray(np.concatenate([hot.reshape(32, -1), add.reshape(32, -1)], 1))


ADA_ROWS = (32, 64, 0)

FFN_PASS = [0, 0, KT]
FFN_ADA_PASS = [0, 1, 0, 1, KT, 2]
FFN_TILES = [0, 0] + FFN_PASS * (GROUPS - 1) + [KT]
FFN_ADA_TILES = [0, 0] + FFN_ADA_PASS * (GROUPS - 1) + [KT]
ADA_FIRST = 12
ADA_FFN = 3 * (GROUPS - 1)
ADA_PARTS = [(0, ADA_FIRST), (ADA_FIRST, ADA_FIRST + ADA_FFN), (ADA_FIRST + ADA_FFN, ADA_FIRST + 2 * ADA_FFN)]
assert ADA_PARTS[-1][1] == 2 * NMOD * D // 256
STREAM = [("ada", 0, [1] * ADA_FIRST), ("ffn", 0, FFN_ADA_TILES), ("pool", 0, [8]), ("ffn", 1, FFN_ADA_TILES),
          ("ffn", 2, FFN_TILES), ("qkv", 0, [2] * 8 + [4] * 4), ("wo", 0, [2] * 4),
          ("ffn", 3, FFN_TILES), ("ffn", 4, FFN_TILES), ("a_in", 0, [2] * 11), ("memkv", 0, [2] * 2),
          ("a_out", 0, [2] * 4), ("ffn", 5, FFN_TILES), ("kv", 0, [2] * 6), ("ffn", 6, FFN_TILES),
          ("b_q", 0, [2] * 4), ("memkv", 1, [2] * 2), ("b_out", 0, [4] * 2), ("ffn", 7, FFN_TILES)]
FIRST = {}
TILE0 = []
DONE = []
for _kind, _i, _tiles in STREAM:
    FIRST[_kind, _i] = len(DONE)
    for _t in _tiles:
        TILE0.append(TILE0[-1] + _last if TILE0 else 0)
        DONE.append((DONE[-1] if DONE else 0) + max(_t, 1))
        _last = _t
FIRST_AFTER = {key: FIRST[key] + len(t) for key, t in (((k, i), t) for k, i, t in STREAM)}
TOTAL = len(DONE)
PADDED = TOTAL + SLOTS
assert PADDED % SLOTS == 0
BANKS = 4


def freed(tiles):
    return BANKS + tiles


def pack(a):
    def cols(w, width=256):
        return [w[:, c:c + width].reshape(-1, 128, width).transpose(1, 0, 2) for c in range(0, w.shape[1], width)]

    def ffn(w_in, w_out):
        gate, up = cols(w_in[:, :DFF]), cols(w_in[:, DFF:])
        down = [w_out[r:r + 256].reshape(2, 128, D).transpose(1, 0, 2) for r in range(0, DFF, 256)]
        return gate, up, down

    def ffn_order(gate, up, down, ada):
        order = [gate[0], up[0]]
        for i in range(1, GROUPS):
            these = [gate[i], up[i], down[i - 1]]
            for j, c in enumerate(these):
                order += [c] + ([ada[3 * (i - 1) + j]] if ada else [])
        return order + [down[-1]]

    chunks = []
    ada = cols(a["ada_w"][0]) + cols(a["ada_w"][1])
    f1 = [ffn(a["ffn_w_in"][l, s], a["ffn_w_out"][l, s]) for l in range(2) for s in range(2)]
    f2 = [ffn(a[f"ffn_{s}_w_in_2"][l], a[f"ffn_{s}_w_out_2"][l]) for l in range(2) for s in ("pre", "post")]
    for kind, i, _ in STREAM:
        if kind == "ada":
            chunks += ada[:ADA_FIRST]
        elif kind == "ffn":
            chunks += ffn_order(*(f1 + f2)[i], ada[slice(*ADA_PARTS[i + 1])] if i < 2 else None)
        elif kind == "pool":
            chunks.append(a["pool_w"][0].reshape(4, 2, 128, 256).transpose(2, 0, 1, 3))
        elif kind == "memkv":
            chunks += cols(a["mem_w_kv_2"][i])
        elif kind == "b_out":
            chunks += cols(a["b_w_out_2"][0], 512)
        else:
            name = {"qkv": "diff_w_qkv", "wo": "diff_w_o", "a_in": "a_w_in_2", "a_out": "a_w_out_2", "b_q": "b_w_q_2"}.get(kind)
            chunks += cols(a[name][0] if name else a["kv_w_2"])
    w = np.zeros((PADDED, 128, CHUNK), np.float32)
    for n, c in enumerate(chunks):
        w[n] = c.reshape(128, CHUNK)
    at, n = vector_columns()
    vec = np.zeros((128, n), np.float32)
    for name, col in at.items():
        v = a[name].reshape(-1, 64) if name in TWICE else a[name].reshape(-1, 128)
        if name in TWICE:
            v = np.concatenate([v, v], 1)
        vec[:, col:col + len(v)] = v.T

    def fm(v):
        return v.T.reshape(KT, 128, -1).transpose(1, 0, 2)

    arrays = dict(
        W=w.reshape(PADDED * 128, CHUNK),
        XT=np.concatenate([fm(a["x"][0]), fm(a["ctx"][0])], 2), MEMT=fm(a["mem_2"][0]),
        VEC=vec, CST=constants()[1], ICNT=pool_counts(), BT=bias_tables(), REL=a["rel_bias_2"],
        LAM=np.broadcast_to(a["diff_lam"][0].reshape(1, 256), (128, 256)),
        W0B=np.broadcast_to(a["a_w0_2"][0].reshape(1, RW), (128, RW)),
        LORA=np.concatenate([a["a_w_up_2"][0], a["a_a_up_2"][0]], 0), GUP=a["a_g_up_2"][0])
    return {k: np.ascontiguousarray(v) for k, v in arrays.items()}




def build(nc, W, XT, MEMT, VEC, CST, ICNT, BT, REL, LAM, W0B, LORA, GUP, OUT, stop=None):
    f32, f32r = mybir.dt.float32, mybir.dt.float32r
    ACT, ALU, AX = mybir.ActivationFunctionType, mybir.AluOpType, mybir.AxisListType
    add, sub, mult, amax = ALU.add, ALU.subtract, ALU.mult, ALU.max
    vat, nvec = vector_columns()
    cat, _ = constants()
    ncst = CST.shape[1]
    ds = bass.ds
    def ffn_pass(f):
        tiles = FFN_ADA_PASS if f < 2 else FFN_PASS
        n0 = FIRST["ffn", f]
        n = len(tiles)
        gap = n // 3
        ada = [n0 + 2 + gap * j + 1 for j in range(3)] if f < 2 else []
        return n, sum(max(t, 1) for t in tiles), sum(tiles), n0 + 2 + gap, n0 + 2 + 2 * gap, ada, n0 + 2 + n * (GROUPS - 1)


    with ExitStack() as ctx:
        def sb(name, shape, dt=f32):
            return ctx.enter_context(nc.sbuf_tensor(name, shape, dt))

        def sem(name):
            return ctx.enter_context(nc.semaphore(name))

        wraw = sb("wraw", [128, SLOTS, CHUNK])
        whi = sb("whi", [128, SLOTS, CHUNK], f32r)
        wlo = sb("wlo", [128, SLOTS, CHUNK], f32r)
        x = sb("x", [128, KT, NTOK])
        tsq = sb("tsq", [128, KT * NTOK])
        vec = sb("vec", [128, nvec])
        cst = sb("cst", [128, ncst])
        mods = sb("mods", [128, 2, 72, 2])
        sc = sb("sc", [128, 2 * KT])
        cs = sb("cs", [128, KT, 4], f32r)
        acol = sb("acol", [128, 2, 3, KT, 2])
        gcol = sb("gcol", [128, 2, 3, KT, 2])
        rstd = sb("rstd", [128, NTOK])
        lamb = sb("lamb", [128, 256])
        cols = sb("cols", [128, 64])
        with nc.sbuf_tensor("hh", [128, KT, NTOK], f32r) as hh, nc.sbuf_tensor("hl", [128, KT, NTOK], f32r) as hl:
            pass
        big = sb("big", [128, 2 * KT * NTOK])
        with nc.sbuf_tensor("ah", [128, 2, NTOK], f32r) as ah, nc.sbuf_tensor("al", [128, 2, NTOK], f32r) as al:
            pass
        hid = sb("hid", [128, 4 * NTOK])
        scr = sb("scr", [128, 10240])
        ps_g = ctx.enter_context(nc.psum_tensor("ps_g", [128, 2, 512], f32))
        ps_u = ctx.enter_context(nc.psum_tensor("ps_u", [128, 2, 512], f32))
        ps_o = ctx.enter_context(nc.psum_tensor("ps_o", [128, 4, 512], f32))
        bias_rows = nc.dram_tensor("bias_rows", [3 * 4 * 512], f32, kind="Internal")

        def V(name, i=0, n=1):
            return vec[:, vat[name] + i:vat[name] + i + n]

        def C(name, n=128):
            return cst[:, cat[name]:cat[name] + n]

        ident, ones, blk = C("ident"), C("ones"), C("blk")
        BANK = [ps_g[:, 0, :], ps_g[:, 1, :], ps_u[:, 0, :], ps_u[:, 1, :]]
        HALVES = (slice(0, NX), slice(NX, NTOK))

        w_here = [sem(f"w_here{s}") for s in range(SLOTS)]
        w_hi, w_lo = sem("w_hi"), sem("w_lo")
        mm_done = sem("mm_done")
        o_free = sem("o_free")
        c_in, c_late, x_in, m_in, ic_in, bt_in, rel_in, lora_in, lam_in = (sem(s) for s in (
            "c_in", "c_late", "x_in", "m_in", "ic_in", "bt_in", "rel_in", "lora_in", "lam_in"))
        nm_sq, nm_sum, nm_std, nm_rstd = sem("nm_sq"), sem("nm_sum"), sem("nm_std"), sem("nm_rstd")
        nm_t, nm_hi, h_ready = sem("nm_t"), sem("nm_hi"), sem("h_ready")
        g_act, u_mul, a_hi, a_ready = sem("g_act"), sem("u_mul"), sem("a_hi"), sem("a_ready")
        ad_silu, ad_hi, ad_lo, ad_zero, ad_turn, ad_col = (sem(n) for n in ("ad_silu", "ad_hi", "ad_lo", "ad_zero", "ad_turn", "ad_col"))
        act_seq, dve_seq = sem("act_seq"), sem("dve_seq")
        y_hi, y_ready = sem("y_hi"), sem("y_ready")
        pl_diff, pl_gp, pool_seq = sem("pl_diff"), sem("pl_gp"), sem("pool_seq")
        lam_sum, lam_exp = sem("lam_sum"), sem("lam_exp")
        ro_mm, ro_sin, ro_done = sem("ro_mm"), sem("ro_sin"), sem("ro_done")
        sl_sq, sl_sum, sl_std, sl_inv, sl_back, sl_y = (sem(n) for n in ("sl_sq", "sl_sum", "sl_std", "sl_inv", "sl_back", "sl_y"))
        hn_sq, hn_sum, hn_std, hn_inv, hn_back, hn_done = (sem(n) for n in ("hn_sq", "hn_sum", "hn_std", "hn_inv", "hn_back", "hn_done"))
        at_s, at_m, at_e, at_p = sem("at_s"), sem("at_m"), sem("at_e"), sem("at_p")
        at_b = [sem(f"at_b{i}") for i in range(4)]
        at_t, at_c, at_o, at_y = sem("at_t"), sem("at_c"), sem("at_o"), sem("at_y")
        bi_row, bi_sb, bi_dram = sem("bi_row"), sem("bi_sb"), sem("bi_dram")
        rw = {n: sem("rw_" + n) for n in (
            "move", "shift", "lora", "z", "zb", "zs", "a_mm", "a_act", "a_free", "g_mm", "g_act", "sq", "ss", "std", "inv", "back", "kk", "bsq", "bsum", "bon",
            "cum", "dec", "feat", "tp", "tm", "lp", "lmask", "p", "pm", "t", "ti", "tt", "tit", "mv", "mvx", "tx", "txs", "rp", "rps",
            "lpm", "mp", "mpm", "tib", "gz", "gzs", "s", "ss2", "y", "y_in", "yout", "mean", "cen", "var", "vstd", "vinv", "vback", "fin")}
        out_done = sem("out_done")
        block = ctx.enter_context(nc.Block())

        def cut(tensor, first, count, pattern=None, **kw):
            v = tensor[:, first:first + count]
            return v.rearrange(pattern, **kw) if pattern else v

        quad = "p (a s u) -> p a s u"
        pads = {"vector": [cut(scr, i * 1088, 1088, quad, a=2, s=2) for i in range(3)],
                "gpsimd": [cut(t, at, 1088, quad, a=2, s=2) for t, at in ((hid, 0), (scr, 7360), (scr, 8448))]}
        icnt = cut(scr, 3 * 1088, 16 * NX)
        q_d = cut(scr, 0, 2048, "p (h n) -> p h n", h=8)
        k_d = cut(scr, 2048, 4096, "p (h n) -> p h n", h=8)
        v_d = cut(scr, 6144, 4096, "p (t n) -> p t n", t=4)
        ada_rows = scr[0:96, 0:256 * (GROUPS - 1)]
        ROWS = [slice(row, row + 4) for row in ADA_ROWS]
        y_all = cut(tsq, 0, 2048, "p (k n) -> p k n", n=NX)
        probs = [cut(tsq, 2048 + 1024 * i, 1024) for i in range(2)]
        probs_t = [[cut(big, 768 * i, 768, "p (b n) -> p b n", n=128) for i in range(2)]] * 4
        probs_t[1] = [cut(tsq, 256 * i, 256, "p (b n) -> p b n", n=128) for i in range(2)]
        mem_x = x[:, :, NX:NTOK]
        mem_k = cut(scr, 2048, 512, "p (k n) -> p k n", n=NX)
        mem_v = cut(scr, 2560, 512, "p (t n) -> p t n", n=256)
        proj = cut(scr, 3072, 20 * 257, "p (i n) -> p i n", n=257)
        mem_q = {0: cut(scr, 8212, 512, "p (k n) -> p k n", n=NX), 1: cut(scr, 7680, 512, "p (k n) -> p k n", n=NX)}
        r_, k_, v_ = proj[:, 0:6, 1:257], proj[:, 6:12, 1:257], proj[:, 12:18, 1:257]
        moved = cut(tsq, 0, 8 * NX, "p (i n) -> p i n", n=NX)
        zs = cut(big, 0, 2 * RW, "p (u n) -> p u n", n=RW)
        aa = cut(big, 1536, 1536, "p (i n) -> p i n", n=NX)
        kk = cut(big, 3072, 1536, "p (i n) -> p i n", n=NX)
        gg = cut(big, 4608, 1536, "p (i n) -> p i n", n=NX)
        bon = cut(big, 6144, 1536, "p (i n) -> p i n", n=NX)
        lora = cut(scr, 0, RW)
        gup = cut(scr, RW, RW)
        w0b = cut(hid, 1280, RW)
        dec = cut(scr, 8724, 768, "p (e n) -> p e n", n=NX)
        dinc, dexc, dinv = dec[:, 0, :], dec[:, 1, :], dec[:, 2, :]
        gi = cut(scr, 9492, 128, "p (c n) -> p c n", n=64)
        zd = cut(scr, 9620, 192, "p (c n) -> p c n", n=64)
        xc = x[:, :, NX:NTOK]
        tmaj = [cut(tsq, 2048, 768, "p (e u n) -> p e u n", e=3, u=2), xc[:, 0:3, :].rearrange("p e (u n) -> p e u n", u=2)]
        lp = [cut(tsq, 3072, 1024, "p (m e n) -> p m e n", m=4, e=2), xc[:, 4:8, :].rearrange("p m (e n) -> p m e n", e=2)]
        mp = [cut(scr, 0, 1024, "p (m e n) -> p m e n", m=4, e=2),
              cst[:, cat["cos"]:cat["cos"] + 1024].rearrange("p (m e n) -> p m e n", m=4, e=2)]
        xs = [cut(scr, 1024 + 1024 * j, 512, "p (m n) -> p m n", m=4) for j in range(2)]
        tx = cut(scr, 1536, 512, "p (m n) -> p m n", m=4)
        ti = cut(big, 7680, 512, "p (m n) -> p m n", m=4)
        tit = [cut(hid, 0, 512, "p (m n) -> p m n", m=4), cut(scr, 8212, 512, "p (m n) -> p m n", m=4)]
        pp = cut(hid, 512, 512, "p (m n) -> p m n", m=4)
        ar = [cut(t, at, 512, "p (u e n) -> p u e n", u=2, e=2) for t, at in ((hid, 1024), (scr, 2560))]
        ends = cols[:, 24:36].rearrange("p (j c) -> p j c", j=3)
        INV, FREE = [ps_o[:, b, :] for b in range(3)], [ps_o[:, 3, :], ps_g[:, 0, :], ps_u[:, 0, :], ps_u[:, 1, :], ps_g[:, 1, :]]
        be = cut(hid, 1536, 256, "p (u n) -> p u n", u=2)
        ka = cut(hid, 1792, 256, "p (u n) -> p u n", u=2)
        rp = cut(rstd, 0, 256, "p (u n) -> p u n", u=2)
        st2 = cut(rstd, 256, 128, "p (c n) -> p c n", n=64)
        k_g = cut(scr, 3072, 1536, "p (k n) -> p k n", n=NX)
        v_g = cut(scr, 4608, 1536, "p (t n) -> p t n", n=RW)
        q_g = cut(scr, 6144, 1536, "p (k n) -> p k n", n=NX)
        bias = [cut(scr, at, 768, "p (g n) -> p g n", g=3) for at in (8192, 8960, 0, 768)]
        NB = len(bias)
        bt = scr[0:32, 0:3072]
        rowb = scr[0:4, 3072:4608]
        rel = cols[0:32, 40:52]
        head_rows, subln_rows = lamb[0:16, 0:NX], lamb[32:40, 0:NX]
        lam_col, subln_gain = cols[:, 52:53], cols[:, 62:63]
        qgain = cols[:, 53:56]

        def over(v, n):
            return v.unsqueeze(1).broadcast_to([v.shape[0], n] + list(v.shape[1:]))

        def pool_edges(ops, pad):
            ops.memset(pad[0][:, :, :, 0:8], 0.0)
            return ops.memset(pad[0][:, :, :, 264:272], 0.0)

        def pool_group(ops, link, pad, g):
            h4 = tsq[:, 1024 * g:1024 * (g + 1)].rearrange("p (a s n) -> p a s n", a=2, s=2)
            link(ops.tensor_copy(pad[0][:, :, :, 8:264], h4))
            link(ops.tensor_tensor(pad[1][:, :, :, 1:272], pad[0][:, :, :, 0:271], pad[0][:, :, :, 1:272], add))
            cur, lo = 1, 1
            for e in range(g):
                b, nxt = 1 << e, 3 - cur
                lo2, hi2 = lo + b, 272 - (2 * b - 1)
                link(ops.tensor_tensor(pad[nxt][:, :, :, lo2:hi2], pad[cur][:, :, :, lo2 - b:hi2 - b], pad[cur][:, :, :, lo2 + b:hi2 + b], add))
                cur, lo = nxt, lo2
            mean = pad[3 - cur][:, :, :, 8:264]
            link(ops.tensor_tensor(mean, pad[cur][:, :, :, 8:264], icnt[:, g * 1024:(g + 1) * 1024].rearrange(quad, a=2, s=2), mult))
            return ops.tensor_tensor(h4, mean, h4, sub)

        two = lambda v: v.rearrange("p (u n) -> p u n", u=2)
        HEADS = lambda h: (h // 2, slice(64 * (h % 2), 64 * (h % 2) + 64))

        def att_diff(g0):
            units = []
            for h in range(DIFF_HEADS):
                for tt in range(2):
                    t = slice(tt * 128, (tt + 1) * 128)
                    units.append(dict(
                        scores=[((slice(0, 128), j, slice(0, 512)), q_d[64 * j:64 * j + 64, h, t], k_d[64 * j:64 * j + 64, h, :])
                                for j in range(2)], width=512, subs=2, nb=4, rows=slice(0, 128),
                        v=[v_d[:, b, h * 128:(h + 1) * 128] for b in range(4)], y=y_all[:, h, t], bias=None))
            return units

        def att_mem(l):
            units = []
            for h in range(4):
                k, r = HEADS(h)
                for tt in range(2):
                    t = slice(tt * 128, (tt + 1) * 128)
                    units.append(dict(
                        scores=[((slice(0, 128), 0, slice(0, 256)), mem_q[l][r, k, t], mem_k[r, k, :])], width=256, subs=1, nb=2,
                        rows=r, v=[mem_v[:, b, h * 64:(h + 1) * 64] for b in range(2)],
                        y=y_all[r, (6 if l == 0 else 2) + k, t], bias=None))
            return units

        def att_dil():
            units = []
            for j in range(4):
                for tt in range(2):
                    t = slice(tt * 128, (tt + 1) * 128)
                    sc_, v = [], []
                    for g in range(3):
                        k, r = HEADS(4 * g + j)
                        sc_.append(((slice(0, 128), g // 2, slice(256 * (g % 2), 256 * (g % 2) + 256)), q_g[r, k, t], k_g[r, k, :]))
                        v += [v_g[:, b, (4 * g + j) * 64:(4 * g + j + 1) * 64] for b in range(2)]
                    k, r = HEADS(j)
                    units.append(dict(scores=sc_, width=768, subs=1, nb=6, rows=r, v=v, y=y_all[r, k, t], bias=(j, tt)))
            return units

        BIASED = len(att_dil())
        ATT = [att_diff(0), att_mem(0), att_dil() + att_mem(1)]
        AT0 = [sum(len(a) for a in ATT[:i]) for i in range(4)]
        DIL0 = AT0[2]

        @block.sync
        def _(sp):
            sp.dma_start(vec[:], VEC).then_inc(c_in, 16)
            for s in range(SLOTS):
                sp.dma_start(wraw[:, s, :], W[s * 128:(s + 1) * 128, :]).then_inc(w_here[s], 16)
                if s == 0:
                    sp.dma_start(cst[:, 0:cat["cos"]], CST[:, 0:cat["cos"]]).then_inc(c_in, 16)
            with sp.Fori(1, PADDED // SLOTS) as i:
                for s in range(SLOTS):
                    sp.wait_ge(w_lo, i * SLOTS + (s + 1 - SLOTS))
                    sp.dma_start(wraw[:, s, :], W[ds(i * (SLOTS * 128) + s * 128, 128), :]).then_inc(w_here[s], 16)
            sp.wait_ge(o_free, freed(TILE0[-1] + KT))
            sp.dma_start(OUT, x[:, :, 0:NX]).then_inc(out_done, 16)
            sp.wait_ge(out_done, 16)

        @block.gpsimd
        def _(pool):
            pool.dma_start(x[:], XT).then_inc(x_in, 16)
            nc.gpsimd.memset(ada_rows, 0.0).then_inc(ad_zero, 1)
            pool.dma_start(lamb[:], LAM).then_inc(lam_in, 16)
            pool.dma_start(rel, REL).then_inc(rel_in, 16)
            pool.wait_ge(ad_turn, 1)
            pool.dma_start(icnt, ICNT).then_inc(ic_in, 16)
            pool.dma_start(cst[:, cat["cos"]:ncst], CST[:, cat["cos"]:ncst]).then_inc(c_late, 16)
            seq = [0]

            def link(ins):
                seq[0] += 1
                ins.then_inc(pool_seq, 1)
                pool.wait_ge(pool_seq, seq[0])

            pool.wait_ge(o_free, freed(TILE0[FIRST["pool", 0]]))
            link(pool_edges(nc.gpsimd, pads["gpsimd"]))
            pool.wait_ge(ic_in, 16)
            pool.wait_ge(nm_hi, 2 * KT + 4 * 3)
            pool_group(nc.gpsimd, link, pads["gpsimd"], 2).then_inc(pl_gp, 1)
            pool.wait_ge(y_hi, 4)
            nc.gpsimd.memset(ada_rows, 0.0).then_inc(ad_zero, 1)
            pool.wait_ge(mm_done, DONE[FIRST["qkv", 0]])
            pool.dma_start(mem_x, MEMT).then_inc(m_in, 16)
            pool.wait_ge(o_free, freed(TILE0[FIRST["ffn", 3]]))
            pool.dma_start(lora, LORA).then_inc(lora_in, 16)
            pool.dma_start(gup, GUP).then_inc(lora_in, 16)
            pool.wait_ge(mm_done, DONE[FIRST["a_in", 0] - 1])
            pool.dma_start(w0b, W0B).then_inc(lora_in, 16)
            pool.wait_ge(o_free, freed(TILE0[FIRST["ffn", 5]]))
            pool.dma_start(bt, BT).then_inc(bt_in, 16)
            pool.wait_ge(bi_sb, 3)
            pool.dma_start(bass.AP(bias_rows, 0, [[512, 4], [2048, 3], [1, 512]]), rowb.rearrange("p (g n) -> p g n", g=3)).then_inc(bi_dram, 16)
            pool.wait_ge(bi_dram, 16)
            pool.dma_start(mem_x, MEMT).then_inc(m_in, 16)
            for u, unit in enumerate(ATT[2][:BIASED]):
                j, tt = unit["bias"]
                if u >= NB:
                    pool.wait_ge(at_m, DIL0 + u - NB + 1)
                pool.dma_start(bias[u % NB], bass.AP(bias_rows, j * 512 + tt * 128, [[1, 128], [2048, 3], [1, 256]])).then_inc(at_b[u % NB], 16)
            for slot in at_b:
                pool.wait_ge(slot, 16 * (BIASED // NB))

        @block.scalar
        def _(act):
            st = {"seq": 0, "k": 0, "t": 0, "h": 0, "hn": 0, "y": 0, "late": []}

            def link(ins):
                st["seq"] += 1
                ins.then_inc(act_seq, 1)
                act.wait_ge(act_seq, st["seq"])

            def split_hi(n, i=None, step=1, per=SLOTS):
                if n >= PADDED:
                    return
                off = 0 if i is None else i
                act.wait_ge(w_here[n % SLOTS], off * (16 * per // SLOTS) + 16 * (n // SLOTS + 1))
                if n >= SLOTS:
                    act.wait_ge(mm_done, off * step + DONE[n - SLOTS])
                nc.scalar.activation(whi[:, n % SLOTS, :], wraw[:, n % SLOTS, :], ACT.Copy).then_inc(w_hi, 1)

            def square(src, N, ready, d):
                ready(act, d)
                nc.scalar.activation(tsq[:, d * NTOK:d * NTOK + N], src(d)[:, 0:N], ACT.Square).then_inc(nm_sq, 1)

            def norm(src, N, B, mode, ready, n, part=None, squared=False, again=False):
                k = st["k"]
                st["k"] += not again
                if st["h"]:
                    act.wait_ge(h_ready, st["h"])
                if not again:
                    nc.scalar.activation(cols[:, 61:62], C("eps", 1), ACT.Sqrt)
                    for d in range(0 if not squared else KT, KT):
                        square(src, N, ready, d)
                    act.wait_ge(nm_sum, k + 1)
                    nc.scalar.activation(rstd[:, 0:N], ps_g[:, 0, 0:N], ACT.Sqrt, bias=C("eps", 1), scale=1.0 / D).then_inc(nm_std, 1)
                if n and mode == "split":
                    act.wait_ge(mm_done, DONE[n - 1])
                if part is not None:
                    act.wait_ge(ad_col, part + 1)
                for d in range(KT):
                    for j in range(N // NX):
                        st["t"] += 1
                        if mode == "final":
                            continue
                        act.wait_ge(nm_t, st["t"])
                        src_t = tsq[:, d * NTOK + j * NX:d * NTOK + (j + 1) * NX]
                        dst = src_t if mode == "plain" else hh[:, d, HALVES[j]]
                        if B is None:
                            nc.scalar.activation(dst, src_t, ACT.Copy).then_inc(nm_hi, 1)
                        else:
                            nc.scalar.activation(dst, src_t, ACT.Identity, bias=B(d, j)).then_inc(nm_hi, 1)
                        st["h"] += mode == "split"
                while st["late"]:
                    split_hi(st["late"].pop())

            def after(n):
                return lambda eng, d: eng.wait_ge(o_free, freed(TILE0[n] - KT + d + 1))

            def with_memory(n, loads):
                def ready(eng, d):
                    after(n)(eng, d)
                    eng.wait_ge(m_in, 16 * loads)
                return ready

            def ffn(f, N):
                n0, g0 = FIRST["ffn", f], f * GROUPS
                sg = tsq[:, 0:1024].rearrange("p (j n) -> p j n", j=2)
                tmp = tsq[:, 1024:2048].rearrange("p (j n) -> p j n", j=2)

                def silu(done, group):
                    act.wait_ge(mm_done, done)
                    if group is not None:
                        act.wait_ge(u_mul, group)
                    nc.scalar.activation(sg[:, :, 0:N], ps_g[:, :, 0:N], ACT.Silu).then_inc(g_act, 1)

                def hidden(group):
                    act.wait_ge(u_mul, group + 1)
                    nc.scalar.activation(ah[:, :, 0:N], tmp[:, :, 0:N], ACT.Copy).then_inc(a_hi, 1)

                per, step, _, _, n_down, _, n_last = ffn_pass(f)
                silu(DONE[n0], g0 or None)
                split_hi(n0 + 3)
                split_hi(n0 + 4)
                hidden(g0)
                with act.Fori(0, GROUPS - 1) as i:
                    split_hi(n0 + 5, i, step, per)
                    silu(i * step + DONE[n0 + 2], i + (g0 + 1))
                    for n in range(n0 + 6, n0 + 5 + per):
                        if n - SLOTS == n_down:
                            act.wait_ge(mm_done, i * step + DONE[n_down])
                            hidden(i + (g0 + 1))
                        split_hi(n, i, step, per)
                st["late"].append(n_last + SLOTS)
                act.wait_ge(a_ready, g0 + GROUPS)

            def chunks(stage, i, late=0):
                for n in range(FIRST[stage, i], FIRST_AFTER[stage, i] - late):
                    split_hi(n + SLOTS)
                st["late"] = list(range(FIRST_AFTER[stage, i] - late + SLOTS, FIRST_AFTER[stage, i] + SLOTS))[::-1]

            def mod(l, a):
                return lambda d, j: mods[:, l, 24 * a + d, j:j + 1]

            def head_norm():
                st["hn"] += 1
                act.wait_ge(hn_sum, st["hn"])
                nc.scalar.activation(head_rows, BANK[3][0:16, 0:NX], ACT.Sqrt, bias=C("eps", 1)[0:16], scale=1.0 / 64).then_inc(hn_std, 1)

            def split_y(src, nt, width=NX):
                nc.scalar.activation(hh[:, 0:nt, 0:width], src, ACT.Copy).then_inc(y_hi, 1)

            def attend(a):
                U = ATT[a]

                def copy(u):
                    g = AT0[a] + u
                    act.wait_ge(at_t, g + 1)
                    if g >= 2:
                        act.wait_ge(at_o, g - 1)
                    nb = U[u]["nb"]
                    for b in range(0, nb, 4):
                        w = min(4, nb - b)
                        ins = nc.scalar.activation(probs_t[a][g % 2][:, b:b + w, :], ps_o[:, b // 4, 0:w * 128].rearrange("p (b n) -> p b n", n=128), ACT.Copy)
                    ins.then_inc(at_c, 1)

                for u, unit in enumerate(U):
                    g = AT0[a] + u
                    act.wait_ge(at_m, g + 1)
                    if g >= 2:
                        act.wait_ge(at_t, g - 1)
                    bank = ps_g if g % 2 == 0 else ps_u
                    w = unit["width"]
                    for j in range(unit["subs"]):
                        src = bank[:, j, 0:w] if unit["bias"] is None else probs[g % 2][:, 0:w]
                        ins = nc.scalar.activation(probs[g % 2][:, j * w:(j + 1) * w], src, ACT.Exp, bias=cols[:, 4 * (g % 2) + j:4 * (g % 2) + j + 1],
                                                   accum_out=cols[:, 8 + 4 * (g % 2) + j:9 + 4 * (g % 2) + j])
                    ins.then_inc(at_e, 1)
                    if u:
                        copy(u - 1)
                copy(len(U) - 1)

            act.wait_ge(c_in, 32)
            x_here = lambda eng, d: eng.wait_ge(x_in, 16)
            nc.scalar.activation(sc[:], V("c", 0, 16), ACT.Silu).then_inc(ad_silu, 1)
            act.wait_ge(ad_silu, 1)
            nc.scalar.activation(cs[:, :, 0:2], sc[:].rearrange("p (v k) -> p k v", v=2), ACT.Copy).then_inc(ad_hi, 1)
            for n in range(SLOTS):
                split_hi(n)
            for n in range(ADA_FIRST):
                split_hi(n + SLOTS)
                if 2 <= n < 2 + KT:
                    square(lambda d: x[:, d, :], NTOK, x_here, n - 2)
            norm(lambda d: x[:, d, :], NTOK, mod(0, 0), "split", x_here, FIRST["ffn", 0], part=0, squared=True)
            ffn(0, NTOK)
            norm(lambda d: x[:, d, :], NTOK, mod(0, 1), "plain", after(FIRST["pool", 0]), FIRST["pool", 0], part=1)
            for g in range(4):
                if g == 2:
                    act.wait_ge(pl_gp, 1)
                else:
                    act.wait_ge(pl_diff, min(g + 1, 3))
                nc.scalar.activation(hh[:, 2 * g:2 * g + 2, :], tsq[:, 1024 * g:1024 * (g + 1)].rearrange("p (a n) -> p a n", a=2), ACT.Copy).then_inc(y_hi, 1)
            chunks("pool", 0, late=1)
            norm(lambda d: x[:, d, :], NTOK, mod(0, 2), "split", after(FIRST["ffn", 1]), FIRST["ffn", 1])
            ffn(1, NTOK)
            norm(lambda d: x[:, d, :], NTOK, mod(1, 0), "split", after(FIRST["ffn", 2]), FIRST["ffn", 2], part=2)
            ffn(2, NTOK)
            norm(lambda d: x[:, d, :], NTOK, mod(1, 1), "split", after(FIRST["qkv", 0]), FIRST["qkv", 0])
            chunks("qkv", 0)
            act.wait_ge(lam_sum, 1)
            nc.scalar.activation(cols[:, 58:60], cols[:, 56:58], ACT.Exp).then_inc(lam_exp, 1)
            attend(0)
            act.wait_ge(sl_sum, 1)
            nc.scalar.activation(subln_rows, ps_o[32:40, 0, 0:NX], ACT.Sqrt, bias=C("eps", 1)[32:40], scale=1.0 / 128).then_inc(sl_std, 1)
            for b in range(4):
                act.wait_ge(sl_y, b + 1)
                nc.scalar.activation(hh[:, 2 * b:2 * b + 2, 0:NX], y_all[:, 2 * b:2 * b + 2, :], ACT.Copy).then_inc(y_hi, 1)
            chunks("wo", 0, late=1)
            norm(lambda d: x[:, d, :], NX, mod(1, 2), "split", after(FIRST["ffn", 3]), FIRST["ffn", 3])
            ffn(3, NX)
            norm(lambda d: x[:, d, :], NX, None, "final", after(FIRST["ffn", 4]), FIRST["ffn", 4])
            t_final = st["t"]
            norm(lambda d: x[:, d, :], NX, None, "split", lambda eng, d: eng.wait_ge(nm_t, t_final), FIRST["ffn", 4])
            ffn(4, NX)
            norm(lambda d: x[:, d, :], NTOK, None, "split", with_memory(FIRST["a_in", 0], 1), FIRST["a_in", 0])
            chunks("a_in", 0)
            chunks("memkv", 0)
            act.wait_ge(rw["shift"], 20)
            nc.scalar.activation(proj[0:64, 18, 1:257], proj[0:64, 18, 1:257], ACT.Tanh)
            nc.scalar.activation(proj[:, 19, 1:257], proj[:, 19, 1:257], ACT.Sigmoid).then_inc(rw["lora"], 1)
            act.wait_ge(rw["zb"], 1)
            nc.scalar.activation(zs, zs, ACT.Sigmoid).then_inc(rw["zs"], 1)
            for i in range(RT):
                act.wait_ge(rw["a_mm"], i + 1)
                nc.scalar.activation(aa[:, i, :], ps_o[:, i % 2, 0:NX], ACT.Sigmoid, bias=V("a_a0_2", i)).then_inc(rw["a_act"], 1)
            for i in range(RT):
                act.wait_ge(rw["g_mm"], i + 1)
                nc.scalar.activation(gg[:, i, :], ps_o[:, 2 + i % 2, 0:NX], ACT.Copy).then_inc(rw["g_act"], 1)
            act.wait_ge(rw["ss"], 1)
            nc.scalar.activation(head_rows, BANK[3][0:16, 0:NX], ACT.Sqrt).then_inc(rw["std"], 1)
            head_norm()
            attend(1)
            c0 = math.exp(-0.5)
            quarters = "p (m n) -> p m n"

            def decays(i):
                act.wait_ge(rw["cum"], i + 1)
                if i:
                    act.wait_ge(rw["feat"], i)
                cum = FREE[1].rearrange("p (u e n) -> p u e n", u=2, e=2)
                nc.scalar.activation(dinc.rearrange("p (u n) -> p u n", u=2), cum[:, :, 0, :], ACT.Exp, scale=-c0)
                nc.scalar.activation(dexc.rearrange("p (u n) -> p u n", u=2), cum[:, :, 1, :], ACT.Exp, scale=-c0)
                nc.scalar.activation(dinv.rearrange("p (u n) -> p u n", u=2), cum[:, :, 0, :], ACT.Exp, scale=c0).then_inc(rw["dec"], 1)

            def token_major(i):
                act.wait_ge(rw["tp"], i + 1)
                nc.scalar.activation(tmaj[i % 2][:, 0:2], FREE[1].rearrange("p (e u n) -> p e u n", e=2, u=2), ACT.Copy)
                nc.scalar.activation(tmaj[i % 2][:, 2, :, :], FREE[4][:, 0:256].rearrange("p (u n) -> p u n", u=2), ACT.Copy)
                al_ = FREE[4][:, 256:512].rearrange("p (u q n) -> p q u n", u=2, q=2)
                nc.scalar.activation(xs[i % 2][:, :, 0:64].rearrange("p (q u) n -> p q u n", q=2), al_, ACT.Copy).then_inc(rw["tm"], 1)

            def mv_out(i):
                act.wait_ge(rw["mv"], i + 1)
                nc.scalar.activation(xs[i % 2][:, :, 64:128], FREE[4][:, 0:256].rearrange(quarters, m=4), ACT.Copy).then_inc(rw["mvx"], 1)

            def tx_out(i):
                act.wait_ge(rw["tx"], i + 1)
                nc.scalar.activation(tx, FREE[0].rearrange(quarters, m=4), ACT.Copy).then_inc(rw["txs"], 1)

            decays(0)
            token_major(0)
            mv_out(0)
            for i in range(RT + 1):
                if i:
                    tx_out(i - 1)
                if i + 1 < RT:
                    decays(i + 1)
                if i + 1 < RT:
                    token_major(i + 1)
                if i + 1 < RT:
                    mv_out(i + 1)
            act.wait_ge(rw["var"], 1)
            nc.scalar.activation(head_rows, BANK[3][0:16, 0:NX], ACT.Sqrt, bias=C("lnx_eps", 1)[0:16], scale=1.0 / 64).then_inc(rw["vstd"], 1)
            act.wait_ge(at_y, AT0[2])
            for b in (3, 0, 1, 2):
                if b < 3:
                    act.wait_ge(rw["fin"], b + 1)
                nc.scalar.activation(hh[:, 2 * b:2 * b + 2, 0:NX], y_all[:, 2 * b:2 * b + 2, :], ACT.Copy).then_inc(y_hi, 1)
            chunks("a_out", 0, late=1)
            norm(lambda d: x[:, d, :], NX, None, "split", after(FIRST["ffn", 5]), FIRST["ffn", 5])
            ffn(5, NX)
            norm(lambda d: x[:, d, :], NX, None, "split", after(FIRST["kv", 0]), FIRST["kv", 0])
            n = FIRST["kv", 0]
            for c in range(6):
                split_hi(n + c + SLOTS)
                if c == 3:
                    head_norm()
            norm(lambda d: x[:, d, :], NX, None, "split", None, FIRST["ffn", 6], again=True)
            ffn(6, NX)
            norm(lambda d: x[:, d, :], NTOK, None, "split", with_memory(FIRST["b_q", 0], 2), FIRST["b_q", 0])
            chunks("b_q", 0)
            head_norm()
            chunks("memkv", 1)
            head_norm()
            attend(2)
            act.wait_ge(at_y, AT0[3])
            split_y(y_all[:, 0:4, :], 4)
            chunks("b_out", 0, late=1)
            norm(lambda d: x[:, d, :], NX, None, "split", after(FIRST["ffn", 7]), FIRST["ffn", 7])
            ffn(7, NX)

        @block.vector
        def _(dve):
            st = {"seq": 0, "k": 0, "t": 0, "hi": 0, "hn": 0, "y": 0, "back": 0, "late": []}
            stt, tt_, ts_ = nc.vector.scalar_tensor_tensor, nc.vector.tensor_tensor, nc.vector.tensor_scalar

            def link(ins):
                st["seq"] += 1
                ins.then_inc(dve_seq, 1)
                dve.wait_ge(dve_seq, st["seq"])

            def split_lo(n, i=None, per=SLOTS):
                if n >= PADDED:
                    return
                dve.wait_ge(w_hi, n + 1 if i is None else i * per + (n + 1))
                tt_(wlo[:, n % SLOTS, :], wraw[:, n % SLOTS, :], whi[:, n % SLOTS, :].bitcast(f32), sub).then_inc(w_lo, 1)

            def norm(src, N, A, B, mode, part=None, again=False):
                k = st["k"] - again
                st["k"] += not again
                if not again:
                    dve.wait_ge(nm_std, k + 1)
                    nc.vector.reciprocal(rstd[:, 0:N], rstd[:, 0:N]).then_inc(nm_rstd, 1)
                if part is not None:
                    ada_part(part)
                dve.wait_ge(nm_rstd, k + 1)
                units = [(d, j) for d in range(KT) for j in range(N // NX)]

                def scaled(d, j):
                    dst = src(d)[:, HALVES[j]] if mode == "final" else tsq[:, d * NTOK + j * NX:d * NTOK + (j + 1) * NX]
                    stt(dst, src(d)[:, HALVES[j]], A(d, j), rstd[:, HALVES[j]], mult, mult).then_inc(nm_t, 1)
                    st["t"] += 1

                def rest(d, j):
                    st["hi"] += 1
                    dve.wait_ge(nm_hi, st["hi"])
                    t = tsq[:, d * NTOK + j * NX:d * NTOK + (j + 1) * NX]
                    up = hh[:, d, HALVES[j]].bitcast(f32)
                    if B is None:
                        tt_(hl[:, d, HALVES[j]], t, up, sub).then_inc(h_ready, 1)
                    else:
                        stt(hl[:, d, HALVES[j]], t, B(d, j), up, add, sub).then_inc(h_ready, 1)

                lag = 3 if mode == "split" else 0
                for q in range(len(units) + lag):
                    if q < len(units):
                        scaled(*units[q])
                    if mode == "split" and q >= lag:
                        rest(*units[q - lag])
                if mode == "plain":
                    st["hi"] += len(units)
                    dve.wait_ge(nm_hi, st["hi"])
                while st["late"]:
                    split_lo(st["late"].pop())

            def out_tiles(n):
                for q in range(DONE[n] - (DONE[n - 1])):
                    dve.wait_ge(mm_done, DONE[n - 1] + q + 1)
                    yield ps_o[:, (TILE0[n] + q) % 4, :]

            def residual(src, d, N, gate):
                for j in range(N // NX):
                    ins = stt(x[:, d, HALVES[j]], src[:, HALVES[j]], gate(d, j), x[:, d, HALVES[j]], mult, add)
                ins.then_inc(o_free, 1)

            def ffn(f, N, gate):
                n0, g0 = FIRST["ffn", f], f * GROUPS
                per, step, _, n_up, n_down, n_ada, n_last = ffn_pass(f)
                sg = tsq[:, 0:1024].rearrange("p (j n) -> p j n", j=2)
                tmp = tsq[:, 1024:2048].rearrange("p (j n) -> p j n", j=2)

                def product(group, done, last=True):
                    dve.wait_ge(mm_done, done)
                    if last:
                        dve.wait_ge(a_ready, group)
                    dve.wait_ge(g_act, group + 1)
                    tt_(tmp[:, :, 0:N], sg[:, :, 0:N], ps_u[:, :, 0:N], mult).then_inc(u_mul, 1)

                def hidden(group):
                    dve.wait_ge(a_hi, group + 1)
                    tt_(al[:, :, 0:N], tmp[:, :, 0:N], ah[:, :, 0:N].bitcast(f32), sub).then_inc(a_ready, 1)

                def down(n, done, between=lambda d: None):
                    for d in range(KT):
                        dve.wait_ge(mm_done, done + (d + 1))
                        residual(ps_o[:, (TILE0[n] + d) % BANKS, :], d, N, gate)
                        between(d)

                product(g0, DONE[n0 + 1], g0 > 0)
                split_lo(n0 + 3)
                split_lo(n0 + 4)
                hidden(g0)
                with dve.Fori(0, GROUPS - 1) as i:
                    split_lo(n0 + 5, i, per)
                    held = {2: n_up + SLOTS, 5: n_up + 1 + SLOTS} if n_ada else {}

                    def between(d):
                        if d in held:
                            split_lo(held[d], i, per)

                    for n in range(n0 + 3, n0 + 2 + per):
                        if n == n_up:
                            product(i + (g0 + 1), i * step + DONE[n])
                        elif n == n_down:
                            down(n, i * step + DONE[n - 1], between)
                            hidden(i + (g0 + 1))
                            if not n_ada:
                                split_lo(n_up + SLOTS, i, per)
                        else:
                            ada_out(n, n_ada.index(n), i, step)
                        if n != n_up and n + SLOTS not in held.values():
                            split_lo(n + SLOTS, i, per)
                down(n_last, DONE[n_last - 1])
                st["late"].append(n_last + SLOTS)

            def ada_out(n, c, i=None, step=0):
                off = 0 if i is None else i * step
                r = ROWS[c % 3]
                rows = ada_rows[r, 256 * (c // 3):256 * (c // 3 + 1)] if i is None else ada_rows[r, ds(i * 256, 256)]
                for q in range(DONE[n] - (DONE[n - 1] if n else 0)):
                    dve.wait_ge(mm_done, off + ((DONE[n - 1] if n else 0) + q + 1))
                    part = ps_o[0:4, (TILE0[n] + q) % BANKS, 0:256]
                    if q:
                        dve.wait_ge(o_free, freed(TILE0[n] + q) + (0 if i is None else i * sum(FFN_ADA_PASS)))
                        tt_(rows, rows, part, add).then_inc(o_free, 1)
                    else:
                        nc.vector.tensor_copy(rows, part).then_inc(o_free, 1)

            def ada_part(e):
                c0, c1 = ADA_PARTS[e]
                dve.wait_ge(ad_turn, e + 1)
                flat = mods[:].rearrange("p l t v -> p (l t) v")
                ps = ps_u[:, 0, 0:4 * (c1 - c0)].rearrange("p (i j c v) -> p v i c j", j=2, c=3, v=2)
                turned = "p (i c j) -> p i c j"
                bias_ = V("ada_b", 2 * c0, 2 * (c1 - c0)).rearrange(turned, c=3, j=2)
                for v in range(2):
                    ins = tt_(flat[:, 2 * c0:2 * c1, v].rearrange(turned, c=3, j=2), ps[:, v], bias_, add)
                link(ins)
                for l, first, last in (((0, 0, 1),), ((0, 1, 3),), ((1, 0, 3),))[e]:
                    m = mods[:, l]
                    for v in range(2):
                        for a in range(first, last):
                            stt(acol[:, l, a, :, v], m[:, 24 * a + 8:24 * a + 16, v], 1.0, V("norm_g", 24 * l + 8 * a, 8), add, mult)
                            gate = m[:, 24 * a + 16:24 * a + 24, v]
                            if a == 1 and l == 0:
                                tt_(gcol[:, l, a, :, v], gate, V("pool_scale", 0, 8), mult)
                            else:
                                ts_(gcol[:, l, a, :, v], gate, 1.0 if a == 1 else 0.5, None, mult)
                nc.vector.memset(cols[:, 60:61], 0.0).then_inc(ad_col, 1)
                dve.wait_ge(ad_col, e + 1)

            def chunks_out(stage, i, take, late=0):
                n0, n1 = FIRST[stage, i], FIRST_AFTER[stage, i]
                for n in range(n0, n1):
                    for q, tile in enumerate(out_tiles(n)):
                        take(n - n0, q, tile)
                    if n < n1 - late:
                        split_lo(n + SLOTS)
                st["late"] = list(range(n1 - late + SLOTS, n1 + SLOTS))[::-1]

            def add_to_x(N, gate, per):
                return lambda c, q, tile: residual(tile, c * per + q, N, gate)

            def head_squares(*bufs):
                st["hn"] += 1
                dve.wait_ge(o_free, freed(st["tiles"]))
                if st["hn"] > 1:
                    dve.wait_ge(hn_done, st["hn"] - 1)
                at = 0
                for buf, _ in bufs:
                    nt = buf.shape[1]
                    ins = tt_(hid[:, at * NX:(at + nt) * NX].rearrange("p (k n) -> p k n", n=NX), buf, buf, mult)
                    at += nt
                ins.then_inc(hn_sq, 1)

            def head_factors():
                dve.wait_ge(hn_std, st["hn"])
                nc.vector.reciprocal(head_rows, head_rows).then_inc(hn_inv, 1)

            def head_scale(*bufs):
                at = 0
                for buf, gain in bufs:
                    for k in range(0, buf.shape[1], 2):
                        st["back"] += 1
                        dve.wait_ge(hn_back, st["back"])
                        two_ = buf[:, k:k + 2, :]
                        ins = stt(two_, two_, gain, BANK[at % 4].rearrange("p (k n) -> p k n", n=NX), mult, mult)
                        at += 1
                ins.then_inc(hn_done, 1)

            def head_norm(*bufs):
                head_squares(*bufs)
                head_factors()
                head_scale(*bufs)

            def rest_y(src, nt, width=NX):
                st["y"] += 1
                dve.wait_ge(y_hi, st["y"])
                tt_(hl[:, 0:nt, 0:width], src, hh[:, 0:nt, 0:width].bitcast(f32), sub).then_inc(y_ready, 1)

            def attend(a):
                U = ATT[a]

                def maximum(u):
                    g, unit = AT0[a] + u, U[u]
                    dve.wait_ge(at_s, g + 1)
                    if g >= 2:
                        dve.wait_ge(at_p, g - 1)
                    bank = ps_g if g % 2 == 0 else ps_u
                    w = unit["width"]
                    nm = cols[:, 4 * (g % 2):4 * (g % 2) + unit["subs"]]
                    if unit["bias"] is None:
                        nc.vector.reduce_max(nm, bank[:, 0:unit["subs"], 0:w], AX.X, negate=True).then_inc(at_m, 1)
                        return
                    dve.wait_ge(at_b[u % NB], 16 * (u // NB + 1))
                    if g >= 2:
                        dve.wait_ge(at_t, g - 1)
                    s = probs[g % 2][:, 0:w]
                    by_group = "p (g n) -> p g n"
                    tt_(s[:, 0:512].rearrange(by_group, g=2), bank[:, 0, :].rearrange(by_group, g=2), bias[u % NB][:, 0:2, ::-1], add)
                    link(tt_(s[:, 512:768], bank[:, 1, 0:256], bias[u % NB][:, 2, ::-1], add))
                    nc.vector.reduce_max(nm, s, AX.X, negate=True).then_inc(at_m, 1)

                def normalise(u):
                    g, unit = AT0[a] + u, U[u]
                    dve.wait_ge(at_e, g + 1)
                    w = unit["width"]
                    su = cols[:, 8 + 4 * (g % 2):8 + 4 * (g % 2) + unit["subs"]]
                    r = cols[:, 16 + 4 * (g % 2):16 + 4 * (g % 2) + unit["subs"]]
                    link(nc.vector.reciprocal(r, su))
                    p = probs[g % 2]
                    if unit["subs"] == 1:
                        ts_(p[:, 0:w], p[:, 0:w], r[:, 0:1], None, mult).then_inc(at_p, 1)
                    else:
                        link(tt_(r[:, 1:2], r[:, 1:2], lam_col, mult))
                        link(ts_(p[:, w:2 * w], p[:, w:2 * w], r[:, 1:2], None, mult))
                        stt(p[:, 0:w], p[:, 0:w], r[:, 0:1], p[:, w:2 * w], mult, add).then_inc(at_p, 1)

                def result(u):
                    g, unit = AT0[a] + u, U[u]
                    dve.wait_ge(at_o, g + 1)
                    nc.vector.tensor_copy(unit["y"], ps_o[unit["rows"], 2 + g % 2, 0:128]).then_inc(at_y, 1)

                for u in range(len(U) + 2):
                    if u < len(U):
                        maximum(u)
                    if 1 <= u <= len(U):
                        normalise(u - 1)
                    if u >= 2:
                        result(u - 2)

            def xs_(d):
                return x[:, d, :]

            def A_mod(l, a):
                return lambda d, j: acol[:, l, a, d, j:j + 1]

            def B_mod(l, a):
                return lambda d, j: mods[:, l, 24 * a + d, j:j + 1]

            def gate(l, a):
                return lambda d, j: gcol[:, l, a, d, j:j + 1]

            def gain(name, l=0):
                return lambda d, j: V(name, KT * l + d)

            half = lambda d, j: 0.5
            one = lambda d, j: 1.0

            dve.sem_inc(o_free, BANKS)
            dve.wait_ge(ad_hi, 1)
            tt_(cs[:, :, 2:4], sc[:].rearrange("p (v k) -> p k v", v=2), cs[:, :, 0:2].bitcast(f32), sub).then_inc(ad_lo, 1)
            for n in range(SLOTS):
                split_lo(n)
            dve.wait_ge(ad_zero, 1)
            for n in range(ADA_FIRST):
                ada_out(n, n)
                split_lo(n + SLOTS)
            norm(xs_, NTOK, A_mod(0, 0), B_mod(0, 0), "split", part=0)
            ffn(0, NTOK, gate(0, 0))
            norm(xs_, NTOK, A_mod(0, 1), None, "plain", part=1)
            link(pool_edges(nc.vector, pads["vector"]))
            dve.wait_ge(ic_in, 16)
            def rest_pooled(g):
                st["y"] += 1
                dve.wait_ge(y_hi, st["y"])
                tt_(hl[:, 2 * g:2 * g + 2, :], tsq[:, 1024 * g:1024 * (g + 1)].rearrange("p (a n) -> p a n", a=2),
                    hh[:, 2 * g:2 * g + 2, :].bitcast(f32), sub).then_inc(y_ready, 1)

            pool_group(nc.vector, link, pads["vector"], 0).then_inc(pl_diff, 1)
            pool_group(nc.vector, link, pads["vector"], 1).then_inc(pl_diff, 1)
            rest_pooled(0)
            rest_pooled(1)
            pool_group(nc.vector, link, pads["vector"], 3).then_inc(pl_diff, 1)
            rest_pooled(2)
            rest_pooled(3)
            chunks_out("pool", 0, add_to_x(NTOK, gate(0, 1), 8), late=1)
            norm(xs_, NTOK, A_mod(0, 2), B_mod(0, 2), "split")
            dve.wait_ge(ad_zero, 2)
            ffn(1, NTOK, gate(0, 2))
            norm(xs_, NTOK, A_mod(1, 0), B_mod(1, 0), "split", part=2)
            ffn(2, NTOK, gate(1, 0))
            norm(xs_, NTOK, A_mod(1, 1), B_mod(1, 1), "split")

            def take_qkv(c, q, tile):
                if c < 4:
                    ts_(q_d[:, 2 * c + q, :], tile[:, 0:NX], 0.125, None, mult).then_inc(o_free, 1)
                elif c < 8:
                    nc.vector.tensor_copy(k_d[:, 2 * (c - 4) + q, :], tile).then_inc(o_free, 1)
                else:
                    nc.vector.tensor_copy(v_d[:, q, 256 * (c - 8):256 * (c - 7)], tile[:, 0:256]).then_inc(o_free, 1)

            chunks_out("qkv", 0, take_qkv)
            dve.wait_ge(c_late, 16)
            for r in range(8):
                z = q_d[:, 2 * r:2 * r + 2, :] if r < 4 else k_d[:, 2 * (r - 4):2 * (r - 4) + 2, 0:NX]
                t = tsq[:, 512 * (r % 4):512 * (r % 4) + 512].rearrange("p (a n) -> p a n", a=2)
                dve.wait_ge(ro_mm, r + 1)
                tt_(t, BANK[r % 4].rearrange("p (a n) -> p a n", a=2), C("sin", 512).rearrange("p (a n) -> p a n", a=2), mult).then_inc(ro_sin, 1)
                link(tt_(z, z, C("cos", 512).rearrange("p (a n) -> p a n", a=2), mult))
                tt_(z, z, t, add).then_inc(ro_done, 1)
            dve.wait_ge(lam_in, 16)
            for j in range(2):
                link(tt_(lamb[:, 128 * j:128 * j + 64], lamb[:, 128 * j:128 * j + 64], lamb[:, 128 * j + 64:128 * j + 128], mult))
            nc.vector.reduce_sum(cols[:, 56:58], lamb[:].rearrange("p (j n) -> p j n", j=2)[:, :, 0:64], AX.X).then_inc(lam_sum, 1)
            dve.wait_ge(lam_exp, 1)
            link(tt_(lam_col, cols[:, 59:60], cols[:, 58:59], sub))
            link(ts_(lam_col, lam_col, -LAM_INIT, None, add))
            attend(0)
            link(ts_(subln_gain, V("diff_subln_g"), 1.0 - LAM_INIT, None, mult))
            dve.wait_ge(at_y, AT0[1])
            tt_(big[:, 2048:4096], tsq[:, 0:2048], tsq[:, 0:2048], mult).then_inc(sl_sq, 1)
            dve.wait_ge(sl_std, 1)
            nc.vector.reciprocal(subln_rows, subln_rows).then_inc(sl_inv, 1)
            for b in range(4):
                dve.wait_ge(sl_back, b + 1)
                y2 = tsq[:, 512 * b:512 * (b + 1)]
                stt(y2, y2, subln_gain, BANK[b], mult, mult).then_inc(sl_y, 1)
            for b in range(4):
                st["y"] += 1
                dve.wait_ge(y_hi, st["y"])
                tt_(hl[:, 2 * b:2 * b + 2, 0:NX], y_all[:, 2 * b:2 * b + 2, :], hh[:, 2 * b:2 * b + 2, 0:NX].bitcast(f32), sub).then_inc(y_ready, 1)
            chunks_out("wo", 0, add_to_x(NX, gate(1, 1), 2), late=1)
            norm(xs_, NX, A_mod(1, 2), B_mod(1, 2), "split")
            ffn(3, NX, gate(1, 2))
            norm(xs_, NX, gain("final_g"), None, "final")
            dve.wait_ge(nm_t, st["t"])
            norm(xs_, NX, gain("ffn_pre_norm_2", 0), None, "split")
            ffn(4, NX, half)

            def take_memkv(c, q, tile):
                nc.vector.tensor_copy(mem_k[:, q, :] if c == 0 else mem_v[:, q, :], tile[:, 0:256]).then_inc(o_free, 1)

            def with_memory(l):
                return lambda d, j: V("mem_norm_2" if j else "mix_norm_2", KT * l + d)

            norm(xs_, NTOK, with_memory(0), None, "split")

            def take_in(c, q, tile):
                i = 2 * c + q
                dst = proj[:, i, 1:257] if i < 20 else mem_q[0][:, i - 20, :]
                nc.vector.tensor_copy(dst, tile[:, 0:NX]).then_inc(o_free, 1)
                j = i - 1
                if 0 <= j < 20:
                    dve.wait_ge(o_free, freed(TILE0[FIRST["a_in", 0]] + j + 1))
                    if j >= 8:
                        dve.wait_ge(rw["shift"], j - 7)
                    tt_(moved[:, j % 8, :], proj[:, j, 0:256], proj[:, j, 1:257], sub).then_inc(rw["move"], 1)
                j = i - 2
                if 0 <= j < 20:
                    dve.wait_ge(rw["move"], j + 1)
                    stt(proj[:, j, 1:257], moved[:, j % 8, :], V("a_shift_mu_2", j), proj[:, j, 1:257], mult, add).then_inc(rw["shift"], 1)

            link(nc.vector.memset(proj[:, :, 0:1], 0.0))
            chunks_out("a_in", 0, take_in)
            link(ts_(qgain, vec[:, vat["mem_q_norm_2"]:vat["mem_q_norm_2"] + 3], 0.125, None, mult))
            chunks_out("memkv", 0, take_memkv)
            st["tiles"] = TILE0[FIRST["a_out", 0]]
            dve.wait_ge(rw["shift"], 20)
            dve.wait_ge(lora_in, 48)
            dve.wait_ge(rw["z"], 1)
            for u in range(2):
                bank = ps_g if u == 0 else ps_u
                tt_(zs[:, u, 0:512], bank[:, 0, :], w0b[:, 0:512], add)
                ins = tt_(zs[:, u, 512:768], bank[:, 1, 0:256], w0b[:, 512:768], add)
            ins.then_inc(rw["zb"], 1)
            for i in range(RT):
                ins = ts_(kk[:, i, :], k_[:, i, :], V("a_kk_scale_2", i), None, mult)
            link(ins)
            tt_(bon, kk, kk, mult).then_inc(rw["sq"], 1)
            sq3 = hid[:, 0:1536].rearrange("p (i n) -> p i n", n=NX)
            dve.wait_ge(rw["std"], 1)
            link(ts_(head_rows, head_rows, 1e-12, None, amax))
            nc.vector.reciprocal(head_rows, head_rows).then_inc(rw["inv"], 1)
            for b in range(3):
                dve.wait_ge(rw["back"], b + 1)
                k2 = kk[:, 2 * b:2 * b + 2, :]
                ins = tt_(k2, k2, BANK[b].rearrange("p (i n) -> p i n", n=NX), mult)
            link(ins)
            dve.wait_ge(rw["a_act"], RT)
            for i in range(RT):
                ins = ts_(sq3[:, i, :], aa[:, i, :], 1.0, V("a_k_a_2", i), sub, mult)
            link(ins)
            link(stt(k_, sq3, 1.0, k_, add, mult))
            for i in range(RT):
                ins = stt(bon[:, i, :], r_[:, i, :], V("a_r_k_2", i), k_[:, i, :], mult, mult)
            ins.then_inc(rw["bsq"], 1)
            link(tt_(aa, aa, kk, mult))
            dve.wait_ge(rw["bsum"], 1)
            dve.wait_ge(rw["bsq"], 1)
            for b in range(3):
                link(tt_(bon[:, 2 * b:2 * b + 2, :], BANK[b].rearrange("p (i n) -> p i n", n=NX), v_[:, 2 * b:2 * b + 2, :], mult))
            nc.vector.memset(cols[:, 60:61], 0.0).then_inc(rw["bon"], 1)
            head_norm((mem_q[0], qgain[:, 0:1]), (mem_k, V("mem_k_norm_2", 0)))
            attend(1)
            m256 = C("lp_mask", 256).rearrange("p (e n) -> p e n", e=2)
            by_unit = "p (m n) -> p m n"

            def features(i):
                dve.wait_ge(rw["dec"], i + 1)
                if i >= 2:
                    dve.wait_ge(rw["rps"], i - 1)
                a = ar[i % 2]
                stt(a[:, :, 0, :], two(kk[:, i, :]), -1.0, two(dexc), mult, mult)
                tt_(a[:, :, 1, :], two(r_[:, i, :]), two(dinc), mult)
                tt_(be, two(aa[:, i, :]), two(dinv), mult)
                nc.vector.tensor_copy(ends[:, i % 3, :], dinc.rearrange("p (c n) -> p c n", n=CH)[:, :, CH - 1])
                tt_(ka, two(k_[:, i, :]), two(dinv), mult).then_inc(rw["feat"], 1)

            def pairs(i, q, which, buf, bank, done):
                dve.wait_ge(rw[which], 2 * i + q + 1)
                tt_(buf[i % 2][:, 2 * q:2 * q + 2], bank.rearrange("p (m e n) -> p m e n", m=2, e=2), over(m256, 2), mult).then_inc(rw[done], 1)

            def start_transposed(i):
                dve.wait_ge(rw["lpm"], 2 * i + 2)
                link(tt_(tit[i % 2], lp[i % 2][:, :, 0, :], over(C("m1t"), 4), mult))
                tt_(tit[i % 2], tit[i % 2], over(ident, 4), add).then_inc(rw["tit"], 1)

            def start_inverse(i):
                dve.wait_ge(rw["tib"], i + 1)
                for q, bank in enumerate((FREE[1], FREE[3])):
                    ins = tt_(ti[:, 2 * q:2 * q + 2, :], bank[:, 0:256].rearrange(by_unit, m=2), over(C("m1"), 2), mult)
                link(ins)
                tt_(ti, ti, over(ident, 4), add).then_inc(rw["lmask"], 1)

            def mask_p(i, l):
                dve.wait_ge(rw["p"], 5 * i + l + 1)
                tt_(pp, INV[0].rearrange(by_unit, m=4), over(C(f"m{2 << l}"), 4), mult).then_inc(rw["pm"], 1)

            def grow(i, l):
                dve.wait_ge(rw["t"], 5 * i + l + 1)
                if l < 4:
                    tt_(ti, ti, INV[1].rearrange(by_unit, m=4), add).then_inc(rw["ti"], 1)
                t = tit[i % 2]
                tt_(t, t, INV[2].rearrange(by_unit, m=4), add).then_inc(rw["tt"], 1)

            def readout(i):
                dve.wait_ge(rw["rp"], i + 1)
                tt_(rp, ar[i % 2][:, :, 1, :], two(FREE[0][:, 0:256]), add).then_inc(rw["rps"], 1)

            def transitions(i):
                dve.wait_ge(rw["gz"], i + 1)
                for c in (1, 2):
                    tt_(gi[:, c - 1, :], FREE[2 + c % 2][:, 64 * (c // 2):64 * (c // 2) + 64], C("ident64", 64), add)
                for c in range(3):
                    ins = ts_(zd[:, c, :], FREE[2 + c % 2][:, 128 + 64 * (c // 2):192 + 64 * (c // 2)], ends[:, i % 3, c:c + 1], None, mult)
                ins.then_inc(rw["gzs"], 1)
                nc.vector.tensor_copy(y_all[:, i, :], FREE[2][:, 256:512]).then_inc(rw["y_in"], 1)

            def state(i, c):
                dve.wait_ge(rw["gzs"], i + 1)
                dve.wait_ge(rw["s"], 2 * i + c + 1)
                stt(st2[:, c, :], FREE[3][:, 256 + 64 * c:320 + 64 * c], ends[:, i % 3, c + 1:c + 2], zd[:, c + 1, :], mult, add).then_inc(rw["ss2"], 1)

            def output(i):
                dve.wait_ge(rw["y_in"], i + 1)
                dve.wait_ge(rw["y"], i + 1)
                y = y_all[:, i, CH:NX]
                tt_(y, y, FREE[2][:, CH:NX], add).then_inc(rw["yout"], 1)

            features(0)
            for q in range(2):
                pairs(0, q, "lp", lp, FREE[q], "lpm")
            for q, b in enumerate((4, 0)):
                pairs(0, q, "mp", mp, FREE[b], "mpm")
            start_transposed(0)
            start_inverse(0)
            for i in range(RT + 1):
                inv, post, pre = i < RT, i > 0, i + 1 < RT
                if inv:
                    mask_p(i, 0)
                    grow(i, 0)
                    mask_p(i, 1)
                if post:
                    readout(i - 1)
                if pre:
                    features(i + 1)
                if inv:
                    grow(i, 1)
                if post:
                    transitions(i - 1)
                if inv:
                    mask_p(i, 2)
                if post:
                    state(i - 1, 0)
                if inv:
                    grow(i, 2)
                if post:
                    state(i - 1, 1)
                if pre:
                    pairs(i + 1, 0, "lp", lp, FREE[0], "lpm")
                if inv:
                    mask_p(i, 3)
                if pre:
                    pairs(i + 1, 1, "lp", lp, FREE[1], "lpm")
                if inv:
                    grow(i, 3)
                if post:
                    output(i - 1)
                if pre:
                    pairs(i + 1, 0, "mp", mp, FREE[4], "mpm")
                if inv:
                    mask_p(i, 4)
                if pre:
                    pairs(i + 1, 1, "mp", mp, FREE[0], "mpm")
                    start_inverse(i + 1)
                if inv:
                    grow(i, 4)
                if pre:
                    start_transposed(i + 1)
            y6 = y_all[:, 0:6, :]
            for i in range(RT):
                ins = ts_(bon[:, i, :], bon[:, i, :], V("a_lnx_b_2", i), None, add)
            dve.wait_ge(rw["mean"], 1)
            for b in range(3):
                ins = stt(y6[:, 2 * b:2 * b + 2, :], BANK[b].rearrange("p (i n) -> p i n", n=NX), -1.0 / 64, y6[:, 2 * b:2 * b + 2, :], mult, add)
            link(ins)
            tt_(sq3, y6, y6, mult).then_inc(rw["cen"], 1)
            dve.wait_ge(rw["vstd"], 1)
            nc.vector.reciprocal(head_rows, head_rows).then_inc(rw["vinv"], 1)
            for i in range(RT):
                if i % 2 == 0:
                    dve.wait_ge(rw["vback"], i // 2 + 1)
                ins = stt(y6[:, i, :], y6[:, i, :], V("a_lnx_g_2", i), BANK[i // 2][:, NX * (i % 2):NX * (i % 2 + 1)], mult, mult)
            link(ins)
            for b in range(3):
                y2 = y6[:, 2 * b:2 * b + 2, :]
                ins = tt_(y2, y2, bon[:, 2 * b:2 * b + 2, :], add)
            link(ins)
            dve.wait_ge(rw["g_act"], RT)
            for b in range(3):
                y2 = y6[:, 2 * b:2 * b + 2, :]
                tt_(y2, y2, gg[:, 2 * b:2 * b + 2, :], mult).then_inc(rw["fin"], 1)
            dve.wait_ge(rw["fin"], 3)
            for b in (3, 0, 1, 2):
                st["y"] += 1
                dve.wait_ge(y_hi, st["y"])
                tt_(hl[:, 2 * b:2 * b + 2, 0:NX], y_all[:, 2 * b:2 * b + 2, :], hh[:, 2 * b:2 * b + 2, 0:NX].bitcast(f32), sub).then_inc(y_ready, 1)
            chunks_out("a_out", 0, add_to_x(NX, one, 2), late=1)
            norm(xs_, NX, gain("ffn_post_norm_2", 0), None, "split")
            ffn(5, NX, half)
            dve.wait_ge(bi_row, 1)
            for g in range(3):
                tt_(rowb[:, 512 * g:512 * (g + 1)], BANK[1 + g][0:4, :], bt[0:4, 1536 + 512 * g:2048 + 512 * g], add).then_inc(bi_sb, 1)
            norm(xs_, NX, gain("kv_norm_2"), None, "split")

            def take_kv(c, q, tile):
                if c < 3:
                    nc.vector.tensor_copy(k_g[:, 2 * c + q, :], tile[:, 0:NX]).then_inc(o_free, 1)
                else:
                    nc.vector.tensor_copy(v_g[:, q, 256 * (c - 3):256 * (c - 2)], tile[:, 0:256]).then_inc(o_free, 1)
                if q == 1:
                    if c == 2:
                        head_squares((k_g, V("kv_k_norm_2")))
                    elif c == 3:
                        head_factors()
                    elif c == 4:
                        head_scale((k_g, V("kv_k_norm_2")))

            dve.wait_ge(bi_dram, 16)
            st["tiles"] = TILE0[FIRST["kv", 0] + 3]
            chunks_out("kv", 0, take_kv)
            norm(xs_, NX, gain("ffn_pre_norm_2", 1), None, "split", again=True)
            ffn(6, NX, half)
            norm(xs_, NTOK, with_memory(1), None, "split")

            def take_q(c, q, tile):
                i = 2 * c + q
                nc.vector.tensor_copy(q_g[:, i, :] if i < 6 else mem_q[1][:, i - 6, :], tile[:, 0:NX]).then_inc(o_free, 1)

            chunks_out("b_q", 0, take_q)
            st["tiles"] = TILE0[FIRST["memkv", 1]]
            head_norm((q_g, qgain[:, 2:3]), (mem_q[1], qgain[:, 1:2]))
            chunks_out("memkv", 1, take_memkv)
            st["tiles"] = TILE0[FIRST["b_out", 0]]
            head_norm((mem_k, V("mem_k_norm_2", 1)))
            attend(2)
            rest_y(y_all[:, 0:4, :], 4)
            chunks_out("b_out", 0, add_to_x(NX, one, 4), late=1)
            norm(xs_, NX, gain("ffn_post_norm_2", 1), None, "split")
            ffn(7, NX, half)

        @block.tensor
        def _(pe):
            st = {"k": 0, "h": 0, "hn": 0, "y": 0, "sums": 0}
            mm = nc.tensor.matmul

            def chunk(n, i=None, per=SLOTS):
                pe.wait_ge(w_lo, n + 1 if i is None else i * per + (n + 1))
                return n % SLOTS

            def weights(s, cols_):
                return (whi[:, s, :].rearrange("p (k n) -> p k n", n=cols_), wlo[:, s, :].rearrange("p (k n) -> p k n", n=cols_))

            def mm3(out, a, b, first, last):
                mm(out, a[1], b[0], start=first, stop=False)
                mm(out, a[0], b[1], start=False, stop=False)
                return mm(out, a[0], b[0], start=False, stop=last)

            def keep_clock(n, bank):
                for _ in range(n):
                    mm(bank, ones, cst[:, 0:bank.shape[-1]], start=True, stop=True)

            LAG = 3

            def sum_squares(N, end):
                for d in range(st["sums"], end):
                    pe.wait_ge(nm_sq, st["k"] * KT + d + 1)
                    ins = mm(ps_g[:, 0, 0:N], ones, tsq[:, d * NTOK:d * NTOK + N], start=d == 0, stop=d == KT - 1)
                    if d == KT - 1:
                        ins.then_inc(nm_sum, 1)
                st["sums"] = max(st["sums"], end)

            def norm(N, split=True, part=None, again=False):
                if again:
                    st["h"] += KT * (N // NX)
                    return
                sum_squares(N, KT)
                if part is not None:
                    ada_turn(part)
                keep_clock(N // 64 - 1 if part is None else 3, BANK[3])
                st["k"], st["sums"] = st["k"] + 1, 0
                if split:
                    st["h"] += KT * (N // NX)

            def tile(n, q):
                T = TILE0[n] + q
                pe.wait_ge(o_free, T + 1)
                return ps_o[:, T % 4, :]

            def split_input(N):
                h0, per = st["h"] - KT * (N // NX), N // NX
                return lambda k: pe.wait_ge(h_ready, h0 + (k + 1) * per)

            def project(n, N, rows=KT, width=256, t0=0, into_x=None):
                w = weights(chunk(n), width)
                for j in range(width // 128):
                    out = tile(n, j)
                    for k in range(rows):
                        c = slice(j * 128, (j + 1) * 128)
                        ins = mm3(out[:, 0:N], (w[0][:, k, c], w[1][:, k, c]), (hh[:, k, t0:t0 + N], hl[:, k, t0:t0 + N]), k == 0, k == rows - 1)
                    ins.then_inc(mm_done, 1)
                    if into_x is not None:
                        sum_squares(N, into_x + j + 1 - LAG)

            def project_first(n, N, of=None):
                ready = split_input(of or N)
                w = [weights(chunk(n + b), 256) for b in range(2)]
                out = [tile(n + b, j)[:, 0:N] for b in range(2) for j in range(2)]
                for k in range(KT):
                    ready(k)
                    for b in range(2):
                        for j in range(2):
                            c = slice(j * 128, (j + 1) * 128)
                            ins = mm3(out[2 * b + j], (w[b][0][:, k, c], w[b][1][:, k, c]), (hh[:, k, 0:N], hl[:, k, 0:N]), k == 0, k == KT - 1)
                            if k == KT - 1:
                                ins.then_inc(mm_done, 1)

            def project_tokens(n, ntok, t0=0):
                w = weights(chunk(n), 256)
                for q in range(ntok // 128):
                    out, c = tile(n, q), slice(t0 + q * 128, t0 + (q + 1) * 128)
                    for k in range(KT):
                        ins = mm3(out[:, 0:256], (hh[:, k, c], hl[:, k, c]), (w[0][:, k, :], w[1][:, k, :]), k == 0, k == KT - 1)
                    ins.then_inc(mm_done, 1)

            def ffn(f, N):
                n0, g0 = FIRST["ffn", f], f * GROUPS
                per, _, tiles, n_up, n_down, n_ada, n_last = ffn_pass(f)
                ready = split_input(N)

                def first_halves():
                    w = [weights(chunk(n), 256) for n in (n0, n0 + 1)]
                    for k in range(KT):
                        ready(k)
                        for b, bank in enumerate((ps_g, ps_u)):
                            for j in range(2):
                                c = slice(j * 128, (j + 1) * 128)
                                ins = mm3(bank[:, j, 0:N], (w[b][0][:, k, c], w[b][1][:, k, c]), (hh[:, k, 0:N], hl[:, k, 0:N]), k == 0, k == KT - 1)
                            if k == KT - 1:
                                ins.then_inc(mm_done, 1)

                def half(bank, n, i=None):
                    w = weights(chunk(n, i, per), 256)
                    for j in range(2):
                        for k in range(KT):
                            c = slice(j * 128, (j + 1) * 128)
                            ins = mm3(bank[:, j, 0:N], (w[0][:, k, c], w[1][:, k, c]), (hh[:, k, 0:N], hl[:, k, 0:N]), k == 0, k == KT - 1)
                    ins.then_inc(mm_done, 1)

                def down(n, T, group, i=None, last=False):
                    w = weights(chunk(n, i, per), D)
                    pe.wait_ge(a_ready, group + 1)
                    for d in range(KT):
                        pe.wait_ge(o_free, T + (d + 1))
                        for k in range(2):
                            c = slice(d * 128, (d + 1) * 128)
                            ins = mm3(ps_o[:, (TILE0[n] + d) % BANKS, 0:N], (w[0][:, k, c], w[1][:, k, c]), (ah[:, k, 0:N], al[:, k, 0:N]), k == 0, k == 1)
                        ins.then_inc(mm_done, 1)
                        if last:
                            sum_squares(NTOK if f in (4, 6) else N, d + 1 - LAG)

                first_halves()
                with pe.Fori(0, GROUPS - 1) as i:
                    pe.wait_ge(g_act, i + (g0 + 1))
                    half(ps_g, n0 + 2, i)
                    for n in range(n0 + 3, n0 + 2 + per):
                        if n == n_up:
                            pe.wait_ge(u_mul, i + (g0 + 1))
                            half(ps_u, n, i)
                        elif n == n_down:
                            down(n, i * tiles + TILE0[n], i + g0, i)
                        else:
                            ada(n, i)
                down(n_last, TILE0[n_last], g0 + GROUPS - 1, last=f < 7)

            def ada(n, i=None):
                w = weights(chunk(n, i, len(FFN_ADA_PASS)), 256)
                parts = DONE[n] - (DONE[n - 1] if n else 0)
                for q in range(parts):
                    T = TILE0[n] + q
                    pe.wait_ge(o_free, T + 1 if i is None else i * sum(FFN_ADA_PASS) + (T + 1))
                    rows = range(q * KT // parts, (q + 1) * KT // parts)
                    for k in rows:
                        out = ps_o[0:4, T % BANKS, 0:256]
                        mm(out, cs[:, k, :], w[1][:, k, :], start=k == rows[0], stop=False)
                        ins = mm(out, cs[:, k, :], w[0][:, k, :], start=False, stop=k == rows[-1])
                    ins.then_inc(mm_done, 1)

            def ada_turn(e):
                c0, c1 = ADA_PARTS[e]
                n_last = [FIRST["ada", 0] + ADA_FIRST, FIRST["ffn", 0] + 2 + 6 * (GROUPS - 1), FIRST["ffn", 1] + 2 + 6 * (GROUPS - 1)][e]
                pe.wait_ge(o_free, freed(TILE0[n_last]))
                for t in range(2 * (c1 - c0) // 3):
                    ins = mm(ps_u[:, 0, 6 * t:6 * t + 6], ada_rows[:, 128 * t:128 * (t + 1)], C("pick", 6)[0:96], start=True, stop=True)
                ins.then_inc(ad_turn, 1)

            def head_sums(nt, idle=2):
                st["hn"] += 1
                keep_clock(idle, BANK[3])
                pe.wait_ge(hn_sq, st["hn"])
                for i in range(nt):
                    ins = mm(BANK[3][0:16, 0:NX], C("sel", 32)[:, 16 - 2 * i:32 - 2 * i], hid[:, NX * i:NX * (i + 1)], start=i == 0, stop=i == nt - 1)
                ins.then_inc(hn_sum, 1)

            def head_spread(nt):
                pe.wait_ge(hn_inv, st["hn"])
                for i in range(nt):
                    ins = mm(BANK[i // 2][:, NX * (i % 2):NX * (i % 2 + 1)], C("spread", 1024)[0:16, 128 * i:128 * (i + 1)], head_rows, start=True, stop=True)
                    if i % 2:
                        ins.then_inc(hn_back, 1)

            def head_norm(nt, idle=2):
                head_sums(nt, idle)
                keep_clock(3, BANK[2])
                head_spread(nt)

            def attend(a):
                U = ATT[a]

                def scores(u):
                    g, unit = AT0[a] + u, U[u]
                    if g >= 2:
                        pe.wait_ge(at_e, g - 1)
                    bank = ps_g if g % 2 == 0 else ps_u
                    for (rows, b, c), q, k in unit["scores"]:
                        ins = mm(bank[rows, b, c], q, k, start=True, stop=True)
                    ins.then_inc(at_s, 1)

                def flip(u):
                    g, unit = AT0[a] + u, U[u]
                    pe.wait_ge(at_p, g + 1)
                    if g:
                        pe.wait_ge(at_c, g)
                    for b in range(unit["nb"]):
                        ins = nc.tensor.transpose(ps_o[:, b // 4, (b % 4) * 128:(b % 4 + 1) * 128], probs[g % 2][:, b * 128:(b + 1) * 128], ident)
                    ins.then_inc(at_t, 1)

                def values(u):
                    g, unit = AT0[a] + u, U[u]
                    pe.wait_ge(at_c, g + 1)
                    if g >= 2:
                        pe.wait_ge(at_y, g - 1)
                    nb = unit["nb"]
                    for b in range(nb):
                        ins = mm(ps_o[unit["rows"], 2 + g % 2, 0:128], unit["v"][b], probs_t[a][g % 2][:, b, :], start=b == 0, stop=b == nb - 1)
                    ins.then_inc(at_o, 1)

                scores(0)
                scores(1)
                for u in range(len(U)):
                    if u:
                        values(u - 1)
                    if u + 2 < len(U):
                        scores(u + 2)
                    if u >= 2:
                        pe.wait_ge(at_y, AT0[a] + u - 1)
                    keep_clock(3 if u < 2 else 1, ps_o[:, 2 + (AT0[a] + u) % 2, 128:512])
                    flip(u)
                values(len(U) - 1)

            def y_split():
                st["y"] += 1
                pe.wait_ge(y_ready, st["y"])

            pe.wait_ge(ad_lo, 1)
            for n in range(ADA_FIRST):
                ada(n)
                sum_squares(NTOK, min(n - 2, KT))
            norm(NTOK, part=0)
            ffn(0, NTOK)
            norm(NTOK, False, part=1)
            n = FIRST["pool", 0]
            w = weights(chunk(n), 256)
            for g in range(4):
                keep_clock((14, 4, 0, 0)[g], BANK[3])
                y_split()
                for j in range(2):
                    out, c = tile(n, 2 * g + j), slice(j * 128, (j + 1) * 128)
                    for k in range(2):
                        ins = mm3(out, (w[0][:, 2 * g + k, c], w[1][:, 2 * g + k, c]), (hh[:, 2 * g + k, :], hl[:, 2 * g + k, :]), k == 0, k == 1)
                    ins.then_inc(mm_done, 1)
                    sum_squares(NTOK, 2 * g + j + 1 - LAG)
            norm(NTOK)
            ffn(1, NTOK)
            norm(NTOK, part=2)
            ffn(2, NTOK)
            norm(NTOK)
            n = FIRST["qkv", 0]
            project_first(n, NX, of=NTOK)
            for c in range(2, 12):
                if c < 8:
                    project(n + c, NX if c < 4 else NTOK)
                else:
                    project_tokens(n + c, NTOK)
            pe.wait_ge(o_free, freed(TILE0[n + 8]))
            for r in range(8):
                z = q_d[:, 2 * r:2 * r + 2, :] if r < 4 else k_d[:, 2 * (r - 4):2 * (r - 4) + 2, 0:NX]
                if r >= 4:
                    pe.wait_ge(ro_sin, r - 3)
                mm(BANK[r % 4].rearrange("p (a n) -> p a n", a=2), C("perm"), z, start=True, stop=True).then_inc(ro_mm, 1)
            pe.wait_ge(o_free, freed(TILE0[n + 12]))
            keep_clock(10, ps_o[:, 3, :])
            pe.wait_ge(ro_done, 8)
            attend(0)
            pe.wait_ge(c_late, 16)
            pe.wait_ge(sl_sq, 1)
            for i in range(KT):
                ins = mm(ps_o[0:40, 0, 0:NX], C("sel8", 47)[:, 7 - i:47 - i], big[:, 2048 + NX * i:2048 + NX * (i + 1)], start=i == 0, stop=i == KT - 1)
            ins.then_inc(sl_sum, 1)
            keep_clock(3, BANK[3])
            pe.wait_ge(sl_inv, 1)
            for i in range(KT):
                ins = mm(BANK[i // 2][:, NX * (i % 2):NX * (i % 2 + 1)], C("spread", 1024)[32:40, 128 * i:128 * (i + 1)], subln_rows, start=True, stop=True)
                if i % 2:
                    ins.then_inc(sl_back, 1)
            for b in range(4):
                y_split()
            for c in range(4):
                project(FIRST["wo", 0] + c, NX, into_x=2 * c if c == 3 else None)
            norm(NX)
            ffn(3, NX)
            norm(NX, False)
            norm(NX)
            ffn(4, NX)

            def mem_kv(l):
                project(FIRST["memkv", l], NX, t0=NX)
                project_tokens(FIRST["memkv", l] + 1, NX, t0=NX)

            norm(NTOK)
            project_first(FIRST["a_in", 0], NX, of=NTOK)
            for c in range(2, 11):
                project(FIRST["a_in", 0] + c, NX)
            mem_kv(0)
            pe.wait_ge(lora_in, 48)
            keep_clock(5, BANK[3])
            pe.wait_ge(rw["lora"], 1)
            for u in range(2):
                bank = ps_g if u == 0 else ps_u
                lhs = proj[0:64, 18, 1 + 128 * u:129 + 128 * u]
                mm(bank[:, 0, :], lhs, lora[0:64, 0:512], start=True, stop=True)
                ins = mm(bank[:, 1, 0:256], lhs, lora[0:64, 512:768], start=True, stop=True)
            ins.then_inc(rw["z"], 1)
            pe.wait_ge(o_free, freed(TILE0[FIRST["a_out", 0]]))
            for i in range(RT):
                if i >= 2:
                    pe.wait_ge(rw["a_act"], i - 1)
                mm(ps_o[:, i % 2, 0:NX], lora[64:128, 128 * i:128 * (i + 1)], proj[64:128, 18, 1:257], start=True, stop=True).then_inc(rw["a_mm"], 1)
            for i in range(RT):
                if i >= 2:
                    pe.wait_ge(rw["g_act"], i - 1)
                mm(ps_o[:, 2 + i % 2, 0:NX], gup[:, 128 * i:128 * (i + 1)], proj[:, 19, 1:257], start=True, stop=True).then_inc(rw["g_mm"], 1)
            pe.wait_ge(rw["sq"], 1)
            def row_sums(src, done):
                for i in range(RT):
                    ins = mm(BANK[3][0:16, 0:NX], C("sel", 32)[:, 16 - 2 * i:32 - 2 * i], src(i), start=i == 0, stop=i == RT - 1)
                ins.then_inc(done, 1)

            def rows_back(done):
                for i in range(RT):
                    ins = mm(BANK[i // 2][:, NX * (i % 2):NX * (i % 2 + 1)], C("spread", 1024)[0:16, 128 * i:128 * (i + 1)], head_rows, start=True, stop=True)
                    if i % 2:
                        ins.then_inc(done, 1)

            row_sums(lambda i: bon[:, i, :], rw["ss"])
            keep_clock(3, ps_u[:, 0, :])
            pe.wait_ge(rw["inv"], 1)
            rows_back(rw["back"])
            keep_clock(7, BANK[3])
            pe.wait_ge(rw["bsq"], 1)
            for b in range(3):
                ins = mm(BANK[b], blk, bon[:, 2 * b:2 * b + 2, :], start=True, stop=True)
            ins.then_inc(rw["bsum"], 1)
            pe.wait_ge(rw["zs"], 1)
            pe.wait_ge(rw["bon"], 1)
            pe.wait_ge(rw["a_act"], RT)
            pe.wait_ge(rw["g_act"], RT)
            head_norm(4)
            pe.wait_ge(hn_done, st["hn"])
            attend(1)
            pe.wait_ge(at_y, AT0[2])
            R = [slice(0, 64), slice(64, 128)]
            def tok(i, e, m):
                return tmaj[i % 2][:, e, m % 2, 64 * (m // 2):64 * (m // 2) + 64]

            def decay_sums(i):
                for u in range(2):
                    ins = mm(FREE[1][:, 256 * u:256 * u + 256], zs[:, u, 128 * i:128 * (i + 1)], C("cum", 256), start=True, stop=True)
                ins.then_inc(rw["cum"], 1)

            def to_tokens(i):
                pe.wait_ge(rw["feat"], i + 1)
                if i:
                    pe.wait_ge(rw["mvx"], i)
                for e, src in enumerate((two(v_[:, i, :]), be, ka, ar[i % 2][:, :, 0, :])):
                    for u in range(2):
                        at = (e % 2) * 256 + u * 128
                        ins = nc.tensor.transpose(FREE[1 + 3 * (e // 2)][:, at:at + 128], src[:, u, :], ident)
                ins.then_inc(rw["tp"], 1)

            def pairs(i, q, lhs, bank, done):
                for u in range(2):
                    ins = mm(bank[:, 256 * u:256 * u + 256].rearrange("p (e n) -> p e n", e=2), lhs[R[q], u, :], ar[i % 2][R[q], u, :, :], start=True, stop=True)
                ins.then_inc(rw[done], 1)

            def pairs_lp(i, q):
                if q:
                    pe.wait_ge(rw["tm"], i + 1)
                elif i >= 2:
                    pe.wait_ge(rw["rps"], i - 1)
                pairs(i, q, be, FREE[q], "lp")

            def pairs_mp(i, q):
                if q:
                    pe.wait_ge(rw["lpm"], 2 * i + 1)
                else:
                    pe.wait_ge(rw["tm"], i + 1)
                pairs(i, q, ka, FREE[4 * (1 - q)], "mp")

            def pairs_ti(i):
                pe.wait_ge(rw["lpm"], 2 * i + 2)
                if i >= 2:
                    pe.wait_ge(rw["ss2"], 2 * (i - 1))
                for q in range(2):
                    for u in range(2):
                        ins = mm(FREE[1 + 2 * q][:, 128 * u:128 * (u + 1)], ar[i % 2][R[q], u, 0, :], be[R[q], u, :], start=True, stop=True)
                ins.then_inc(rw["tib"], 1)

            def mix_values(i):
                pe.wait_ge(rw["mpm"], 2 * i + 2)
                for m in range(4):
                    ins = mm(FREE[4][:, 64 * m:64 * (m + 1)], mp[i % 2][:, m, 0, :], tok(i, 0, m), start=True, stop=True)
                ins.then_inc(rw["mv"], 1)

            def level_p(i, l):
                if l:
                    pe.wait_ge(rw["ti"], 4 * i + l)
                else:
                    pe.wait_ge(rw["lmask"], i + 1)
                for m in range(4):
                    ins = mm(INV[0][:, 128 * m:128 * (m + 1)], lp[i % 2][:, m, 0, :], ti[:, m, :], start=True, stop=True)
                ins.then_inc(rw["p"], 1)

            def level_t(i, l):
                pe.wait_ge(rw["pm"], 5 * i + l + 1)
                if l:
                    pe.wait_ge(rw["tt"], 5 * i + l)
                else:
                    pe.wait_ge(rw["tit"], i + 1)
                for m in range(4):
                    c = slice(128 * m, 128 * (m + 1))
                    if l < 4:
                        mm(INV[1][:, c], tit[i % 2][:, m, :], pp[:, m, :], start=True, stop=True)
                    ins = mm(INV[2][:, c], pp[:, m, :], tit[i % 2][:, m, :], start=True, stop=True)
                ins.then_inc(rw["t"], 1)

            def solve(i):
                pe.wait_ge(rw["mvx"], i + 1)
                pe.wait_ge(rw["tt"], 5 * (i + 1))
                if i + 1 < RT:
                    pe.wait_ge(rw["mpm"], 2 * (i + 2))
                for m in range(4):
                    ins = mm(FREE[0][:, 128 * m:128 * (m + 1)], tit[i % 2][:, m, :], xs[i % 2][:, m, :], start=True, stop=True)
                ins.then_inc(rw["tx"], 1)

            def read_out(i):
                pe.wait_ge(rw["txs"], i + 1)
                if i:
                    pe.wait_ge(rw["yout"], i)
                for m in range(4):
                    q, u = m // 2, m % 2
                    ins = mm(FREE[0][R[q], 128 * u:128 * (u + 1)], tx[:, m, 0:64], lp[i % 2][:, m, 1, :], start=True, stop=True)
                ins.then_inc(rw["rp"], 1)
                for u in range(2):
                    for q in range(2):
                        m = 2 * q + u
                        o = FREE[2][R[q], 256 + 128 * u:384 + 128 * u]
                        mm(o, tx[:, m, 64:128], lp[i % 2][:, m, 1, :], start=True, stop=False)
                        mm(o, tok(i, 0, m), mp[i % 2][:, m, 1, :], start=False, stop=True)
                for m in range(4):
                    q, u = m // 2, m % 2
                    for e in range(2):
                        c = 2 * u + e
                        if c in (1, 2):
                            mm(FREE[2 + e][R[q], 64 * u:64 * (u + 1)], tx[R[e], m, 0:64], tok(i, 1, m)[R[e]], start=True, stop=True)
                        if c < 3:
                            o = FREE[2 + e][R[q], 128 + 64 * u:192 + 64 * u]
                            mm(o, tok(i, 1, m)[R[e]], tx[R[e], m, 64:128], start=True, stop=False)
                            ins = mm(o, tok(i, 2, m)[R[e]], tok(i, 0, m)[R[e]], start=False, stop=True)
                ins.then_inc(rw["gz"], 1)

            states = [None, zd[:, 0, :], st2[:, 0, :], st2[:, 1, :]]

            def carry(i, c):
                if c == 0:
                    pe.wait_ge(rw["gzs"], i + 1)
                else:
                    pe.wait_ge(rw["ss2"], 2 * i + 1)
                for q in range(2):
                    ins = mm(FREE[3][R[q], 256 + 64 * c:320 + 64 * c], gi[R[q], c, :], states[c + 1][R[q]], start=True, stop=True)
                ins.then_inc(rw["s"], 1)

            def output(i):
                pe.wait_ge(rw["rps"], i + 1)
                pe.wait_ge(rw["ss2"], 2 * i + 2)
                for c in range(1, 4):
                    for q in range(2):
                        u, e = c // 2, c % 2
                        ins = mm(FREE[2][R[q], CH * c:CH * (c + 1)], states[c][R[q]], rp[R[q], u, 64 * e:64 * e + 64], start=True, stop=True)
                ins.then_inc(rw["y"], 1)

            decay_sums(0)
            to_tokens(0)
            pairs_lp(0, 0)
            pairs_lp(0, 1)
            pairs_mp(0, 0)
            pairs_mp(0, 1)
            pairs_ti(0)
            mix_values(0)
            for i in range(RT + 1):
                inv, post, pre = i < RT, i > 0, i + 1 < RT
                if inv:
                    level_p(i, 0)
                if post:
                    solve(i - 1)
                if inv:
                    level_t(i, 0)
                if pre:
                    decay_sums(i + 1)
                if inv:
                    level_p(i, 1)
                if post:
                    read_out(i - 1)
                if inv:
                    level_t(i, 1)
                if pre:
                    to_tokens(i + 1)
                if inv:
                    level_p(i, 2)
                if post:
                    carry(i - 1, 0)
                if pre:
                    pairs_lp(i + 1, 0)
                if inv:
                    level_t(i, 2)
                if post:
                    carry(i - 1, 1)
                if pre:
                    pairs_lp(i + 1, 1)
                if inv:
                    level_p(i, 3)
                if post:
                    output(i - 1)
                if pre:
                    pairs_mp(i + 1, 0)
                if inv:
                    level_t(i, 3)
                if pre:
                    pairs_mp(i + 1, 1)
                if inv:
                    level_p(i, 4)
                if pre:
                    pairs_ti(i + 1)
                if inv:
                    level_t(i, 4)
                if pre:
                    mix_values(i + 1)
            pe.wait_ge(rw["yout"], RT)
            for b in range(3):
                ins = mm(BANK[b], blk, y_all[:, 2 * b:2 * b + 2, :], start=True, stop=True)
            ins.then_inc(rw["mean"], 1)
            keep_clock(4, BANK[3])
            pe.wait_ge(rw["cen"], 1)
            row_sums(lambda i: hid[:, NX * i:NX * (i + 1)], rw["var"])
            keep_clock(3, ps_o[:, 0, :])
            pe.wait_ge(rw["vinv"], 1)
            rows_back(rw["vback"])
            keep_clock(7, ps_o[:, 0, :])
            for b in range(4):
                y_split()
            for c in range(4):
                project(FIRST["a_out", 0] + c, NX, into_x=2 * c if c == 3 else None)
            norm(NX)
            ffn(5, NX)
            pe.wait_ge(bt_in, 16)
            pe.wait_ge(rel_in, 16)
            for g in range(3):
                ins = mm(BANK[1 + g][0:4, :], rel[:, 4 * g:4 * g + 4], bt[:, 512 * g:512 * (g + 1)], start=True, stop=True)
            ins.then_inc(bi_row, 1)
            pe.wait_ge(bi_sb, 3)
            norm(NX)
            project_first(FIRST["kv", 0], NX)
            project(FIRST["kv", 0] + 2, NX)
            project_tokens(FIRST["kv", 0] + 3, NX)
            head_sums(6, idle=0)
            project_tokens(FIRST["kv", 0] + 4, NX)
            head_spread(6)
            project_tokens(FIRST["kv", 0] + 5, NX)
            pe.wait_ge(hn_done, st["hn"])
            norm(NX, again=True)
            ffn(6, NX)
            norm(NTOK)
            project_first(FIRST["b_q", 0], NX, of=NTOK)
            for c in range(2, 4):
                project(FIRST["b_q", 0] + c, NX)
            mem_kv(1)
            head_norm(8)
            head_norm(2, idle=0)
            pe.wait_ge(hn_done, st["hn"])
            attend(2)
            y_split()
            for c in range(2):
                project(FIRST["b_out", 0] + c, NX, rows=4, width=512, into_x=4 * c if c == 1 else None)
            norm(NX)
            ffn(7, NX)


def kernel(**inputs):
    import concourse.bacc as _bacc
    from concourse.bass_utils import run_bass_kernel_spmd as _run

    a = {k: np.asarray(v) for k, v in inputs.items()}
    arrays = pack(a)
    nc = _bacc.Bacc("TRN2", target_bir_lowering=False, num_devices=1)
    args = [nc.dram_tensor("in_" + k, v.shape, mybir.dt.from_np(v.dtype), kind="ExternalInput").ap() for k, v in arrays.items()]
    out = nc.dram_tensor("out", (128, KT, NX), mybir.dt.float32, kind="ExternalOutput").ap()
    build(nc, *args, out)
    r = _run(nc, [{"in_" + k: v for k, v in arrays.items()}], core_ids=[0])
    return np.ascontiguousarray(np.asarray(r.results[0]["out"]).transpose(2, 1, 0)).reshape(1, NX, D)
```
